# Optimizing a Trainium2 kernel written in Bass

```python
import math
import jax, jax.numpy as jnp
from jax import lax
import numpy as np

D_MODEL = 1024
BATCH = 1
SEQ = 256
DEPTH = 2

N_HEADS = 16
HEAD_DIM = D_MODEL // N_HEADS
Q_CHUNK = 64
NEG_INF = -1e30
LN_EPS = 1e-5
MOBA_BLOCK = 256
MOBA_TOPK = 3
NSA_KV_HEADS = 4
NSA_GROUP = N_HEADS // NSA_KV_HEADS
CMP_LEN = 32
CMP_STRIDE = 16
CMP_HIDDEN = 256
SLC_BLOCK = 64
SLC_TOPN = 16
SLC_LOCAL = 2
WINDOW = 512
REL_BUCKETS = 32
REL_MAX_DIST = 128
N_EXPERTS = 32
N_GROUPS = 8
EXPERTS_PER_GROUP = N_EXPERTS // N_GROUPS
TOP_K = 2
D_EXPERT = 512
MOE_BLOCK = 128
N_MOBA_LAYERS = (DEPTH + 1) // 2
N_NSA_LAYERS = DEPTH // 2
DEEPNORM_ALPHA = (2 * DEPTH) ** 0.25
DEEPNORM_BETA = (8 * DEPTH) ** -0.25

kernel_name = 'moba_nsa_deepnorm_grouped_moe'

def layer_norm(x, g, b):
    xf = x.astype(jnp.float32)
    mu = jnp.mean(xf, axis=-1, keepdims=True)
    var = jnp.mean(jnp.square(xf - mu), axis=-1, keepdims=True)
    y = (xf - mu) * lax.rsqrt(var + LN_EPS)
    return (y * g.astype(jnp.float32) + b.astype(jnp.float32)).astype(x.dtype)

def t5_bucket(rel):
    n = jnp.maximum(rel, 0)
    max_exact = REL_BUCKETS // 2
    nf = jnp.maximum(n, 1).astype(jnp.float32)
    large = max_exact + (jnp.log(nf / max_exact) / math.log(REL_MAX_DIST / max_exact)
                         * (REL_BUCKETS - max_exact)).astype(jnp.int32)
    large = jnp.minimum(large, REL_BUCKETS - 1)
    return jnp.where(n < max_exact, n, large)

def masked_softmax(s, valid):
    return jax.nn.softmax(jnp.where(valid, s, NEG_INF), axis=-1)

def gather_blocks(blocks, idx):
    return jax.vmap(lambda bl, ix: bl[ix])(blocks, idx)

def moba_attention(x, w_in, w_out, rel_bias):
    B, S, _ = x.shape
    H, d, BLK = N_HEADS, HEAD_DIM, MOBA_BLOCK
    scale = d ** -0.5
    proj = x @ w_in
    q, k, v = jnp.split(proj, 3, axis=-1)
    to_heads = lambda t: t.reshape(B, S, H, d).transpose(0, 2, 1, 3)
    q, k, v = to_heads(q), to_heads(k), to_heads(v)
    S_pad = -(-S // BLK) * BLK
    padw = ((0, 0), (0, 0), (0, S_pad - S), (0, 0))
    q, k, v = jnp.pad(q, padw), jnp.pad(k, padw), jnp.pad(v, padw)
    nb = S_pad // BLK
    topk = min(MOBA_TOPK, nb)
    tbl = rel_bias.T

    def one_seq(args):
        qs, ks, vs = args
        kb = ks.reshape(H, nb, BLK, d)
        vb = vs.reshape(H, nb, BLK, d)
        kmean = jnp.mean(kb.astype(jnp.float32), axis=2).astype(ks.dtype)

        def one_chunk(c):
            start = c * Q_CHUNK
            qc = lax.dynamic_slice_in_dim(qs, start, Q_CHUNK, axis=1)
            qpos = start + jnp.arange(Q_CHUNK)
            qblk = start // BLK
            gate = jnp.einsum('hqd,hnd->hqn', qc, kmean).astype(jnp.float32)
            gate = jnp.where(jnp.arange(nb) < qblk, gate, -jnp.inf)
            _, idx = lax.top_k(gate, topk)
            sel_valid = idx < qblk
            kg = gather_blocks(kb, idx)
            vg = gather_blocks(vb, idx)
            kpos_sel = idx[..., None] * BLK + jnp.arange(BLK)
            s_sel = jnp.einsum('hqd,hqnkd->hqnk', qc, kg).reshape(H, Q_CHUNK, topk * BLK)
            own_start = qblk * BLK
            ko = lax.dynamic_slice_in_dim(ks, own_start, BLK, axis=1)
            vo = lax.dynamic_slice_in_dim(vs, own_start, BLK, axis=1)
            kpos_own = own_start + jnp.arange(BLK)
            s_own = jnp.einsum('hqd,hkd->hqk', qc, ko)
            scores = jnp.concatenate([s_sel, s_own], axis=-1).astype(jnp.float32) * scale
            kpos = jnp.concatenate([kpos_sel.reshape(H, Q_CHUNK, topk * BLK),
                                    jnp.broadcast_to(kpos_own, (H, Q_CHUNK, BLK))], axis=-1)
            valid_sel = jnp.broadcast_to(sel_valid[..., None], (H, Q_CHUNK, topk, BLK)).reshape(H, Q_CHUNK, topk * BLK)
            valid_own = jnp.broadcast_to(kpos_own[None, :] <= qpos[:, None], (H, Q_CHUNK, BLK))
            valid = jnp.concatenate([valid_sel, valid_own], axis=-1)
            rel = qpos[None, :, None] - kpos
            bias = jax.vmap(lambda t, bk: t[bk])(tbl, t5_bucket(rel)).astype(jnp.float32)
            p = masked_softmax(scores + bias, valid).astype(vs.dtype)
            o = (jnp.einsum('hqnk,hqnkd->hqd', p[..., :topk * BLK].reshape(H, Q_CHUNK, topk, BLK), vg)
                 + jnp.einsum('hqk,hkd->hqd', p[..., topk * BLK:], vo))
            return o

        outs = lax.map(one_chunk, jnp.arange(S_pad // Q_CHUNK))
        return outs.transpose(1, 0, 2, 3).reshape(H, S_pad, d)

    o = lax.map(one_seq, (q, k, v))
    o = o[:, :, :S].transpose(0, 2, 1, 3).reshape(B, S, H * d)
    return o @ w_out

def nsa_attention(x, w_in, w_out, pos_k, pos_v, ck_w1, ck_w2, cv_w1, cv_w2, rel_bias):
    B, S, _ = x.shape
    H, Hkv, G, d = N_HEADS, NSA_KV_HEADS, NSA_GROUP, HEAD_DIM
    scale = d ** -0.5
    proj = x @ w_in
    sizes = [H * d] + [Hkv * d] * 6 + [3 * H]
    q, kc, vc, ks, vs, kw, vw, g = jnp.split(proj, np.cumsum(sizes)[:-1].tolist(), axis=-1)
    q = q.reshape(B, S, Hkv, G, d).transpose(0, 2, 3, 1, 4)
    kv_heads = lambda t: t.reshape(B, S, Hkv, d)
    kc, vc, ks, vs, kw, vw = [kv_heads(t) for t in (kc, vc, ks, vs, kw, vw)]
    g = jax.nn.sigmoid(g).reshape(B, S, Hkv, G, 3).transpose(0, 2, 3, 1, 4)

    n_cmp = (S - CMP_LEN) // CMP_STRIDE + 1
    cidx = np.arange(n_cmp)[:, None] * CMP_STRIDE + np.arange(CMP_LEN)[None, :]

    def compress(t, pos, w1, w2):
        blk = t[:, cidx] + pos[None, None, :, None, :]
        blk = blk.transpose(0, 1, 3, 2, 4).reshape(B, n_cmp, Hkv, CMP_LEN * d)
        return (jax.nn.gelu(blk @ w1) @ w2).transpose(0, 2, 1, 3)

    kcmp = compress(kc, pos_k, ck_w1, ck_w2)
    vcmp = compress(vc, pos_v, cv_w1, cv_w2)
    to_hm = lambda t: t.transpose(0, 2, 1, 3)
    ks, vs = to_hm(ks), to_hm(vs)
    padw = ((0, 0), (0, 0), (WINDOW, 0), (0, 0))
    kw_pad, vw_pad = jnp.pad(to_hm(kw), padw), jnp.pad(to_hm(vw), padw)

    n_slc = S // SLC_BLOCK
    topn = min(SLC_TOPN, n_slc)
    ci = np.arange(n_cmp)[:, None] * CMP_STRIDE
    sj = np.arange(n_slc)[None, :] * SLC_BLOCK
    cmp_to_slc = jnp.asarray(((ci < sj + SLC_BLOCK) & (ci + CMP_LEN > sj)).astype(np.float32))
    cmp_end = jnp.arange(n_cmp) * CMP_STRIDE + CMP_LEN - 1
    tbl = rel_bias.T.reshape(Hkv, G, REL_BUCKETS)

    def one_seq(args):
        qs, kcm, vcm, kss, vss, kwp, vwp, gs = args
        ksb = kss.reshape(Hkv, n_slc, SLC_BLOCK, d)
        vsb = vss.reshape(Hkv, n_slc, SLC_BLOCK, d)

        def one_chunk(c):
            start = c * Q_CHUNK
            qc = lax.dynamic_slice_in_dim(qs, start, Q_CHUNK, axis=2)
            qpos = start + jnp.arange(Q_CHUNK)
            s_c = jnp.einsum('hgqd,hnd->hgqn', qc, kcm).astype(jnp.float32) * scale
            v_c = cmp_end[None, :] <= qpos[:, None]
            p_c = masked_softmax(s_c, v_c) * v_c
            o_c = jnp.einsum('hgqn,hnd->hgqd', p_c.astype(vcm.dtype), vcm)
            imp = jnp.einsum('hgqn,nj->hqj', p_c, cmp_to_slc)
            qblk = qpos // SLC_BLOCK
            j = jnp.arange(n_slc)[None, :]
            qb = qblk[:, None]
            forced = (j == 0) | ((j <= qb) & (j > qb - SLC_LOCAL))
            future = j > qb
            imp = jnp.where(forced[None], jnp.inf, jnp.where(future[None], -jnp.inf, imp))
            _, idx = lax.top_k(imp, topn)
            sel_valid = idx <= qblk[None, :, None]
            kg = gather_blocks(ksb, idx)
            vg = gather_blocks(vsb, idx)
            kpos_s = idx[..., None] * SLC_BLOCK + jnp.arange(SLC_BLOCK)
            rel_s = qpos[None, :, None, None] - kpos_s
            valid_s = sel_valid[..., None] & (rel_s >= 0)
            s_s = jnp.einsum('hgqd,hqnkd->hgqnk', qc, kg).astype(jnp.float32) * scale
            bias_s = jax.vmap(lambda t, bk: t[:, bk])(tbl, t5_bucket(rel_s)).astype(jnp.float32)
            s_s = jnp.where(valid_s[:, None], s_s + bias_s, NEG_INF).reshape(Hkv, G, Q_CHUNK, topn * SLC_BLOCK)
            p_s = jax.nn.softmax(s_s, axis=-1).reshape(Hkv, G, Q_CHUNK, topn, SLC_BLOCK)
            o_s = jnp.einsum('hgqnk,hqnkd->hgqd', p_s.astype(vg.dtype), vg)
            kwin = lax.dynamic_slice_in_dim(kwp, start, WINDOW + Q_CHUNK, axis=1)
            vwin = lax.dynamic_slice_in_dim(vwp, start, WINDOW + Q_CHUNK, axis=1)
            kpos_w = start - WINDOW + jnp.arange(WINDOW + Q_CHUNK)
            rel_w = qpos[:, None] - kpos_w[None, :]
            valid_w = (rel_w >= 0) & (rel_w < WINDOW) & (kpos_w[None, :] >= 0)
            s_w = jnp.einsum('hgqd,hkd->hgqk', qc, kwin).astype(jnp.float32) * scale
            bias_w = tbl[:, :, t5_bucket(rel_w)].astype(jnp.float32)
            p_w = masked_softmax(s_w + bias_w, valid_w)
            o_w = jnp.einsum('hgqk,hkd->hgqd', p_w.astype(vwin.dtype), vwin)
            gc = lax.dynamic_slice_in_dim(gs, start, Q_CHUNK, axis=2)
            return gc[..., 0:1] * o_c + gc[..., 1:2] * o_s + gc[..., 2:3] * o_w

        outs = lax.map(one_chunk, jnp.arange(S // Q_CHUNK))
        return outs.transpose(1, 2, 0, 3, 4).reshape(Hkv, G, S, d)

    o = lax.map(one_seq, (q, kcmp, vcmp, ks, vs, kw_pad, vw_pad, g))
    o = o.transpose(0, 3, 1, 2, 4).reshape(B, S, H * d)
    return o @ w_out

def grouped_moe(x, router_w, router_b, w_gate, w_up, w_down):
    B, S, D = x.shape
    N = B * S
    h = x.reshape(N, D)
    probs = jax.nn.softmax((h @ router_w).astype(jnp.float32) + router_b.astype(jnp.float32), axis=-1)
    grp = probs.reshape(N, N_GROUPS, EXPERTS_PER_GROUP)
    grp_score = lax.top_k(grp, TOP_K)[0].sum(-1)
    best = jnp.argmax(grp_score, axis=-1)
    in_grp = jnp.take_along_axis(grp, best[:, None, None], axis=1)[:, 0]
    wts, local = lax.top_k(in_grp, TOP_K)
    wts = wts / jnp.sum(wts, axis=-1, keepdims=True)
    expert = best[:, None] * EXPERTS_PER_GROUP + local
    A = N * TOP_K
    e_flat = expert.reshape(A)
    tok = jnp.repeat(jnp.arange(N), TOP_K)
    w_flat = wts.reshape(A)
    order = jnp.argsort(e_flat)
    e_s, tok_s, w_s = e_flat[order], tok[order], w_flat[order]
    counts = jnp.bincount(e_flat, length=N_EXPERTS)
    starts = jnp.cumsum(counts) - counts
    padded = (counts + MOE_BLOCK - 1) // MOE_BLOCK * MOE_BLOCK
    pends = jnp.cumsum(padded)
    pstarts = pends - padded
    dest = pstarts[e_s] + (jnp.arange(A) - starts[e_s])
    R = A + N_EXPERTS * MOE_BLOCK
    n_blk = R // MOE_BLOCK
    row_tok = jnp.zeros((R,), jnp.int32).at[dest].set(tok_s)
    row_w = jnp.zeros((R,), jnp.float32).at[dest].set(w_s)
    blk_e = jnp.minimum(jnp.searchsorted(pends, jnp.arange(n_blk) * MOE_BLOCK, side='right'), N_EXPERTS - 1)
    xb = h[row_tok].reshape(n_blk, MOE_BLOCK, D)

    def expert_block(args):
        xt, e = args
        hid = jax.nn.silu(xt @ w_gate[e]) * (xt @ w_up[e])
        return hid @ w_down[e]

    yb = lax.map(expert_block, (xb, blk_e)).reshape(R, D)
    out = jnp.zeros((N, D), x.dtype).at[row_tok].add(yb * row_w[:, None].astype(yb.dtype))
    return out.reshape(B, S, D)

def setup_inputs(seed: int = 0) -> dict:
    key = jax.random.key(seed)
    ks = jax.random.split(key, 20)
    nrm = lambda k, shape, s: jax.random.normal(k, shape, jnp.float32) * s
    HD = N_HEADS * HEAD_DIM
    d_in_nsa = HD + 6 * NSA_KV_HEADS * HEAD_DIM + 3 * N_HEADS
    return dict(
        x=nrm(ks[0], (BATCH, SEQ, D_MODEL), 1.0),
        rel_bias=nrm(ks[1], (REL_BUCKETS, N_HEADS), 0.5),
        router_w=nrm(ks[2], (D_MODEL, N_EXPERTS), D_MODEL ** -0.5),
        router_b=nrm(ks[3], (N_EXPERTS,), 0.01),
        ln_g=1.0 + nrm(ks[4], (DEPTH, 2, D_MODEL), 0.05),
        ln_b=nrm(ks[5], (DEPTH, 2, D_MODEL), 0.05),
        moba_w_in=nrm(ks[6], (N_MOBA_LAYERS, D_MODEL, 3 * HD), D_MODEL ** -0.5),
        moba_w_out=nrm(ks[7], (N_MOBA_LAYERS, HD, D_MODEL), DEEPNORM_BETA * HD ** -0.5),
        nsa_w_in=nrm(ks[8], (N_NSA_LAYERS, D_MODEL, d_in_nsa), D_MODEL ** -0.5),
        nsa_w_out=nrm(ks[9], (N_NSA_LAYERS, HD, D_MODEL), DEEPNORM_BETA * HD ** -0.5),
        nsa_pos_k=nrm(ks[10], (N_NSA_LAYERS, CMP_LEN, HEAD_DIM), 0.1),
        nsa_pos_v=nrm(ks[11], (N_NSA_LAYERS, CMP_LEN, HEAD_DIM), 0.1),
        nsa_ck_w1=nrm(ks[12], (N_NSA_LAYERS, CMP_LEN * HEAD_DIM, CMP_HIDDEN), (CMP_LEN * HEAD_DIM) ** -0.5),
        nsa_ck_w2=nrm(ks[13], (N_NSA_LAYERS, CMP_HIDDEN, HEAD_DIM), CMP_HIDDEN ** -0.5),
        nsa_cv_w1=nrm(ks[14], (N_NSA_LAYERS, CMP_LEN * HEAD_DIM, CMP_HIDDEN), (CMP_LEN * HEAD_DIM) ** -0.5),
        nsa_cv_w2=nrm(ks[15], (N_NSA_LAYERS, CMP_HIDDEN, HEAD_DIM), CMP_HIDDEN ** -0.5),
        moe_w_gate=nrm(ks[16], (DEPTH, N_EXPERTS, D_MODEL, D_EXPERT), D_MODEL ** -0.5),
        moe_w_up=nrm(ks[17], (DEPTH, N_EXPERTS, D_MODEL, D_EXPERT), D_MODEL ** -0.5),
        moe_w_down=nrm(ks[18], (DEPTH, N_EXPERTS, D_EXPERT, D_MODEL), DEEPNORM_BETA * D_EXPERT ** -0.5),
    )

def reference(x, rel_bias, router_w, router_b, ln_g, ln_b, moba_w_in, moba_w_out,
              nsa_w_in, nsa_w_out, nsa_pos_k, nsa_pos_v, nsa_ck_w1, nsa_ck_w2,
              nsa_cv_w1, nsa_cv_w2, moe_w_gate, moe_w_up, moe_w_down):
    for i in range(DEPTH):
        j = i // 2
        if i % 2 == 0:
            mix = moba_attention(x, moba_w_in[j], moba_w_out[j], rel_bias)
        else:
            mix = nsa_attention(x, nsa_w_in[j], nsa_w_out[j], nsa_pos_k[j], nsa_pos_v[j],
                                nsa_ck_w1[j], nsa_ck_w2[j], nsa_cv_w1[j], nsa_cv_w2[j], rel_bias)
        x = layer_norm(DEEPNORM_ALPHA * x + mix, ln_g[i, 0], ln_b[i, 0])
        ffn = grouped_moe(x, router_w, router_b, moe_w_gate[i], moe_w_up[i], moe_w_down[i])
        x = layer_norm(DEEPNORM_ALPHA * x + ffn, ln_g[i, 1], ln_b[i, 1])
    return x


_drawn_inputs = setup_inputs


def setup_inputs(seed=0):
    import zlib

    import numpy as np

    out = dict(_drawn_inputs(seed))
    spreads = {}
    factors = {'nsa_pos_k': 25.074, 'nsa_pos_v': 2.732}
    for name, (base, spread) in spreads.items():
        noise = np.random.default_rng([zlib.crc32(name.encode()), seed]).standard_normal(out[name].shape)
        drawn = base * np.exp(spread * noise) if base else spread * noise
        out[name] = __import__('jax').numpy.asarray(drawn.astype(out[name].dtype))
    for name, factor in factors.items():
        out[name] = (out[name] * factor).astype(out[name].dtype)
    return out
```

```python
from contextlib import ExitStack

import numpy as np

import concourse.bass as bass
from concourse import mybir

F32 = mybir.dt.float32
I32 = mybir.dt.int32
ALU = mybir.AluOpType
ACT = mybir.ActivationFunctionType
AX = mybir.AxisListType.X

P = 128
D = 1024
SEQ = 256
NT = SEQ // P
KT = D // P
HEADS, DH = 16, 64
KV = 4
GROUP = HEADS // KV
LAYERS = 2
BUCKETS, MAX_DIST = 32, 128
CMP_LEN, CMP_STRIDE, CMP_HID = 32, 16, 256
N_CMP = (SEQ - CMP_LEN) // CMP_STRIDE + 1
E, EG, NG = 32, 4, 8
FF = 512
FT = FF // P
CAP = 64
PAIRS = E // 2
ALPHA = (2 * LAYERS) ** 0.25
EPS = 1e-5
NEG = -1e30
BIAS_W = 384
SLOT = 4096
NSLOT = 6
SMALL_LOADS = 6 * 16
OV_PE = 2 * 6


def t5_buckets(n):
    exact = BUCKETS // 2
    nf = np.maximum(n, 1).astype(np.float32)
    large = exact + (np.log(nf / np.float32(exact)) / np.float32(np.log(MAX_DIST / exact))
                     * (BUCKETS - exact)).astype(np.int32)
    return np.where(n < exact, n, np.minimum(large, BUCKETS - 1))


def shape_tables():
    p = np.arange(P)
    cols = {}
    cols["ident"] = np.eye(P)
    cols["flip"] = np.eye(P)[::-1]
    cols["before"] = (p[:, None] < p[None, :]).astype(float)
    cols["ones"] = np.ones((P, P))
    cols["slot"] = np.tile(np.arange(P) % CAP, (P, 1))
    cols["slot2"] = np.tile(np.arange(P), (P, 1))
    cols["first32"] = np.tile(E - np.arange(E), (P, 1))
    cols["first8"] = np.tile(NG - np.arange(NG), (P, 1))
    q = np.arange(NT)[None, :, None] * P + p[:, None, None]
    seen = np.arange(16)[None, None, :] * CMP_STRIDE + CMP_LEN - 1 <= q
    cols["seen"] = seen.reshape(P, -1)
    cols["unseen"] = np.where(seen, 0.0, NEG).reshape(P, -1)
    dist = SEQ - 1 - np.arange(BIAS_W)
    hot = np.zeros((P, BIAS_W))
    hot[t5_buckets(np.maximum(dist, 0)), np.arange(BIAS_W)] = dist >= 0
    hot[BUCKETS] = dist < 0
    cols["bucket"] = hot
    at, place = 0, {}
    for name, c in cols.items():
        place[name] = (at, at + c.shape[1])
        at += c.shape[1]
    return np.ascontiguousarray(np.concatenate(list(cols.values()), 1), dtype=np.float32), place


def after(eng, sem, value):
    if not isinstance(value, int) or value > 0:
        eng.wait_ge(sem, value)


def build(nc, x_in, rel_bias, router_w, router_b, ln_g, ln_b, moba_w_in, moba_w_out, nsa_w_in, nsa_w_out,
          nsa_pos_k, nsa_pos_v, nsa_ck_w1, nsa_ck_w2, nsa_cv_w1, nsa_cv_w2,
          moe_w_gate, moe_w_up, moe_w_down, tables, place, out):
    ctx = ExitStack()
    with ctx:
        def sb(name, shape, dt=F32):
            return ctx.enter_context(nc.sbuf_tensor(name, shape, dt))

        def sem(name):
            return ctx.enter_context(nc.semaphore(name))

        def sem2(name):
            return [sem(f"{name}_{l}") for l in range(LAYERS)]

        ring = sb("ring", [P, NSLOT, SLOT])
        xs = sb("xs", [P, NT, D])
        acc = sb("acc", [P, NT, D])
        norm_w = sb("norm_w", [P, 2, 2, D])
        bias = sb("bias", [P, HEADS, SEQ])
        xT = sb("xT", [P, KT, SEQ])
        work = sb("work", [P, 4 * 2048])
        tab = sb("tab", [P, place["bucket"][0]])
        probs = sb("probs", [P, 4, 3 * P])
        probsT = sb("probsT", [P, 2, 3, P])
        rel_w = sb("rel_w", [BUCKETS + 1, HEADS])
        router = sb("router", [P, KT, E])
        router_bias = sb("router_bias", [P, E])
        pos_rows = sb("pos_rows", [16, 2, P])
        pos_cols = sb("pos_cols", [P, 2, 16])
        cmp_w2 = sb("cmp_w2", [P, 2, 2, DH])
        gate_w = sb("gate_w", [P, KT, 3 * HEADS])
        gates = sb("gates", [P, NT, 3 * HEADS])
        cmp_hid = sb("cmp_hid", [P, 2, 2, KV * N_CMP])
        cmp_keyT = sb("cmp_keyT", [P, KV, 16])
        cmp_val = sb("cmp_val", [P, KV, DH])
        cmp_max = sb("cmp_max", [P, NT, HEADS])
        cmp_sum = sb("cmp_sum", [P, NT, HEADS])
        job_max = sb("job_max", [P, 4, NT])
        job_sum = sb("job_sum", [P, 4, NT])
        job_scale = sb("job_scale", [P, 4, NT])
        stats = sb("stats", [P, NT, 12])
        moments = sb("moments", [P, NT, 2])
        rstd = sb("rstd", [P, NT])
        one = sb("one", [P, 8, NT])
        slot_of = sb("slot_of", [P, NT, E])
        chosen = sb("chosen", [P, NT, E])
        weight = sb("weight", [P, NT, E])
        crowded = sb("crowded", [P, 1])
        crowded_i = sb("crowded_i", [P, 1], I32)

        bank = [ctx.enter_context(nc.psum_tensor(f"bank{i}", [P, 512], F32)) for i in range(8)]
        dist_dram = nc.dram_tensor("dist_rows", [HEADS, BIAS_W], F32)

        bucket_rows = acc[0:BUCKETS + 1, 0, 0:BIAS_W]
        dist_row = acc[0:HEADS, 1, 0:BIAS_W]

        def table(name, n=P):
            a, b = place[name]
            return tab[0:n, a:b]

        ident, flip = table("ident"), table("flip")

        qT = work[:, 0:2048].rearrange("p (m q) -> p m q", q=SEQ)
        kT = work[:, 2048:4096].rearrange("p (m q) -> p m q", q=SEQ)
        v_tok = work[:, 4096:6144].rearrange("p (k n) -> p k n", k=NT)
        oT = work[:, 6144:8192].rearrange("p (m q) -> p m q", q=SEQ)
        hankel = work[:, 4096:8192].rearrange("p (h k) -> p h k", k=SEQ)
        nsa_kT = work[:, 2048:4096].rearrange("p (b k q) -> p b k q", b=2, k=KV)
        nsa_v = work[:, 4096:5120].rearrange("p (b k n) -> p b k n", b=2, k=NT)
        cmp_p = work[:, 5120:6144].rearrange("p (t h n) -> p t h n", t=NT, n=32)
        cmp_pT = xT[:, 0:4, :]
        cmp_in = acc[:, :, :].rearrange("p t d -> p (t d)")[:, 0:2 * 16 * KV * N_CMP].rearrange(
            "p (b l n) -> p b l n", b=2, l=16)
        xgT = work[:, 0:1024].rearrange("p (t s) -> p t s", s=P)
        yT = work[:, 1024:2048].rearrange("p (t s) -> p t s", s=P)
        y_slot = work[:, 2048:3072]
        hid = work[:, 3072:3584]
        silu = work[:, 3584:4096]
        pick = work[:, 4096:4352].rearrange("p (t e s) -> p t e s", t=NT, e=2)
        pick_w = work[:, 4352:4608].rearrange("p (t e s) -> p t e s", t=NT, e=2)
        pick_wT = work[:, 4608:4864].rearrange("p (t q) -> p t q", t=NT)
        hidT = work[:, 5504:6016].rearrange("p (m s) -> p m s", s=P)
        route = work[:, 4864:5376].rearrange("p (k t e) -> p k t e", t=NT, e=E)
        small = work[:, 5376:5504].rearrange("p (k t g) -> p k t g", t=NT, g=NG)

        def cols(w, c):
            return w[:, c * 512:(c + 1) * 512].rearrange("(p t) n -> p t n", t=KT)

        def rows(w, c):
            return w[c * 512:(c + 1) * 512, :].rearrange("(m p) n -> p m n", p=P)

        moba_uses = [cols(moba_w_in[0], c) for c in (0, 2, 4, 1, 3, 5)] + [rows(moba_w_out[0], c) for c in (0, 1)]
        nsa_uses = ([cols(nsa_w_in[0], c) for c in range(5)]
                    + [w[0].rearrange("(l p) n -> p l n", p=P) for w in (nsa_ck_w1, nsa_cv_w1)]
                    + [rows(nsa_w_out[0], c) for c in (0, 1)])
        first_use = [0, len(moba_uses) + 3 * E]
        first_moe = [len(moba_uses), len(moba_uses) + 3 * E + len(nsa_uses)]
        USES_PER_PAIR = 6

        def slot_no(u):
            return u % NSLOT

        def slot8(u):
            return ring[:, slot_no(u), :].rearrange("p (t n) -> p t n", t=KT)

        def slot4(u):
            return ring[:, slot_no(u), :].rearrange("p (t n) -> p t n", t=4)

        def slot16(u):
            return ring[:, slot_no(u), :].rearrange("p (t n) -> p t n", t=16)

        loaded = [sem(f"loaded{s}") for s in range(NSLOT)]
        x_loaded, tables_loaded, small_loaded = sem("x_loaded"), sem("tables_loaded"), sem("small_loaded")
        norm_loaded = sem2("norm_loaded")
        mask_row, rel_loaded = sem("mask_row"), sem("rel_loaded")
        dist_ready, dist_copied, dist_stored, hankel_loaded = (
            sem("dist_ready"), sem("dist_copied"), sem("dist_stored"), sem("hankel_loaded"))
        flipped, bias_copied = sem("flipped"), sem("bias_copied")
        xT_ready, xT_dve, xT_act = (sem(n) for n in ("xT_ready", "xT_dve", "xT_act"))
        proj_ready, proj_dve, proj_act = sem2("proj_ready"), sem2("proj_dve"), sem2("proj_act")
        scores_ready, scores_read = sem2("scores_ready"), sem2("scores_read")
        max_ready, exp_ready, probs_ready = sem2("max_ready"), sem2("exp_ready"), sem2("probs_ready")
        probsT_ready, probsT_copied = sem2("probsT_ready"), sem2("probsT_copied")
        pv_done, o_ready, o_copied = sem2("pv_done"), sem2("o_ready"), sem2("o_copied")
        mix_ready = sem2("mix_ready")
        var_ready, std_ready = sem("var_ready"), sem("std_ready")
        norm_done = sem("norm_done")
        gate_ready, gate_exp, gates_ready = sem("gate_ready"), sem("gate_exp"), sem("gates_ready")
        cpos_ready, cpos_copied = sem("cpos_ready"), sem("cpos_copied")
        cin_copied, cin_ready = sem("cin_copied"), sem("cin_ready")
        chid_psum, chid_ready = sem("chid_psum"), sem("chid_ready")
        ckv_psum, ckv_ready = sem("ckv_psum"), sem("ckv_ready")
        cs_ready, cs_centred, cs_exp, cp_ready = sem("cs_ready"), sem("cs_centred"), sem("cs_exp"), sem("cp_ready")
        cpT_psum, cpT_dve, cpT_act = sem("cpT_psum"), sem("cpT_dve"), sem("cpT_act")
        logits_ready, logits_shifted, logits_exp = sem2("logits_ready"), sem2("logits_shifted"), sem2("logits_exp")
        chosen_ready, ranks_ready, flag_ready = sem2("chosen_ready"), sem2("ranks_ready"), sem2("flag_ready")
        pick_ready, pickw_ready, pickwT_psum, pickwT_ready = (
            sem2("pick_ready"), sem2("pickw_ready"), sem2("pickwT_psum"), sem2("pickwT_ready"))
        gathered, xg_dve, xg_act = sem2("gathered"), sem2("xg_dve"), sem2("xg_act")
        gate_done, up_done, silu_ready, hid_ready = (
            sem2("gate_done"), sem2("up_done"), sem2("silu_ready"), sem2("hid_ready"))
        hidT_psum, hidT_ready = sem2("hidT_psum"), sem2("hidT_ready")
        down_done, y_dve, y_act = sem2("down_done"), sem2("y_dve"), sem2("y_act")
        spread_ready, acc_added, acc_started = sem2("spread_ready"), sem2("acc_added"), sem2("acc_started")
        dve_chain = sem("dve_chain")
        ov_loaded = [sem2(f"ov_loaded{s}") for s in range(3)]
        ov_pe, ov_dve, ov_act = sem2("ov_pe"), sem2("ov_dve"), sem2("ov_act")
        ov_silu, ov_chain = sem2("ov_silu"), sem2("ov_chain")
        stored = sem("stored")

        freed = {}
        for l, uses in enumerate((moba_uses, nsa_uses)):
            for n in range(len(uses) - 2):
                freed[first_use[l] + n] = (proj_ready[l], 2 * n + 2)
            for n in (0, 1):
                freed[first_use[l] + len(uses) - 2 + n] = (mix_ready[l], 4 * (n + 1))

        for b in range(2):
            freed[first_use[1] + 5 + b] = (chid_psum, b + 1)

        PAIR_USES = [("gate", 0), ("gate", 1), ("up", 0), ("up", 1), ("down", 0), ("down", 1)]

        def pair_freed(l, j, i):
            kind, _ = PAIR_USES[j]
            if kind == "down":
                return down_done[l], 2 * i + 2
            return (gate_done if kind == "gate" else up_done)[l], i + 1

        def slot_for(kind, s):
            r = ring[:, s, :]
            return r.rearrange("p (t n) -> p t n", t=4 if kind == "down" else KT)

        def copy_cmp_in(copy, b, ps):
            for hkv in range(KV):
                for o in range(2):
                    src = ps[DH * (hkv % 2):DH * (hkv % 2) + DH, (hkv // 2) * SEQ + o:(hkv // 2) * SEQ + o + 1]
                    src = bass.AP(tensor=src.tensor, offset=src.offset, ap=[list(src.ap[0]), [2, 16], [CMP_STRIDE, N_CMP]])
                    last = copy(cmp_in[DH * o:DH * o + DH, b, :, hkv * N_CMP:(hkv + 1) * N_CMP], src)
            return last

        block = ctx.enter_context(nc.Block())

        @block.sync
        def _(sp):
            def load_fixed(l, uses):
                for n, src in enumerate(uses):
                    u = first_use[l] + n
                    if u >= NSLOT:
                        sp.wait_ge(*released(u - NSLOT))
                    dst = ring[:, slot_no(u), :].rearrange("p (t n) -> p t n", t=src.shape[1])
                    sp.dma_start(dst, src).then_inc(loaded[slot_no(u)], 16)

            def released(u):
                if u in freed:
                    return freed[u]
                l = 0 if u < first_use[1] else 1
                i, j = divmod(u - first_moe[l], USES_PER_PAIR)
                return pair_freed(l, j, i)

            def load_pair(l, i, j):
                kind, e = PAIR_USES[j]
                s = slot_no(first_moe[l] + j)
                src = (moe_w_down if kind == "down" else moe_w_gate if kind == "gate" else moe_w_up)[
                    l, bass.ds(2 * i + e, 1), :, :]
                if kind == "down":
                    src = src.rearrange("a (m p) n -> p (a m) n", p=P)
                else:
                    src = src.rearrange("a (p t) n -> p (a t) n", t=KT)
                sp.dma_start(slot_for(kind, s), src).then_inc(loaded[s], 16)

            sp.dma_start(xs[:, :, :], x_in[0].rearrange("(t p) d -> p t d", p=P)).then_inc(x_loaded, 16)
            sp.dma_start(tab[:, :], tables[:, 0:place["bucket"][0]]).then_inc(tables_loaded, 16)
            sp.dma_start(bucket_rows, tables[0:BUCKETS + 1, place["bucket"][0]:place["bucket"][1]]).then_inc(tables_loaded, 16)
            for l, uses in enumerate((moba_uses, nsa_uses)):
                load_fixed(l, uses)
                for j in range(USES_PER_PAIR):
                    sp.wait_ge(*released(first_moe[l] + j - NSLOT))
                    load_pair(l, 0, j)
                with sp.Fori(1, PAIRS) as i:
                    for j in range(USES_PER_PAIR):
                        s, n = pair_freed(l, j, i - 1)
                        sp.wait_ge(s, n)
                        load_pair(l, i, j)
                if True:
                    sp.wait_ge(flag_ready[l], 1)
                    flag = sp.value_load(crowded_i[0:1, 0:1], min_val=0, max_val=1)
                    with sp.If(flag > 0):
                        for j in range(USES_PER_PAIR):
                            sp.wait_ge(*pair_freed(l, j, PAIRS - 1))
                        with sp.Fori(0, E) as e:
                            sp.wait_ge(ov_pe[l], e * OV_PE + 1)
                            for s, (kind, w) in enumerate((("gate", moe_w_gate), ("up", moe_w_up), ("down", moe_w_down))):
                                src = w[l, bass.ds(e, 1), :, :]
                                if kind == "down":
                                    src = src.rearrange("a (m p) n -> p (a m) n", p=P)
                                else:
                                    src = src.rearrange("a (p t) n -> p (a t) n", t=KT)
                                sp.dma_start(slot_for(kind, s), src).then_inc(ov_loaded[s][l], 16)
                        sp.wait_ge(ov_pe[l], E * OV_PE + 1)
                    with sp.Else():
                        sp.nop()
            sp.wait_ge(norm_done, 2 * 2 * NT)
            sp.dma_start(out[0].rearrange("(t p) d -> p t d", p=P), xs[:, :, :]).then_inc(stored, 16)
            sp.wait_ge(stored, 16)

        @block.gpsimd
        def _(pool):
            nc.gpsimd.memset(rel_w[BUCKETS:BUCKETS + 1, :], NEG).then_inc(mask_row, 1)
            pool.dma_start(rel_w[0:BUCKETS, :], rel_bias).then_inc(rel_loaded, 16)
            pool.dma_start(router[:, :, :], router_w.rearrange("(p t) n -> p t n", t=KT)).then_inc(small_loaded, 16)
            pool.dma_start(router_bias[:, :], bass.AP(tensor=router_b.tensor, offset=0, ap=[[0, P], [1, E]])).then_inc(small_loaded, 16)
            for b, src in enumerate((nsa_pos_k, nsa_pos_v)):
                pool.dma_start(pos_rows[:, b, :], src[0].rearrange("(l o) d -> l (o d)", o=2)).then_inc(small_loaded, 16)
            for b, src in enumerate((nsa_ck_w2, nsa_cv_w2)):
                pool.dma_start(cmp_w2[:, b, :, :], src[0].rearrange("(f p) d -> p f d", p=P)).then_inc(small_loaded, 16)
            pool.wait_ge(dist_copied, 1)
            pool.dma_start(dist_dram.ap(), dist_row).then_inc(dist_stored, 16)
            pool.wait_ge(dist_stored, 16)
            pool.dma_start(hankel, bass.AP(tensor=dist_dram.ap().tensor, offset=0, ap=[[1, P], [BIAS_W, HEADS], [1, SEQ]])).then_inc(hankel_loaded, 16)
            pool.dma_start(gate_w[:, :, :], nsa_w_in[0][:, 2560:2608].rearrange("(p t) n -> p t n", t=KT)).then_inc(small_loaded, 16)
            for l in range(LAYERS):
                if l:
                    pool.wait_ge(norm_done, 2 * NT * l)
                for n in range(2):
                    for w, src in enumerate((ln_g, ln_b)):
                        pool.dma_start(norm_w[:, n, w, :], bass.AP(tensor=src.tensor, offset=(2 * l + n) * D, ap=[[0, P], [1, D]])).then_inc(norm_loaded[l], 16)


        @block.tensor
        def _(pe):
            mm, tr = nc.tensor.matmul, nc.tensor.transpose

            def arrived(u):
                pe.wait_ge(loaded[slot_no(u)], 16 * (u // NSLOT + 1))

            def transpose_x(n):
                for j in range(4):
                    g = 4 * n + j
                    after(pe, xT_dve if g % 2 == 0 else xT_act, g // 2)
                    for t in (2 * j, 2 * j + 1):
                        for tt in range(NT):
                            c = (t % 2) * SEQ + tt * P
                            last = tr(bank[4 + g % 2][:, c:c + P], xs[:, tt, t::KT], ident)
                    last.then_inc(xT_ready, 1)

            def xT_copied(n):
                pe.wait_ge(xT_dve, 2 * (n + 1))
                pe.wait_ge(xT_act, 2 * (n + 1))

            def proj_bank_free(l, g):
                after(pe, proj_dve[l] if g % 2 == 0 else proj_act[l], g // 2)

            def project_T(l, g, w, lhs_cols):
                proj_bank_free(l, g)
                for n, pick_cols in enumerate(lhs_cols):
                    for t in range(KT):
                        last = mm(bank[g % 2][:, n * SEQ:(n + 1) * SEQ], pick_cols(w, t), xT[:, t, :],
                                  start=(t == 0), stop=(t == KT - 1))
                return last

            def project_tok(l, g, w, tt, width=512):
                proj_bank_free(l, g)
                for t in range(KT):
                    last = mm(bank[g % 2][:, 0:width], xT[:, t, tt * P:(tt + 1) * P], w[:, t, 0:width],
                              start=(t == 0), stop=(t == KT - 1))
                return last

            def tile_cols(m):
                return lambda w, t: w[:, t, m * P:(m + 1) * P]

            def attention(l, jobs, extra):
                for s in range(len(jobs) + 3):
                    if s < len(jobs):
                        if s >= 2:
                            pe.wait_ge(scores_read[l], s - 1)
                        q, k = jobs[s]["q"], jobs[s]["k"]
                        ps = bank[2 + s % 2]
                        mm(ps[:, 0:P], q[:, 0:P], k[:, 0:P], start=True, stop=True)
                        mm(ps[:, P:3 * P], q[:, P:SEQ], k[:, :], start=True, stop=True).then_inc(scores_ready[l], 1)
                    if 0 <= s - 2 < len(jobs):
                        j = s - 2
                        pe.wait_ge(probs_ready[l], j + 1)
                        if j >= 2:
                            pe.wait_ge(probsT_copied[l], j - 1)
                        for b in range(3):
                            last = tr(bank[4 + j % 2][:, b * P:(b + 1) * P], probs[:, j % 4, b * P:(b + 1) * P], ident)
                        last.then_inc(probsT_ready[l], 1)
                    if 0 <= s - 3:
                        j = s - 3
                        job = jobs[j]
                        h = job["head"]
                        pe.wait_ge(probsT_copied[l], j + 1)
                        if job["first"] and h % 2 == 0 and h >= 4:
                            pe.wait_ge(o_copied[l], h // 2 - 1)
                        half = DH * (h % 2)
                        ps = bank[6 + (h // 2) % 2][half:half + DH, :]
                        pt = probsT[:, j % 2, :, :].rearrange("p b q -> p (b q)")
                        last_job = job["last"]
                        mm(ps[:, 0:SEQ], job["v"](0), pt[:, 0:SEQ], start=job["first"], stop=False)
                        last = mm(ps[:, P:SEQ], job["v"](1), pt[:, SEQ:3 * P], start=False, stop=last_job and not extra)
                        last.then_inc(pv_done[l], 1)
                        if last_job and extra:
                            extra(h, ps[:, 0:SEQ]).then_inc(o_ready[l], 1)

            def out_proj(l):
                pe.wait_ge(o_copied[l], HEADS // 2)
                u = first_moe[l] - 2
                for c in (0, 1):
                    arrived(u + c)
                    for tt in range(NT):
                        for n in range(2):
                            for t in range(4):
                                last = mm(bank[2 * tt + n][:, :], oT[:, 4 * c + t, tt * P:(tt + 1) * P],
                                          slot4(u + c)[:, t, n * 512:(n + 1) * 512],
                                          start=(c == 0 and t == 0), stop=(c == 1 and t == 3))
                            last.then_inc(mix_ready[l], 1)

            def route_tokens(l):
                transpose_x(2 * l + 1)
                xT_copied(2 * l + 1)
                pe.wait_ge(small_loaded, SMALL_LOADS)
                for tt in range(NT):
                    for t in range(KT):
                        last = mm(bank[6][:, tt * E:(tt + 1) * E], xT[:, t, tt * P:(tt + 1) * P], router[:, t, :],
                                  start=(t == 0), stop=(t == KT - 1))
                last.then_inc(logits_ready[l], 1)
                pe.wait_ge(chosen_ready[l], 1)
                mm(bank[7][:, 0:E], table("before"), chosen[:, 0, :], start=True, stop=True)
                mm(bank[7][:, E:2 * E], table("ones"), chosen[:, 0, :], start=True, stop=False)
                mm(bank[7][:, E:2 * E], table("before"), chosen[:, 1, :], start=False, stop=True)
                mm(bank[7][:, 2 * E:3 * E], table("ones"), chosen[:, 0, :], start=True, stop=False)
                mm(bank[7][:, 2 * E:3 * E], table("ones"), chosen[:, 1, :], start=False, stop=True).then_inc(ranks_ready[l], 1)

            SPREAD_BANKS = [4, 0, 1, 7]

            def gather(l, i):
                pe.wait_ge(pick_ready[l], i + 1)
                for half in range(2):
                    after(pe, acc_added[l], 4 * (i - 2) + 2 + half)
                    for t in range(4):
                        for tt in range(NT):
                            last = mm(bank[half][:, t * P:(t + 1) * P], xs[:, tt, 4 * half + t::KT],
                                      pick[:, tt, :, :].rearrange("p e s -> p (e s)"), start=(tt == 0), stop=(tt == 1))
                    last.then_inc(gathered[l], 1)

            def gate_up(l, i, use):
                pe.wait_ge(xg_dve[l], i + 1)
                pe.wait_ge(xg_act[l], i + 1)
                for k, done, read in ((0, gate_done, silu_ready), (1, up_done, hid_ready)):
                    after(pe, read[l], i)
                    for e in range(2):
                        use(2 * k + e)
                    for t in range(KT):
                        for e in range(2):
                            last = mm(bank[2 + k][e * CAP:(e + 1) * CAP, :], xgT[:, t, e * CAP:(e + 1) * CAP],
                                      slot8(first_moe[l] + 2 * k + e)[:, t, :], start=(t == 0), stop=(t == KT - 1))
                    last.then_inc(done[l], 1)

            def transpose_hidden(l, i):
                pe.wait_ge(hid_ready[l], i + 1)
                after(pe, acc_added[l], 4 * (i - 1) + 1)
                for m in range(FT):
                    last = tr(bank[4][:, m * P:(m + 1) * P], hid[:, m * P:(m + 1) * P], ident)
                last.then_inc(hidT_psum[l], 1)

            def weights_by_slot(l, i):
                pe.wait_ge(pickw_ready[l], i + 1)
                after(pe, acc_added[l], 4 * i)
                for tt in range(NT):
                    last = tr(bank[7][:, tt * P:(tt + 1) * P], pick_w[:, tt, :, :].rearrange("p e s -> p (e s)"), ident)
                last.then_inc(pickwT_psum[l], 1)

            def down(l, i, use):
                pe.wait_ge(hidT_ready[l], i + 1)
                for e in range(2):
                    use(4 + e)
                for n in range(2):
                    for m in range(FT):
                        for e in range(2):
                            last = mm(bank[5 + n][e * CAP:(e + 1) * CAP, :], hidT[:, m, e * CAP:(e + 1) * CAP],
                                      slot4(first_moe[l] + 4 + e)[:, m, n * 512:(n + 1) * 512], start=(m == 0), stop=(m == FT - 1))
                    last.then_inc(down_done[l], 1)

            def spread(l, i):
                pe.wait_ge(y_dve[l], i + 1)
                pe.wait_ge(y_act[l], i + 1)
                pe.wait_ge(pickwT_ready[l], i + 1)
                for k, b in enumerate(SPREAD_BANKS):
                    tt, n = divmod(k, 2)
                    mm(bank[b][:, :], pick_wT[:, tt, :], y_slot[:, n * 512:(n + 1) * 512], start=True, stop=True).then_inc(spread_ready[l], 1)

            def experts(l):
                def pair(i, first, last):
                    def use(j):
                        u = first_moe[l] + j
                        pe.wait_ge(loaded[slot_no(u)], 16 * (u // NSLOT + 1) + 16 * i)
                    gate_up(l, i, use)
                    if not first:
                        spread(l, i - 1)
                    transpose_hidden(l, i)
                    if not last:
                        gather(l, i + 1)
                    weights_by_slot(l, i)
                    down(l, i, use)

                gather(l, 0)
                pair(0, True, False)
                with pe.Fori(1, PAIRS - 1) as i:
                    pair(i, False, False)
                pair(PAIRS - 1, False, True)
                spread(l, PAIRS - 1)

            def overflow(l):
                pe.wait_ge(flag_ready[l], 1)
                flag = pe.value_load(crowded_i[0:1, 0:1], min_val=0, max_val=1)
                with pe.If(flag > 0):
                    pe.wait_ge(acc_added[l], 4 * PAIRS)
                    tr(bank[6][:, 0:P], ident, ident).then_inc(ov_pe[l], 1)
                    with pe.Fori(0, E) as e:
                        for s in range(3):
                            pe.wait_ge(ov_loaded[s][l], 16 * e + 16)
                        for r in range(2):
                            n = e * 12 + 6 * r
                            m = e * 4 + 2 * r
                            pe.wait_ge(ov_dve[l], n + 2)
                            for half in range(2):
                                for t in range(4):
                                    for tt in range(NT):
                                        mm(bank[half][:, t * P:(t + 1) * P], xs[:, tt, 4 * half + t::KT],
                                           pick[:, tt, :, :].rearrange("p e s -> p (e s)"), start=(tt == 0), stop=(tt == 1))
                            for tt in range(NT):
                                last = tr(bank[2][:, tt * P:(tt + 1) * P], pick_w[:, tt, :, :].rearrange("p e s -> p (e s)"), ident)
                            last.then_inc(ov_pe[l], 1)
                            pe.wait_ge(ov_dve[l], n + 3)
                            pe.wait_ge(ov_act[l], m + 1)
                            for k in range(2):
                                w = ring[:, k, :].rearrange("p (t n) -> p t n", t=KT)
                                for mt in range(FT):
                                    for t in range(KT):
                                        last = mm(bank[2 + k][:, mt * P:(mt + 1) * P], w[:, t, mt * P:(mt + 1) * P], xgT[:, t, :],
                                                  start=(t == 0), stop=(t == KT - 1))
                            last.then_inc(ov_pe[l], 1)
                            pe.wait_ge(ov_dve[l], n + 4)
                            w = ring[:, 2, :].rearrange("p (t n) -> p t n", t=4)
                            hid_all = hid.rearrange("p (m s) -> p m s", s=P)
                            for c in range(KT):
                                for mt in range(FT):
                                    last = mm(bank[4 + c // 4][:, (c % 4) * P:(c % 4 + 1) * P], w[:, mt, c * P:(c + 1) * P],
                                              hid_all[:, mt, :], start=(mt == 0), stop=(mt == FT - 1))
                            last.then_inc(ov_pe[l], 1)
                            pe.wait_ge(ov_dve[l], n + 5)
                            for c in range(KT):
                                last = tr(bank[6 + c // 4][:, (c % 4) * P:(c % 4 + 1) * P], yT[:, c, :], ident)
                            last.then_inc(ov_pe[l], 1)
                            pe.wait_ge(ov_act[l], m + 2)
                            for tt in range(NT):
                                for c in range(2):
                                    last = mm(bank[6 * (1 - tt) + c][:, :], pick_wT[:, tt, :], y_slot[:, c * 512:(c + 1) * 512],
                                              start=True, stop=True)
                            last.then_inc(ov_pe[l], 1)
                            pe.wait_ge(ov_dve[l], n + 6)
                            tr(bank[6][:, 0:P], ident, ident).then_inc(ov_pe[l], 1)
                with pe.Else():
                    pe.nop()

            pe.wait_ge(tables_loaded, 32)
            pe.wait_ge(rel_loaded, 16)
            pe.wait_ge(mask_row, 1)
            mm(bank[6][0:HEADS, 0:BIAS_W], rel_w[:, :], bucket_rows, start=True, stop=True).then_inc(dist_ready, 1)
            pe.wait_ge(x_loaded, 16)
            transpose_x(0)
            xT_copied(0)
            for g in range(12):
                u, part = divmod(g, 2)
                if part == 0:
                    arrived(u)
                if u % 3 < 2:
                    last = project_T(0, g, slot8(u), [tile_cols(2 * part), tile_cols(2 * part + 1)])
                else:
                    last = project_tok(0, g, slot8(u), part)
                last.then_inc(proj_ready[0], 1)
                if g == 3:
                    pe.wait_ge(hankel_loaded, 16)
                    for j in range(HEADS // 2):
                        b = bank[6] if j % 2 == 0 else bank[5]
                        if j >= 2:
                            pe.wait_ge(bias_copied, j - 1)
                        mm(b[:, :], flip, hankel[:, 2 * j:2 * j + 2, :].rearrange("p h k -> p (h k)"),
                           start=True, stop=True).then_inc(flipped, 1)
            pe.wait_ge(proj_dve[0], 6)
            pe.wait_ge(proj_act[0], 6)
            pe.wait_ge(bias_copied, 8)

            def moba_job(h):
                half = slice(DH * (h % 2), DH * (h % 2) + DH)
                return dict(head=h, first=True, last=True, q=qT[half, h // 2, :], k=kT[half, h // 2, :],
                            v=lambda kt: v_tok[:, kt, h * DH:(h + 1) * DH])
            attention(0, [moba_job(h) for h in range(HEADS)], None)
            out_proj(0)
            pe.wait_ge(norm_done, NT)
            route_tokens(0)
            experts(0)
            overflow(0)

            pe.wait_ge(norm_done, 2 * NT)
            transpose_x(2)
            xT_copied(2)
            u0 = first_use[1]
            for g in range(12):
                c, part = divmod(g, 2)
                if part == 0 and c < 5:
                    arrived(u0 + c)
                w = slot8(u0 + c)
                if c < 3:
                    last = project_T(1, g, w, [tile_cols(2 * part), tile_cols(2 * part + 1)])
                elif c < 5 and part == 0:
                    last = project_T(1, g, w, [tile_cols(0), tile_cols(1)])
                elif c < 5:
                    proj_bank_free(1, g)
                    for tt in range(NT):
                        for t in range(KT):
                            last = mm(bank[g % 2][:, tt * 256:(tt + 1) * 256], xT[:, t, tt * P:(tt + 1) * P], w[:, t, 256:512],
                                      start=(t == 0), stop=(t == KT - 1))
                elif part == 0:
                    proj_bank_free(1, g)
                    for tt in range(NT):
                        for t in range(KT):
                            last = mm(bank[g % 2][:, tt * 48:(tt + 1) * 48], xT[:, t, tt * P:(tt + 1) * P], gate_w[:, t, :],
                                      start=(t == 0), stop=(t == KT - 1))
                else:
                    continue
                last.then_inc(proj_ready[1], 1)
            for b in range(2):
                last = tr(bank[6][:, b * 16:(b + 1) * 16], pos_rows[:, b, :], ident[0:16, 0:16])
            last.then_inc(cpos_ready, 1)
            pe.wait_ge(cin_ready, 1)
            for b in range(2):
                arrived(u0 + 5 + b)
                w = slot16(u0 + 5 + b)
                for f in range(2):
                    for lp in range(16):
                        last = mm(bank[2 + b][:, f * 64:f * 64 + KV * N_CMP], w[:, lp, f * P:(f + 1) * P], cmp_in[:, b, lp, :],
                                  start=(lp == 0), stop=(lp == 15))
                last.then_inc(chid_psum, 1)
            pe.wait_ge(chid_ready, 2)
            for hp in (0, DH):
                for hkv in range(KV):
                    for f in range(2):
                        mm(bank[4][hp:hp + DH, hkv * 16:hkv * 16 + N_CMP], cmp_w2[:, 0, f, :],
                           cmp_hid[:, 0, f, hkv * N_CMP:(hkv + 1) * N_CMP], start=(f == 0), stop=(f == 1))
            for g in range(GROUP):
                for hkv in range(KV):
                    for f in range(2):
                        last = mm(bank[5][32 * g:32 * g + N_CMP, hkv * DH:(hkv + 1) * DH],
                                  cmp_hid[:, 1, f, hkv * N_CMP:(hkv + 1) * N_CMP], cmp_w2[:, 1, f, :], start=(f == 0), stop=(f == 1))
            last.then_inc(ckv_psum, 1)
            pe.wait_ge(ckv_ready, 1 + GROUP)
            pe.wait_ge(proj_dve[1], 5)
            pe.wait_ge(proj_act[1], 5)
            for tt in range(NT):
                for h in range(HEADS):
                    half = slice(DH * (h % 2), DH * (h % 2) + DH)
                    c = (tt * HEADS // 2 + h // 2) * 16
                    last = mm(bank[2 + h % 2][:, c:c + N_CMP],
                              qT[half, h // 2, tt * P:(tt + 1) * P], cmp_keyT[half, h // GROUP, 0:N_CMP], start=True, stop=True)
            last.then_inc(cs_ready, 1)
            pe.wait_ge(cp_ready, 1)
            for b in range(2):
                for tt in range(NT):
                    for g in (2 * b, 2 * b + 1):
                        last = tr(bank[4 + b][:, (g % 2) * SEQ + tt * P:(g % 2) * SEQ + (tt + 1) * P],
                                  cmp_p[:, tt, 4 * g:4 * g + 4, :].rearrange("p h n -> p (h n)"), ident)
                last.then_inc(cpT_psum, 1)
            pe.wait_ge(cpT_dve, 1)
            pe.wait_ge(cpT_act, 1)
            pe.wait_ge(gates_ready, 1)

            def nsa_job(h, b):
                hkv, g = divmod(h, GROUP)
                half = slice(DH * (h % 2), DH * (h % 2) + DH)
                return dict(head=h, first=b == 0, last=b == 1, q=qT[half, h // 2, :],
                            k=nsa_kT[half, b, 2 * (hkv % 2) + hkv // 2, :], v=lambda kt: nsa_v[:, b, kt, hkv * DH:(hkv + 1) * DH])

            def compressed(h, ps):
                hkv, g = divmod(h, GROUP)
                at = slice(32 * g, 32 * g + N_CMP)
                return mm(ps, cmp_val[at, hkv, :], cmp_pT[at, hkv, :], start=False, stop=True)
            attention(1, [nsa_job(h, b) for h in range(HEADS) for b in range(2)], compressed)
            out_proj(1)
            pe.wait_ge(norm_done, 3 * NT)
            route_tokens(1)
            experts(1)
            overflow(1)

        @block.vector
        def _(dve):
            v = nc.vector
            links = [0]

            def link(ins):
                links[0] += 1
                ins.then_inc(dve_chain, 1)
                dve.wait_ge(dve_chain, links[0])

            def xT_copy(n):
                for j in (0, 2):
                    dve.wait_ge(xT_ready, 4 * n + j + 1)
                    v.tensor_copy(xT[:, 2 * j:2 * j + 2, :].rearrange("p t q -> p (t q)"), bank[4][:, :]).then_inc(xT_dve, 1)

            def softmax_jobs(l, jobs, scale):
                for s in range(len(jobs) + 1):
                    if s < len(jobs):
                        h = jobs[s]
                        dve.wait_ge(scores_ready[l], s + 1)
                        if s >= 4:
                            dve.wait_ge(probsT_ready[l], s - 3)
                        ps, pr = bank[2 + s % 2], probs[:, s % 4, :]
                        for tt, (a, b) in enumerate(((0, P), (P, 3 * P))):
                            last = v.tensor_tensor_reduce(
                                out=pr[:, a:b], in0=ps[:, a:b], in1=bias[:, h, P - tt * P:SEQ], scale=1.0, scalar=-3e38,
                                op0=ALU.add, op1=ALU.max, accum_out=job_max[:, s % 4, tt:tt + 1])
                        last.then_inc(scores_read[l], 1)
                        dve.wait_ge(scores_read[l], s + 1)
                        v.tensor_scalar(job_max[:, s % 4, :], job_max[:, s % 4, :], -1.0, None, ALU.mult).then_inc(max_ready[l], 1)
                    if s >= 1:
                        j = s - 1
                        dve.wait_ge(exp_ready[l], 2 * j + 2)
                        link(v.reciprocal(job_scale[:, j % 4, :], job_sum[:, j % 4, :]))
                        if scale:
                            link(v.tensor_tensor(job_scale[:, j % 4, :], job_scale[:, j % 4, :], scale(j), ALU.mult))
                        for tt, (a, b) in enumerate(((0, P), (P, 3 * P))):
                            last = v.tensor_scalar(probs[:, j % 4, a:b], probs[:, j % 4, a:b], job_scale[:, j % 4, tt:tt + 1], None, ALU.mult)
                        last.then_inc(probs_ready[l], 1)
                    copy_o(l, len(jobs) // HEADS, s - 4)

            def copy_o(l, per_head, j):
                if j >= 0 and (j + 1) % (2 * per_head) == 0:
                    m = (j + 1) // (2 * per_head) - 1
                    dve.wait_ge(*((o_ready[l], 2 * (m + 1)) if per_head == 2 else (pv_done[l], 2 * (m + 1))))
                    v.tensor_copy(oT[:, m, :], bank[6 + m % 2][:, 0:SEQ]).then_inc(o_copied[l], 1)

            def finish_o(l, n_jobs):
                for j in range(n_jobs - 3, n_jobs):
                    copy_o(l, n_jobs // HEADS, j)

            def residual(l):
                for tt in range(NT):
                    for n in range(2):
                        dve.wait_ge(mix_ready[l], 4 + 2 * tt + n + 1)
                        c = slice(n * 512, (n + 1) * 512)
                        link(v.scalar_tensor_tensor(acc[:, tt, c], xs[:, tt, c], ALPHA, bank[2 * tt + n][:, :], ALU.mult, ALU.add))

            def norm(l, n):
                dve.wait_ge(norm_loaded[l], 64)
                for tt in range(NT):
                    for c in range(2):
                        last = v.bn_stats(stats[:, tt, 6 * c:6 * c + 6], acc[:, tt, c * 512:(c + 1) * 512])
                link(last)
                for tt in range(NT):
                    last = v.bn_aggr(moments[:, tt, :], stats[:, tt, :])
                link(last)
                v.tensor_scalar(rstd[:, :], moments[:, :, 1], EPS, None, ALU.add).then_inc(var_ready, 1)
                dve.wait_ge(std_ready, 2 * l + n + 1)
                link(v.reciprocal(rstd[:, :], rstd[:, :]))
                for tt in range(NT):
                    link(v.tensor_scalar(acc[:, tt, :], acc[:, tt, :], moments[:, tt, 0:1], rstd[:, tt:tt + 1], ALU.subtract, ALU.mult))
                    link(v.tensor_tensor(acc[:, tt, :], acc[:, tt, :], norm_w[:, n, 0, :], ALU.mult))
                    v.tensor_tensor(xs[:, tt, :], acc[:, tt, :], norm_w[:, n, 1, :], ALU.add).then_inc(norm_done, 1)

            def route_tokens(l):
                dve.wait_ge(norm_done, 2 * NT * l + NT)
                v.tensor_scalar(acc[:, :, :].rearrange("p t d -> p (t d)"), xs[:, :, :].rearrange("p t d -> p (t d)"),
                                ALPHA, None, ALU.mult).then_inc(acc_started[l], 1)
                xT_copy(2 * l + 1)

                def wide(x):
                    return x.unsqueeze(2).to_broadcast([P, NT, E])

                def flat_table(name, n):
                    return table(name).unsqueeze(1).to_broadcast([P, NT, n])

                pr = route[:, 0, :, :]
                dve.wait_ge(logits_ready[l], 1)
                link(v.tensor_tensor(pr, bank[6][:, 0:NT * E].rearrange("p (t e) -> p t e", e=E),
                                     router_bias[:, :].unsqueeze(1).to_broadcast([P, NT, E]), ALU.add))
                link(v.tensor_reduce(one[:, 0, :], pr, AX, ALU.max))
                v.tensor_tensor(pr, pr, wide(one[:, 0, :]), ALU.subtract).then_inc(logits_shifted[l], 1)
                dve.wait_ge(logits_exp[l], 1)
                link(v.tensor_reduce(one[:, 1, :], pr, AX, ALU.add))
                link(v.reciprocal(one[:, 2, :], one[:, 1, :]))
                link(v.tensor_tensor(pr, pr, wide(one[:, 2, :]), ALU.mult))
                g4 = pr.rearrange("p t (g e) -> p t g e", e=EG)
                pairs = [(small[:, 0, :, :], small[:, 1, :, :], 0), (small[:, 2, :, :], small[:, 3, :, :], 2)]
                for hi, lo, a in pairs:
                    v.tensor_tensor(hi, g4[:, :, :, a], g4[:, :, :, a + 1], ALU.max)
                    link(v.tensor_tensor(lo, g4[:, :, :, a], g4[:, :, :, a + 1], ALU.min))
                v.tensor_tensor(small[:, 4, :, :], small[:, 0, :, :], small[:, 2, :, :], ALU.max)
                v.tensor_tensor(small[:, 5, :, :], small[:, 0, :, :], small[:, 2, :, :], ALU.min)
                link(v.tensor_tensor(small[:, 6, :, :], small[:, 1, :, :], small[:, 3, :, :], ALU.max))
                link(v.tensor_tensor(small[:, 5, :, :], small[:, 5, :, :], small[:, 6, :, :], ALU.max))
                link(v.tensor_tensor(small[:, 7, :, :], small[:, 4, :, :], small[:, 5, :, :], ALU.add))
                def wide8(x):
                    return x.unsqueeze(2).to_broadcast([P, NT, NG])
                link(v.tensor_reduce(one[:, 3, :], small[:, 7, :, :], AX, ALU.max))
                link(v.tensor_tensor(small[:, 0, :, :], small[:, 7, :, :], wide8(one[:, 3, :]), ALU.is_equal))
                link(v.tensor_tensor(small[:, 0, :, :], small[:, 0, :, :], flat_table("first8", NG), ALU.mult))
                link(v.tensor_reduce(one[:, 3, :], small[:, 0, :, :], AX, ALU.max))
                link(v.tensor_tensor(small[:, 1, :, :], small[:, 0, :, :], wide8(one[:, 3, :]), ALU.is_equal))
                link(v.tensor_scalar(small[:, 2, :, :], small[:, 1, :, :], 4.0, -4.0, ALU.mult, ALU.add))
                cand = route[:, 1, :, :]
                link(v.tensor_tensor(cand.rearrange("p t (g e) -> p t g e", e=EG), g4,
                                     small[:, 2, :, :].unsqueeze(3).to_broadcast([P, NT, NG, EG]), ALU.add))
                hot = [route[:, 3, :, :], route[:, 4, :, :]]
                for k in range(2):
                    link(v.tensor_reduce(one[:, 4 + k, :], cand, AX, ALU.max))
                    link(v.tensor_tensor(route[:, 2, :, :], cand, wide(one[:, 4 + k, :]), ALU.is_equal))
                    link(v.tensor_tensor(route[:, 2, :, :], route[:, 2, :, :], flat_table("first32", E), ALU.mult))
                    link(v.tensor_reduce(one[:, 3, :], route[:, 2, :, :], AX, ALU.max))
                    link(v.tensor_tensor(hot[k], route[:, 2, :, :], wide(one[:, 3, :]), ALU.is_equal))
                    if k == 0:
                        link(v.scalar_tensor_tensor(cand, hot[0], -16.0, cand, ALU.mult, ALU.add))
                v.tensor_tensor(chosen[:, :, :], hot[0], hot[1], ALU.add).then_inc(chosen_ready[l], 1)
                link(v.tensor_tensor(one[:, 6, :], one[:, 4, :], one[:, 5, :], ALU.add))
                link(v.reciprocal(one[:, 7, :], one[:, 6, :]))
                for k in range(2):
                    link(v.tensor_tensor(one[:, 4 + k, :], one[:, 4 + k, :], one[:, 7, :], ALU.mult))
                    link(v.tensor_tensor(hot[k], hot[k], wide(one[:, 4 + k, :]), ALU.mult))
                link(v.tensor_tensor(weight[:, :, :], hot[0], hot[1], ALU.add))
                dve.wait_ge(ranks_ready[l], 1)
                ranks = bank[7][:, 0:NT * E].rearrange("p (t e) -> p t e", e=E)
                link(v.scalar_tensor_tensor(route[:, 5, :, :], ranks, 1.0, chosen[:, :, :], ALU.add, ALU.mult))
                link(v.tensor_scalar(slot_of[:, :, :], route[:, 5, :, :], -1.0, None, ALU.add))
                link(v.tensor_reduce(crowded[:, :], bank[7][:, NT * E:(NT + 1) * E], AX, ALU.max))
                link(v.tensor_scalar(crowded[:, :], crowded[:, :], float(CAP), None, ALU.is_gt))
                v.tensor_copy(crowded_i[:, :], crowded[:, :]).then_inc(flag_ready[l], 1)

            def choice(l, i):
                v.tensor_tensor(pick, table("slot").rearrange("p (e s) -> p e s", e=2).unsqueeze(1).to_broadcast([P, NT, 2, CAP]),
                                slot_of[:, :, bass.ds(2 * i, 2)].unsqueeze(3).to_broadcast([P, NT, 2, CAP]), ALU.is_equal).then_inc(pick_ready[l], 1)

            def experts(l):
                def hidden(i):
                    dve.wait_ge(up_done[l], i + 1)
                    dve.wait_ge(silu_ready[l], i + 1)
                    v.tensor_tensor(hid, silu, bank[3][:, :], ALU.mult).then_inc(hid_ready[l], 1)

                def add(i):
                    after(dve, acc_added[l], 4 * i)
                    for k, b in enumerate((4, 0, 1, 7)):
                        tt, n = divmod(k, 2)
                        dve.wait_ge(spread_ready[l], 4 * i + k + 1)
                        c = acc[:, tt, n * 512:(n + 1) * 512]
                        v.tensor_tensor(c, c, bank[b][:, :], ALU.add).then_inc(acc_added[l], 1)

                def copy_xg(i):
                    dve.wait_ge(gathered[l], 2 * i + 1)
                    v.tensor_copy(xgT[:, 0:4, :].rearrange("p t s -> p (t s)"), bank[0][:, :]).then_inc(xg_dve[l], 1)

                def copy_y(i):
                    dve.wait_ge(down_done[l], 2 * i + 1)
                    v.tensor_copy(y_slot[:, 0:512], bank[5][:, :]).then_inc(y_dve[l], 1)

                def pair(i, first, last):
                    if not first:
                        dve.wait_ge(pickwT_psum[l], i)
                    dve.wait_ge(pick_ready[l], i + 1)
                    v.tensor_tensor(pick_w, pick, weight[:, :, bass.ds(2 * i, 2)].unsqueeze(3).to_broadcast([P, NT, 2, CAP]),
                                    ALU.mult).then_inc(pickw_ready[l], 1)
                    if not last:
                        dve.wait_ge(pickw_ready[l], i + 1)
                        dve.wait_ge(gathered[l], 2 * i + 2)
                        choice(l, i + 1)
                    hidden(i)
                    if not first:
                        add(i - 1)
                    if not last:
                        copy_xg(i + 1)
                    copy_y(i)

                dve.wait_ge(acc_started[l], 1)
                choice(l, 0)
                copy_xg(0)
                pair(0, True, False)
                with dve.Fori(1, PAIRS - 1) as i:
                    pair(i, False, False)
                pair(PAIRS - 1, False, True)
                add(PAIRS - 1)
                dve.wait_ge(acc_added[l], 4 * PAIRS)

            def overflow(l):
                dve.wait_ge(flag_ready[l], 1)
                flag = dve.value_load(crowded_i[0:1, 0:1], min_val=0, max_val=1)
                flat = lambda x: x.rearrange("p t e s -> p t (e s)")
                with dve.If(flag > 0):
                    dve.wait_ge(ov_pe[l], 1)
                    with dve.Fori(0, E) as e:
                        for r in range(2):
                            n = e * 12 + 6 * r
                            k = e * 12 + 6 * r + 1
                            if r == 0:
                                dve.wait_ge(ov_pe[l], k)
                            v.tensor_scalar(route[:, 6, :, :], slot_of[:, :, :], -float(CAP + P * r), None, ALU.add).then_inc(ov_dve[l], 1)
                            dve.wait_ge(ov_dve[l], n + 1)
                            v.tensor_tensor(flat(pick), table("slot2").unsqueeze(1).to_broadcast([P, NT, P]),
                                            route[:, 6, :, bass.ds(e, 1)].to_broadcast([P, NT, P]), ALU.is_equal).then_inc(ov_chain[l], 1)
                            dve.wait_ge(ov_chain[l], e * 2 + r + 1)
                            v.tensor_tensor(flat(pick_w), flat(pick), weight[:, :, bass.ds(e, 1)].to_broadcast([P, NT, P]),
                                            ALU.mult).then_inc(ov_dve[l], 1)
                            dve.wait_ge(ov_pe[l], k + 1)
                            v.tensor_copy(xgT[:, 0:4, :].rearrange("p t s -> p (t s)"), bank[0][:, :])
                            v.tensor_copy(xgT[:, 4:8, :].rearrange("p t s -> p (t s)"), bank[1][:, :]).then_inc(ov_dve[l], 1)
                            dve.wait_ge(ov_silu[l], e * 2 + r + 1)
                            v.tensor_tensor(hid, silu, bank[3][:, :], ALU.mult).then_inc(ov_dve[l], 1)
                            dve.wait_ge(ov_pe[l], k + 3)
                            v.tensor_copy(yT[:, 0:4, :].rearrange("p t s -> p (t s)"), bank[4][:, :])
                            v.tensor_copy(yT[:, 4:8, :].rearrange("p t s -> p (t s)"), bank[5][:, :]).then_inc(ov_dve[l], 1)
                            dve.wait_ge(ov_pe[l], k + 5)
                            for tt in range(NT):
                                for c in range(2):
                                    a = acc[:, tt, c * 512:(c + 1) * 512]
                                    last = v.tensor_tensor(a, a, bank[6 * (1 - tt) + c][:, :], ALU.add)
                            last.then_inc(ov_dve[l], 1)
                            dve.wait_ge(ov_dve[l], n + 6)
                with dve.Else():
                    dve.nop()

            dve.wait_ge(dist_ready, 1)
            v.tensor_copy(dist_row, bank[6][0:HEADS, 0:BIAS_W]).then_inc(dist_copied, 1)
            xT_copy(0)
            for g in range(0, 12, 2):
                u = g // 2
                dve.wait_ge(proj_ready[0], g + 1)
                hh = u // 3
                if u % 3 == 0:
                    ins = v.tensor_scalar(qT[:, 4 * hh:4 * hh + 2, :].rearrange("p m q -> p (m q)"), bank[0][:, :], DH ** -0.5, None, ALU.mult)
                elif u % 3 == 1:
                    ins = v.tensor_copy(kT[:, 4 * hh:4 * hh + 2, :].rearrange("p m q -> p (m q)"), bank[0][:, :])
                else:
                    ins = v.tensor_copy(v_tok[:, 0, hh * 512:(hh + 1) * 512], bank[0][:, :])
                ins.then_inc(proj_dve[0], 1)
                if g == 2:
                    for j in range(HEADS // 2):
                        dve.wait_ge(flipped, j + 1)
                        b = bank[6] if j % 2 == 0 else bank[5]
                        v.tensor_copy(bias[:, 2 * j:2 * j + 2, :].rearrange("p h k -> p (h k)"), b[:, :]).then_inc(bias_copied, 1)
            dve.wait_ge(bias_copied, 8)
            softmax_jobs(0, list(range(HEADS)), None)
            finish_o(0, HEADS)
            residual(0)
            norm(0, 0)
            route_tokens(0)
            experts(0)
            overflow(0)
            norm(0, 1)

            xT_copy(2)
            for g in range(0, 12, 2):
                c = g // 2
                dve.wait_ge(proj_ready[1], g + 1)
                if c < 2:
                    ins = v.tensor_scalar(qT[:, 4 * c:4 * c + 2, :].rearrange("p m q -> p (m q)"), bank[0][:, :], DH ** -0.5, None, ALU.mult)
                elif c == 2:
                    ins = copy_cmp_in(nc.vector.tensor_copy, 0, bank[0])
                elif c < 5:
                    for dst in (0, DH):
                        for a in range(2):
                            ins = v.tensor_copy(nsa_kT[dst:dst + DH, c - 3, 2 * a:2 * a + 2, :].rearrange("p j q -> p (j q)"),
                                                bank[0][DH * a:DH * a + DH, :])
                else:
                    dve.wait_ge(gate_exp, 1)
                    link(v.tensor_scalar(gates[:, :, :], gates[:, :, :], 1.0, None, ALU.add))
                    ins = v.reciprocal(gates[:, :, :], gates[:, :, :])
                    ins.then_inc(gates_ready, 1)
                    break
                ins.then_inc(proj_dve[1], 1)
            dve.wait_ge(cpos_ready, 1)
            link(v.tensor_copy(pos_cols[:, :, :].rearrange("p b l -> p (b l)"), bank[6][:, 0:32]))
            dve.wait_ge(proj_dve[1], 3)
            dve.wait_ge(proj_act[1], 3)
            v.tensor_tensor(cmp_in, cmp_in, pos_cols[:, :, :].unsqueeze(3).to_broadcast([P, 2, 16, KV * N_CMP]), ALU.add).then_inc(cin_ready, 1)
            dve.wait_ge(ckv_psum, 1)
            v.memset(cmp_p, 0.0).then_inc(cs_centred, 1)
            v.tensor_copy(cmp_keyT[:, :, 0:N_CMP], bank[4][:, 0:16 * KV].rearrange("p (j n) -> p j n", n=16)[:, :, 0:N_CMP]).then_inc(ckv_ready, 1)
            for g in range(GROUP):
                at = slice(32 * g, 32 * g + N_CMP)
                v.tensor_copy(cmp_val[at, :, :].rearrange("p h d -> p (h d)"), bank[5][at, 0:KV * DH]).then_inc(ckv_ready, 1)
            dve.wait_ge(cs_ready, 1)
            dve.wait_ge(cs_centred, 1)
            cp = cmp_p[:, :, :, 0:N_CMP]
            for tt in range(NT):
                unseen = table("unseen")[:, 16 * tt:16 * tt + N_CMP].unsqueeze(1).to_broadcast([P, HEADS // 2, N_CMP])
                for odd in range(2):
                    link(v.tensor_tensor(cp[:, tt, odd::2, :],
                                         bank[2 + odd][:, tt * 128:(tt + 1) * 128].rearrange("p (h n) -> p h n", n=16)[:, :, 0:N_CMP],
                                         unseen, ALU.add))
            link(v.tensor_reduce(cmp_max[:, :, :], cp, AX, ALU.max))
            v.tensor_tensor(cp, cp, cmp_max[:, :, :].unsqueeze(3).to_broadcast([P, NT, HEADS, N_CMP]), ALU.subtract).then_inc(cs_centred, 1)
            dve.wait_ge(cs_exp, 1)
            link(v.tensor_reduce(cmp_sum[:, :, :], cp, AX, ALU.add))
            link(v.reciprocal(cmp_sum[:, :, :], cmp_sum[:, :, :]))
            dve.wait_ge(gates_ready, 1)
            gate3 = gates[:, :, :].rearrange("p t (h b) -> p t h b", b=3)
            link(v.tensor_tensor(cmp_sum[:, :, :], cmp_sum[:, :, :], gate3[:, :, :, 0], ALU.mult))
            for tt in range(NT):
                seen_tt = table("seen")[:, 16 * tt:16 * tt + N_CMP].unsqueeze(1).to_broadcast([P, HEADS, N_CMP])
                link(v.tensor_tensor(cp[:, tt, :, :], cp[:, tt, :, :], seen_tt, ALU.mult))
            v.tensor_tensor(cp, cp, cmp_sum[:, :, :].unsqueeze(3).to_broadcast([P, NT, HEADS, N_CMP]), ALU.mult).then_inc(cp_ready, 1)
            dve.wait_ge(cpT_psum, 1)
            v.tensor_copy(cmp_pT[:, 0:2, :].rearrange("p g q -> p (g q)"), bank[4][:, :]).then_inc(cpT_dve, 1)
            softmax_jobs(1, [h for h in range(HEADS) for _ in range(2)], lambda j: gate3[:, :, j // 2, 1 + j % 2])
            finish_o(1, 2 * HEADS)
            residual(1)
            norm(1, 0)
            route_tokens(1)
            experts(1)
            overflow(1)
            norm(1, 1)

        @block.scalar
        def _(act):
            s_ = nc.scalar

            def xT_copy(n):
                for j in (1, 3):
                    act.wait_ge(xT_ready, 4 * n + j + 1)
                    s_.copy(xT[:, 2 * j:2 * j + 2, :].rearrange("p t q -> p (t q)"), bank[5][:, :]).then_inc(xT_act, 1)

            def softmax_jobs(l, n_jobs):
                for s in range(n_jobs + 2):
                    if s < n_jobs:
                        act.wait_ge(max_ready[l], s + 1)
                        for tt, (a, b) in enumerate(((0, P), (P, 3 * P))):
                            pr = probs[:, s % 4, a:b]
                            s_.activation(pr, pr, ACT.Exp, bias=job_max[:, s % 4, tt:tt + 1],
                                          accum_out=job_sum[:, s % 4, tt:tt + 1]).then_inc(exp_ready[l], 1)
                    if s >= 2:
                        j = s - 2
                        act.wait_ge(probsT_ready[l], j + 1)
                        if j >= 2:
                            act.wait_ge(pv_done[l], j - 1)
                        s_.copy(probsT[:, j % 2, :, :].rearrange("p b q -> p (b q)"), bank[4 + j % 2][:, 0:3 * P]).then_inc(probsT_copied[l], 1)

            def norm(l, n):
                act.wait_ge(var_ready, 2 * l + n + 1)
                s_.activation(rstd[:, :], rstd[:, :], ACT.Sqrt).then_inc(std_ready, 1)

            def route_tokens(l):
                xT_copy(2 * l + 1)
                act.wait_ge(logits_shifted[l], 1)
                s_.activation(route[:, 0, :, :], route[:, 0, :, :], ACT.Exp).then_inc(logits_exp[l], 1)

            def experts(l):
                def gated(i):
                    act.wait_ge(gate_done[l], i + 1)
                    after(act, hid_ready[l], i)
                    s_.activation(silu, bank[2][:, :], ACT.Silu).then_inc(silu_ready[l], 1)

                def copy_hidT(i):
                    act.wait_ge(hidT_psum[l], i + 1)
                    s_.copy(hidT.rearrange("p m s -> p (m s)"), bank[4][:, :]).then_inc(hidT_ready[l], 1)

                def copy_xg(i):
                    act.wait_ge(gathered[l], 2 * i + 2)
                    s_.copy(xgT[:, 4:8, :].rearrange("p t s -> p (t s)"), bank[1][:, :]).then_inc(xg_act[l], 1)

                def copy_pickwT(i):
                    act.wait_ge(pickwT_psum[l], i + 1)
                    s_.copy(pick_wT.rearrange("p t q -> p (t q)"), bank[7][:, 0:SEQ]).then_inc(pickwT_ready[l], 1)

                def copy_y(i):
                    act.wait_ge(down_done[l], 2 * i + 2)
                    s_.copy(y_slot[:, 512:1024], bank[6][:, :]).then_inc(y_act[l], 1)

                def pair(i, first, last):
                    gated(i)
                    copy_hidT(i)
                    if not last:
                        copy_xg(i + 1)
                    copy_pickwT(i)
                    copy_y(i)

                copy_xg(0)
                pair(0, True, False)
                with act.Fori(1, PAIRS - 1) as i:
                    pair(i, False, False)
                pair(PAIRS - 1, False, True)

            def overflow(l):
                act.wait_ge(flag_ready[l], 1)
                flag = act.value_load(crowded_i[0:1, 0:1], min_val=0, max_val=1)
                with act.If(flag > 0):
                    with act.Fori(0, E) as e:
                        for r in range(2):
                            k = e * 12 + 6 * r + 1
                            act.wait_ge(ov_pe[l], k + 1)
                            s_.copy(pick_wT.rearrange("p t q -> p (t q)"), bank[2][:, 0:SEQ]).then_inc(ov_act[l], 1)
                            act.wait_ge(ov_pe[l], k + 2)
                            s_.activation(silu, bank[2][:, :], ACT.Silu).then_inc(ov_silu[l], 1)
                            act.wait_ge(ov_pe[l], k + 4)
                            s_.copy(y_slot[:, 0:512], bank[6][:, :])
                            s_.copy(y_slot[:, 512:1024], bank[7][:, :]).then_inc(ov_act[l], 1)
                with act.Else():
                    act.nop()

            xT_copy(0)
            for g in range(1, 12, 2):
                u = g // 2
                act.wait_ge(proj_ready[0], g + 1)
                hh = u // 3
                if u % 3 == 0:
                    ins = s_.mul(qT[:, 4 * hh + 2:4 * hh + 4, :].rearrange("p m q -> p (m q)"), bank[1][:, :], DH ** -0.5)
                elif u % 3 == 1:
                    ins = s_.copy(kT[:, 4 * hh + 2:4 * hh + 4, :].rearrange("p m q -> p (m q)"), bank[1][:, :])
                else:
                    ins = s_.copy(v_tok[:, 1, hh * 512:(hh + 1) * 512], bank[1][:, :])
                ins.then_inc(proj_act[0], 1)
            softmax_jobs(0, HEADS)
            norm(0, 0)
            route_tokens(0)
            experts(0)
            overflow(0)
            norm(0, 1)
            xT_copy(2)
            for g in range(1, 10, 2):
                c = g // 2
                act.wait_ge(proj_ready[1], g + 1)
                if c < 2:
                    ins = s_.mul(qT[:, 4 * c + 2:4 * c + 4, :].rearrange("p m q -> p (m q)"), bank[1][:, :], DH ** -0.5)
                elif c == 2:
                    ins = copy_cmp_in(nc.scalar.copy, 1, bank[1])
                else:
                    ins = s_.copy(nsa_v[:, c - 3, :, :].rearrange("p k n -> p (k n)"), bank[1][:, :])
                ins.then_inc(proj_act[1], 1)
            act.wait_ge(proj_ready[1], 11)
            s_.activation(gates[:, :, :].rearrange("p t n -> p (t n)"), bank[0][:, 0:96], ACT.Exp, scale=-1.0).then_inc(gate_exp, 1)
            for b in range(2):
                act.wait_ge(chid_psum, b + 1)
                s_.activation(cmp_hid[:, b, :, :], bank[2 + b][:, 0:128].rearrange("p (f n) -> p f n", n=64)[:, :, 0:KV * N_CMP],
                              ACT.Gelu_apprx_tanh).then_inc(chid_ready, 1)
            act.wait_ge(cs_centred, 2)
            cp = cmp_p[:, :, :, 0:N_CMP]
            s_.activation(cp.rearrange("p t h n -> p (t h) n"), cp.rearrange("p t h n -> p (t h) n"), ACT.Exp).then_inc(cs_exp, 1)
            act.wait_ge(cpT_psum, 2)
            s_.copy(cmp_pT[:, 2:4, :].rearrange("p g q -> p (g q)"), bank[5][:, :]).then_inc(cpT_act, 1)
            softmax_jobs(1, 2 * HEADS)
            norm(1, 0)
            route_tokens(1)
            experts(1)
            overflow(1)
            norm(1, 1)


_INS = ['x', 'rel_bias', 'router_w', 'router_b', 'ln_g', 'ln_b', 'moba_w_in', 'moba_w_out', 'nsa_w_in', 'nsa_w_out',
        'nsa_pos_k', 'nsa_pos_v', 'nsa_ck_w1', 'nsa_ck_w2', 'nsa_cv_w1', 'nsa_cv_w2', 'moe_w_gate', 'moe_w_up', 'moe_w_down']


def kernel(**inputs):
    import concourse.bacc as bacc
    from concourse.bass_utils import run_bass_kernel_spmd

    nc = bacc.Bacc("TRN2", target_bir_lowering=False, num_devices=1)
    arrays, args = {}, []
    for name in _INS:
        a = np.ascontiguousarray(inputs[name])
        arrays[f"in_{name}"] = a
        args.append(nc.dram_tensor(f"in_{name}", a.shape, mybir.dt.from_np(a.dtype), kind="ExternalInput").ap())
    tables, place = shape_tables()
    arrays["in_tables"] = tables
    args.append(nc.dram_tensor("in_tables", tables.shape, F32, kind="ExternalInput").ap())
    out = nc.dram_tensor("out", (1, SEQ, D), F32, kind="ExternalOutput").ap()
    build(nc, *args, place, out)
    return run_bass_kernel_spmd(nc, [arrays], core_ids=[0]).results[0]["out"]
```

```python
from contextlib import ExitStack

import numpy as np

import concourse.bass as bass
from concourse import mybir

F32 = mybir.dt.float32
I32 = mybir.dt.int32
ALU = mybir.AluOpType
ACT = mybir.ActivationFunctionType
AX = mybir.AxisListType.X

P = 128
D = 1024
SEQ = 256
NT = SEQ // P
KT = D // P
HEADS, DH = 16, 64
KV = 4
GROUP = HEADS // KV
LAYERS = 2
BUCKETS, MAX_DIST = 32, 128
CMP_LEN, CMP_STRIDE, CMP_HID = 32, 16, 256
N_CMP = (SEQ - CMP_LEN) // CMP_STRIDE + 1
CMP_ROWS = 64
E, EG, NG = 32, 4, 8
FF = 512
FT = FF // P
CAP = 64
PAIRS = E // 2
ALPHA = (2 * LAYERS) ** 0.25
EPS = 1e-5
NEG = -1e30
BIAS_W = 384
SLOT = 4096
NSLOT = 6
SMALL_LOADS = 6 * 16
DVE_COLS = 640
OV_PE = 2 * 6


def t5_buckets(n):
    exact = BUCKETS // 2
    nf = np.maximum(n, 1).astype(np.float32)
    large = exact + (np.log(nf / np.float32(exact)) / np.float32(np.log(MAX_DIST / exact))
                     * (BUCKETS - exact)).astype(np.int32)
    return np.where(n < exact, n, np.minimum(large, BUCKETS - 1))


def shape_tables():
    p = np.arange(P)
    cols = {}
    cols["ident"] = np.eye(P)
    cols["flip"] = np.eye(P)[::-1]
    cols["before"] = (p[:, None] < p[None, :]).astype(float)
    cols["ones"] = np.ones((P, P))
    cols["slot"] = np.tile(np.arange(P) % CAP, (P, 1))
    cols["slot2"] = np.tile(np.arange(P), (P, 1))
    cols["first32"] = np.tile(E - np.arange(E), (P, 1))
    cols["first8"] = np.tile(NG - np.arange(NG), (P, 1))
    q = np.arange(NT)[None, :, None] * P + p[:, None, None]
    seen = np.arange(16)[None, None, :] * CMP_STRIDE + CMP_LEN - 1 <= q
    cols["seen"] = seen.reshape(P, -1)
    cols["unseen"] = np.where(seen, 0.0, NEG).reshape(P, -1)
    dist = SEQ - 1 - np.arange(BIAS_W)
    hot = np.zeros((P, BIAS_W))
    hot[t5_buckets(np.maximum(dist, 0)), np.arange(BIAS_W)] = dist >= 0
    hot[BUCKETS] = dist < 0
    cols["bucket"] = hot
    at, place = 0, {}
    for name, c in cols.items():
        place[name] = (at, at + c.shape[1])
        at += c.shape[1]
    return np.ascontiguousarray(np.concatenate(list(cols.values()), 1), dtype=np.float32), place


def after(eng, sem, value):
    if not isinstance(value, int) or value > 0:
        eng.wait_ge(sem, value)


def build(nc, x_in, rel_bias, router_w, router_b, ln_g, ln_b, moba_w_in, moba_w_out, nsa_w_in, nsa_w_out,
          nsa_pos_k, nsa_pos_v, nsa_ck_w1, nsa_ck_w2, nsa_cv_w1, nsa_cv_w2,
          moe_w_gate, moe_w_up, moe_w_down, tables, place, out):
    ctx = ExitStack()
    with ctx:
        def sb(name, shape, dt=F32):
            return ctx.enter_context(nc.sbuf_tensor(name, shape, dt))

        def sem(name):
            return ctx.enter_context(nc.semaphore(name))

        def sem2(name):
            return [sem(f"{name}_{l}") for l in range(LAYERS)]

        ring = sb("ring", [P, NSLOT, SLOT])
        xs = sb("xs", [P, NT, D])
        acc = sb("acc", [P, NT, D])
        norm_w = sb("norm_w", [P, 2, D])
        bias = sb("bias", [P, HEADS, SEQ])
        xT = sb("xT", [P, KT, SEQ])
        work = sb("work", [P, 4 * 2048])
        tab = sb("tab", [P, place["bucket"][0]])
        probs = sb("probs", [P, 6, 3 * P])
        probsT = sb("probsT", [P, 4, 3 * P])
        rel_w = sb("rel_w", [BUCKETS + 1, HEADS])
        router = sb("router", [P, (KT - 1) * E + P])
        gate_w = sb("gate_w", [P, (KT - 1) * 3 * HEADS + P])
        router_bias = sb("router_bias", [P, E])
        pos_rows = sb("pos_rows", [16, 2, P])
        pos_cols = sb("pos_cols", [P, 2, 16])
        cmp_w2 = sb("cmp_w2", [P, 2, 2, DH])
        gates = sb("gates", [P, NT, 3 * HEADS])
        cmp_hid = sb("cmp_hid", [P, CMP_HID])
        cmp_hidT = sb("cmp_hidT", [P, 2, P])
        cmp_keyT = sb("cmp_keyT", [P, CMP_ROWS])
        cmp_val = sb("cmp_val", [P, KV, DH])
        cmp_max = sb("cmp_max", [P, NT, HEADS])
        cmp_sum = sb("cmp_sum", [P, NT, HEADS])
        job_max = sb("job_max", [P, 3, 2, NT])
        job_sum = sb("job_sum", [P, 3, 2, NT])
        job_scale = sb("job_scale", [P, 3, 2, NT])
        stats = sb("stats", [P, NT, 12])
        moments = sb("moments", [P, NT, 2])
        rstd = sb("rstd", [P, NT])
        one = sb("one", [P, 8, NT])
        slot_of = sb("slot_of", [P, NT, E])
        chosen = sb("chosen", [P, NT, E])
        weight = sb("weight", [P, NT, E])
        crowded = sb("crowded", [P, 1])
        crowded_i = sb("crowded_i", [P, 1], I32)

        bank = [ctx.enter_context(nc.psum_tensor(f"bank{i}", [P, 512], F32)) for i in range(8)]
        dist_dram = nc.dram_tensor("dist_rows", [HEADS, BIAS_W], F32)

        bucket_rows = acc[0:BUCKETS + 1, 0, 0:BIAS_W]
        dist_row = acc[0:HEADS, 1, 0:BIAS_W]

        def table(name, n=P):
            a, b = place[name]
            return tab[0:n, a:b]

        ident, flip = table("ident"), table("flip")

        qT = work[:, 0:2048].rearrange("p (m q) -> p m q", q=SEQ)
        kT = work[:, 2048:4096].rearrange("p (m q) -> p m q", q=SEQ)
        v_tok = work[:, 4096:6144].rearrange("p (k n) -> p k n", k=NT)
        oT = work[:, 6144:8192].rearrange("p (m q) -> p m q", q=SEQ)
        hankel = [acc[:, :, :].rearrange("p t d -> p (t d)").rearrange("p (h k) -> p h k", k=SEQ), oT]
        nsa_kT = work[:, 2048:4096].rearrange("p (b k q) -> p b k q", b=2, k=KV)
        nsa_v = work[:, 4096:5120].rearrange("p (b k n) -> p b k n", b=2, k=NT)
        cmp_p = work[:, 5120:6144].rearrange("p (t h n) -> p t h n", t=NT, n=32)
        cmp_pT = xT[:, 0:4, :]
        cmp_in = acc[:, :, :].rearrange("p t d -> p (t d)").rearrange("p (b l n) -> p b l n", b=2, l=16)
        xgT = work[:, 0:1024].rearrange("p (t s) -> p t s", s=P)
        yT = work[:, 1024:2048].rearrange("p (t s) -> p t s", s=P)
        y_slot = work[:, 2048:3072]
        hid = work[:, 3072:3584]
        silu = work[:, 3584:4096]
        pick = work[:, 4096:4352].rearrange("p (t e s) -> p t e s", t=NT, e=2)
        pick_w = work[:, 4352:4608].rearrange("p (t e s) -> p t e s", t=NT, e=2)
        pick_wT = work[:, 4608:4864].rearrange("p (t q) -> p t q", t=NT)
        hidT = work[:, 5504:6016].rearrange("p (m s) -> p m s", s=P)
        route = work[:, 4864:5376].rearrange("p (k t e) -> p k t e", t=NT, e=E)
        small = work[:, 5376:5504].rearrange("p (k t g) -> p k t g", t=NT, g=NG)

        def cols(w, c):
            return w[:, c * 512:(c + 1) * 512].rearrange("(p t) n -> p t n", t=KT)

        def rows(w, c):
            return w[c * 512:(c + 1) * 512, :].rearrange("(m p) n -> p m n", p=P)

        moba_uses = [cols(moba_w_in[0], c) for c in (0, 2, 4, 1, 3, 5)] + [rows(moba_w_out[0], c) for c in (0, 1)]
        cmp_w1 = [w[0].rearrange("(l p) n -> p l n", p=P) for w in (nsa_ck_w1, nsa_cv_w1)]
        nsa_uses = ([cols(nsa_w_in[0], c) for c in (2, 0, 1)] + cmp_w1 + [cols(nsa_w_in[0], c) for c in (3, 4)]
                    + [rows(nsa_w_out[0], c) for c in (0, 1)])
        first_use = [0, len(moba_uses) + 3 * E]
        first_moe = [len(moba_uses), len(moba_uses) + 3 * E + len(nsa_uses)]
        USES_PER_PAIR = 6

        def slot_no(u):
            return u % NSLOT

        def slot8(u):
            return ring[:, slot_no(u), :].rearrange("p (t n) -> p t n", t=KT)

        def slot4(u):
            return ring[:, slot_no(u), :].rearrange("p (t n) -> p t n", t=4)

        def slot16(u):
            return ring[:, slot_no(u), :].rearrange("p (t n) -> p t n", t=16)

        loaded = [sem(f"loaded{s}") for s in range(NSLOT)]
        x_loaded, tables_loaded, small_loaded = sem("x_loaded"), sem("tables_loaded"), sem("small_loaded")
        norm_loaded = sem("norm_loaded")
        mask_row, rel_loaded = sem("mask_row"), sem("rel_loaded")
        dist_ready, dist_copied, dist_stored, hankel_loaded = (
            sem("dist_ready"), sem("dist_copied"), sem("dist_stored"), sem("hankel_loaded"))
        flipped, bias_copied = sem("flipped"), sem("bias_copied")
        xT_ready, xT_copied = sem("xT_ready"), sem("xT_copied")
        proj_ready, proj_dve, proj_act = sem2("proj_ready"), sem2("proj_dve"), sem2("proj_act")
        scores_ready, scores_read = sem2("scores_ready"), sem2("scores_read")
        max_ready, exp_ready, scale_ready, probs_ready = (
            sem2("max_ready"), sem2("exp_ready"), sem2("scale_ready"), sem2("probs_ready"))
        probsT_ready, probsT_dve, probsT_act = sem2("probsT_ready"), sem2("probsT_dve"), sem2("probsT_act")
        pv_done, o_copied = sem2("pv_done"), sem2("o_copied")
        mix_ready, mix_added = sem2("mix_ready"), sem2("mix_added")
        var_ready, std_ready, norm_scaled = sem("var_ready"), sem("std_ready"), sem("norm_scaled")
        norm_mult, norm_dve, norm_pool = sem("norm_mult"), sem("norm_dve"), sem("norm_pool")
        pads_ready = sem("pads_ready")
        gate_ready, gate_exp, gates_ready = sem("gate_ready"), sem("gate_exp"), sem("gates_ready")
        cpos_ready, cpos_copied = sem("cpos_ready"), sem("cpos_copied")
        cin_copied, cin_ready = sem("cin_copied"), sem("cin_ready")
        chid_psum, chid_ready = sem("chid_psum"), sem("chid_ready")
        chidT_psum, chidT_ready = sem("chidT_psum"), sem("chidT_ready")
        ckv_psum, ckv_ready = sem("ckv_psum"), sem("ckv_ready")
        cs_ready, cs_centred, cs_exp, cp_ready = sem("cs_ready"), sem("cs_centred"), sem("cs_exp"), sem("cp_ready")
        cpT_psum, cpT_dve, cpT_act = sem("cpT_psum"), sem("cpT_dve"), sem("cpT_act")
        logits_ready, logits_shifted, logits_exp = sem2("logits_ready"), sem2("logits_shifted"), sem2("logits_exp")
        chosen_ready, ranks_ready, flag_ready = sem2("chosen_ready"), sem2("ranks_ready"), sem2("flag_ready")
        pick_ready, pickw_ready, pickwT_psum, pickwT_ready = (
            sem2("pick_ready"), sem2("pickw_ready"), sem2("pickwT_psum"), sem2("pickwT_ready"))
        gathered, xg_dve, xg_act = sem2("gathered"), sem2("xg_dve"), sem2("xg_act")
        gate_done, up_done, silu_ready, hid_ready = (
            sem2("gate_done"), sem2("up_done"), sem2("silu_ready"), sem2("hid_ready"))
        hidT_psum, hidT_ready = sem2("hidT_psum"), sem2("hidT_ready")
        down_done, y_dve, y_act = sem2("down_done"), sem2("y_dve"), sem2("y_act")
        spread_ready, acc_added, acc_started = sem2("spread_ready"), sem2("acc_added"), sem2("acc_started")
        dve_chain = sem("dve_chain")
        ov_loaded = [sem2(f"ov_loaded{s}") for s in range(3)]
        ov_pe, ov_dve, ov_act = sem2("ov_pe"), sem2("ov_dve"), sem2("ov_act")
        ov_silu, ov_chain = sem2("ov_silu"), sem2("ov_chain")
        stored = sem("stored")

        freed = {}
        for l, uses in enumerate((moba_uses, nsa_uses)):
            for n in (0, 1):
                freed[first_use[l] + len(uses) - 2 + n] = (mix_ready[l], 4 * (n + 1))
        for n in range(6):
            freed[n] = (proj_ready[0], 2 * n + 2)
        for n, g in ((0, 2), (1, 5), (2, 7), (5, 9), (6, 11)):
            freed[first_use[1] + n] = (proj_ready[1], g)
        for n in (3, 4):
            freed[first_use[1] + n] = (chid_psum, 1)

        PAIR_USES = [("gate", 0), ("gate", 1), ("up", 0), ("up", 1), ("down", 0), ("down", 1)]

        def pair_freed(l, j, i):
            kind, _ = PAIR_USES[j]
            if kind == "down":
                return down_done[l], 2 * i + 2
            return (gate_done if kind == "gate" else up_done)[l], i + 1

        def slot_for(kind, s):
            r = ring[:, s, :]
            return r.rearrange("p (t n) -> p t n", t=4 if kind == "down" else KT)

        def copy_cmp_in(copy, b, ps):
            for hkv in range(KV):
                for o in range(2):
                    src = ps[DH * (hkv % 2):DH * (hkv % 2) + DH, (hkv // 2) * SEQ + o:(hkv // 2) * SEQ + o + 1]
                    src = bass.AP(tensor=src.tensor, offset=src.offset, ap=[list(src.ap[0]), [2, 16], [CMP_STRIDE, N_CMP]])
                    last = copy(cmp_in[DH * o:DH * o + DH, b, :, hkv * N_CMP:(hkv + 1) * N_CMP], src)
            return last

        job_pairs = [[(m, 0) for m in range(HEADS // 2)],
                     [(m, b) for m in range(HEADS // 2) for b in range(2)]]
        beside = [{0: [("proj", 6), ("proj", 7)], 1: [("proj", 8)], 2: [("proj", 9), ("proj", 10)], 3: [("proj", 11)],
                   8: [("out", 0)], 9: [("out", 1), ("out", 2)], 10: [("out", 3)]},
                  {12: [("out", 0)], 13: [("out", 1)], 14: [("out", 2)], 15: [("out", 3)]}]

        def norm_tiles(l, n, tt):
            return NT * (2 * l + n) + tt + 1

        block = ctx.enter_context(nc.Block())

        @block.sync
        def _(sp):
            def load_fixed(l, uses):
                for n, src in enumerate(uses):
                    u = first_use[l] + n
                    if u >= NSLOT:
                        sp.wait_ge(*released(u - NSLOT))
                    dst = ring[:, slot_no(u), :].rearrange("p (t n) -> p t n", t=src.shape[1])
                    sp.dma_start(dst, src).then_inc(loaded[slot_no(u)], 16)

            def released(u):
                if u in freed:
                    return freed[u]
                l = 0 if u < first_use[1] else 1
                i, j = divmod(u - first_moe[l], USES_PER_PAIR)
                return pair_freed(l, j, i)

            def load_pair(l, i, j):
                kind, e = PAIR_USES[j]
                s = slot_no(first_moe[l] + j)
                src = (moe_w_down if kind == "down" else moe_w_gate if kind == "gate" else moe_w_up)[
                    l, bass.ds(2 * i + e, 1), :, :]
                if kind == "down":
                    src = src.rearrange("a (m p) n -> p (a m) n", p=P)
                else:
                    src = src.rearrange("a (p t) n -> p (a t) n", t=KT)
                sp.dma_start(slot_for(kind, s), src).then_inc(loaded[s], 16)

            sp.dma_start(xs[:, :, :], x_in[0].rearrange("(t p) d -> p t d", p=P)).then_inc(x_loaded, 16)
            sp.dma_start(tab[:, :], tables[:, 0:place["bucket"][0]]).then_inc(tables_loaded, 16)
            sp.dma_start(bucket_rows, tables[0:BUCKETS + 1, place["bucket"][0]:place["bucket"][1]]).then_inc(tables_loaded, 16)
            for l, uses in enumerate((moba_uses, nsa_uses)):
                load_fixed(l, uses)
                for j in range(USES_PER_PAIR):
                    sp.wait_ge(*released(first_moe[l] + j - NSLOT))
                    load_pair(l, 0, j)
                with sp.Fori(1, PAIRS) as i:
                    for j in range(USES_PER_PAIR):
                        s, n = pair_freed(l, j, i - 1)
                        sp.wait_ge(s, n)
                        load_pair(l, i, j)
                if True:
                    sp.wait_ge(flag_ready[l], 1)
                    flag = sp.value_load(crowded_i[0:1, 0:1], min_val=0, max_val=1)
                    with sp.If(flag > 0):
                        for j in range(USES_PER_PAIR):
                            sp.wait_ge(*pair_freed(l, j, PAIRS - 1))
                        with sp.Fori(0, E) as e:
                            sp.wait_ge(ov_pe[l], e * OV_PE + 1)
                            for s, (kind, w) in enumerate((("gate", moe_w_gate), ("up", moe_w_up), ("down", moe_w_down))):
                                src = w[l, bass.ds(e, 1), :, :]
                                if kind == "down":
                                    src = src.rearrange("a (m p) n -> p (a m) n", p=P)
                                else:
                                    src = src.rearrange("a (p t) n -> p (a t) n", t=KT)
                                sp.dma_start(slot_for(kind, s), src).then_inc(ov_loaded[s][l], 16)
                        sp.wait_ge(ov_pe[l], E * OV_PE + 1)
                    with sp.Else():
                        sp.nop()
            for tt in range(NT):
                sp.wait_ge(norm_dve, norm_tiles(1, 1, tt))
                sp.wait_ge(norm_pool, norm_tiles(1, 1, tt))
                sp.dma_start(out[0, tt * P:(tt + 1) * P, :], xs[:, tt, :]).then_inc(stored, 16)
            sp.wait_ge(stored, 16 * NT)

        @block.gpsimd
        def _(pool):
            nc.gpsimd.memset(rel_w[BUCKETS:BUCKETS + 1, :], NEG).then_inc(mask_row, 1)
            pool.dma_start(rel_w[0:BUCKETS, :], rel_bias).then_inc(rel_loaded, 16)
            pool.wait_ge(mask_row, 1)
            nc.gpsimd.memset(router[:, KT * E:], 0.0).then_inc(pads_ready, 1)
            nc.gpsimd.memset(gate_w[:, KT * 3 * HEADS:], 0.0).then_inc(pads_ready, 1)
            pool.dma_start(router[:, 0:KT * E].rearrange("p (t n) -> p t n", t=KT),
                           router_w.rearrange("(p t) n -> p t n", t=KT)).then_inc(small_loaded, 16)
            pool.dma_start(router_bias[:, :], bass.AP(tensor=router_b.tensor, offset=0, ap=[[0, P], [1, E]])).then_inc(small_loaded, 16)
            for b, src in enumerate((nsa_pos_k, nsa_pos_v)):
                pool.dma_start(pos_rows[:, b, :], src[0].rearrange("(l o) d -> l (o d)", o=2)).then_inc(small_loaded, 16)
            for b, src in enumerate((nsa_ck_w2, nsa_cv_w2)):
                pool.dma_start(cmp_w2[:, b, :, :], src[0].rearrange("(f p) d -> p f d", p=P)).then_inc(small_loaded, 16)
            pool.wait_ge(dist_copied, 1)
            pool.dma_start(dist_dram.ap(), dist_row).then_inc(dist_stored, 16)
            pool.wait_ge(dist_stored, 16)
            pool.wait_ge(dist_ready, 1)
            for i in range(2):
                src = bass.AP(tensor=dist_dram.ap().tensor, offset=i * 8 * BIAS_W, ap=[[1, P], [BIAS_W, 8], [1, SEQ]])
                pool.dma_start(hankel[i], src).then_inc(hankel_loaded, 16)
            pool.dma_start(gate_w[:, 0:KT * 3 * HEADS].rearrange("p (t n) -> p t n", t=KT),
                           nsa_w_in[0][:, 2560:2608].rearrange("(p t) n -> p t n", t=KT)).then_inc(small_loaded, 16)

            def load_norm(k):
                if k:
                    pool.wait_ge(norm_dve, NT * k)
                    pool.wait_ge(norm_pool, NT * k)
                for w, src in enumerate((ln_g, ln_b)):
                    pool.dma_start(norm_w[:, w, :], bass.AP(tensor=src.tensor, offset=k * D, ap=[[0, P], [1, D]])).then_inc(norm_loaded, 16)

            def scale_probs(l):
                for s in range(len(job_pairs[l])):
                    pool.wait_ge(scale_ready[l], s + 1)
                    for jj in range(2):
                        for tt, (a, b) in enumerate(((0, P), (P, 3 * P))):
                            pr = probs[:, 2 * (s % 3) + jj, a:b]
                            last = nc.gpsimd.tensor_scalar(pr, pr, job_scale[:, s % 3, jj, tt:tt + 1], None, ALU.mult)
                    last.then_inc(probs_ready[l], 1)

            def norm(l, n):
                pool.wait_ge(norm_loaded, 32 * (2 * l + n + 1))
                for tt in range(NT):
                    k = norm_tiles(l, n, tt)
                    pool.wait_ge(norm_scaled, k)
                    nc.gpsimd.tensor_tensor(acc[:, tt, DVE_COLS:], acc[:, tt, DVE_COLS:], norm_w[:, 0, DVE_COLS:], ALU.mult).then_inc(norm_mult, 1)
                    pool.wait_ge(norm_mult, k)
                    nc.gpsimd.tensor_tensor(xs[:, tt, DVE_COLS:], acc[:, tt, DVE_COLS:], norm_w[:, 1, DVE_COLS:], ALU.add).then_inc(norm_pool, 1)

            load_norm(0)
            for l in range(LAYERS):
                if l:
                    nc.gpsimd.memset(cmp_in[:, :, :, KV * N_CMP:], 0.0).then_inc(pads_ready, 1)
                scale_probs(l)
                norm(l, 0)
                pool.wait_ge(norm_dve, norm_tiles(l, 0, NT - 1))
                pool.wait_ge(norm_pool, norm_tiles(l, 0, NT - 1))
                nc.gpsimd.tensor_scalar(acc[:, :, :].rearrange("p t d -> p (t d)"), xs[:, :, :].rearrange("p t d -> p (t d)"),
                                        ALPHA, None, ALU.mult).then_inc(acc_started[l], 1)
                load_norm(2 * l + 1)
                norm(l, 1)
                if l + 1 < LAYERS:
                    load_norm(2 * l + 2)

        @block.tensor
        def _(pe):
            mm, tr = nc.tensor.matmul, nc.tensor.transpose

            def arrived(u):
                pe.wait_ge(loaded[slot_no(u)], 16 * (u // NSLOT + 1))

            def transpose_x(n, tt):
                after(pe, xT_copied, 2 * (NT * n + tt))
                for half in range(2):
                    for t in range(4):
                        last = tr(bank[4 + half][:, t * P:(t + 1) * P], xs[:, tt, 4 * half + t::KT], ident)
                    last.then_inc(xT_ready, 1)

            def xT_here(n, tt):
                pe.wait_ge(xT_copied, 2 * (NT * n + tt + 1))

            def normed(l, n, tt):
                k = norm_tiles(l, n, tt)
                pe.wait_ge(norm_dve, k)
                pe.wait_ge(norm_pool, k)

            def proj_bank_free(l, g):
                after(pe, proj_dve[l] if g % 2 == 0 else proj_act[l], g // 2)

            def project_T(l, g, w, lhs_cols):
                proj_bank_free(l, g)
                for n, pick_cols in enumerate(lhs_cols):
                    for t in range(KT):
                        last = mm(bank[g % 2][:, n * SEQ:(n + 1) * SEQ], pick_cols(w, t), xT[:, t, :],
                                  start=(t == 0), stop=(t == KT - 1))
                return last

            def project_tok(l, g, w, tt, width=512):
                proj_bank_free(l, g)
                for t in range(KT):
                    last = mm(bank[g % 2][:, 0:width], xT[:, t, tt * P:(tt + 1) * P], w[:, t, 0:width],
                              start=(t == 0), stop=(t == KT - 1))
                return last

            def tile_cols(m):
                return lambda w, t: w[:, t, m * P:(m + 1) * P]

            def attention(l, job, compressed):
                n_steps = len(job_pairs[l])
                for s in range(n_steps + 3):
                    if s < n_steps:
                        m, br = job_pairs[l][s]
                        after(pe, scores_read[l], s)
                        both = [job(2 * m + a, br) for a in range(2)]
                        for a in range(2):
                            mm(bank[2 + a][:, 0:P], both[a]["q"][:, 0:P], both[a]["k"][:, 0:P], start=True, stop=True)
                        for a in range(2):
                            last = mm(bank[2 + a][:, P:3 * P], both[a]["q"][:, P:SEQ], both[a]["k"], start=True, stop=True)
                        last.then_inc(scores_ready[l], 1)
                    for kind, k in beside[l].get(s, []):
                        if kind == "proj":
                            moba_group(k)
                        else:
                            out_piece(l, k)
                    if 0 <= s - 2 < n_steps:
                        j = s - 2
                        pe.wait_ge(probs_ready[l], j + 1)
                        after(pe, probsT_dve[l], j)
                        after(pe, probsT_act[l], j)
                        for a in range(2):
                            for b in range(3):
                                last = tr(bank[4 + a][:, b * P:(b + 1) * P], probs[:, 2 * (j % 3) + a, b * P:(b + 1) * P], ident)
                        last.then_inc(probsT_ready[l], 1)
                    if 0 <= s - 3:
                        j = s - 3
                        m, br = job_pairs[l][j]
                        final = j + 1 == n_steps or job_pairs[l][j + 1][0] != m
                        both = [job(2 * m + a, br) for a in range(2)]
                        pe.wait_ge(probsT_dve[l], j + 1)
                        pe.wait_ge(probsT_act[l], j + 1)
                        if br == 0:
                            after(pe, o_copied[l], m - 1)
                        ps = [bank[6 + m % 2][DH * a:DH * a + DH, :] for a in range(2)]
                        pt = [probsT[:, 2 * (j % 2) + a, :] for a in range(2)]
                        for a in range(2):
                            mm(ps[a][:, 0:SEQ], both[a]["v"](0), pt[a][:, 0:SEQ], start=br == 0, stop=False)
                        for a in range(2):
                            last = mm(ps[a][:, P:SEQ], both[a]["v"](1), pt[a][:, SEQ:3 * P], start=False, stop=final and not compressed)
                        if final and compressed:
                            for a in range(2):
                                last = compressed(2 * m + a, ps[a][:, 0:SEQ])
                        last.then_inc(pv_done[l], 1)

            def out_piece(l, k):
                c, tt, n = k // 4, k // 2 % 2, k % 2
                if k % 4 == 0:
                    arrived(first_moe[l] - 2 + c)
                    pe.wait_ge(o_copied[l], 4 * (c + 1))
                after(pe, mix_added[l], k - 1)
                w = slot4(first_moe[l] - 2 + c)
                for t in range(4):
                    last = mm(bank[k % 2][:, :], oT[:, 4 * c + t, tt * P:(tt + 1) * P], w[:, t, n * 512:(n + 1) * 512],
                              start=(t == 0), stop=(t == 3))
                last.then_inc(mix_ready[l], 1)

            def route_tokens(l):
                for tt in range(NT):
                    normed(l, 0, tt)
                    transpose_x(2 * l + 1, tt)
                    if tt == 0:
                        pe.wait_ge(small_loaded, SMALL_LOADS)
                        pe.wait_ge(pads_ready, 2)
                    xT_here(2 * l + 1, tt)
                    for t in range(KT):
                        last = mm(bank[6][:, tt * P:(tt + 1) * P], xT[:, t, tt * P:(tt + 1) * P], router[:, t * E:t * E + P],
                                  start=(t == 0), stop=(t == KT - 1))
                last.then_inc(logits_ready[l], 1)
                pe.wait_ge(chosen_ready[l], 1)
                mm(bank[7][:, 0:E], table("before"), chosen[:, 0, :], start=True, stop=True)
                mm(bank[7][:, E:2 * E], table("ones"), chosen[:, 0, :], start=True, stop=False)
                mm(bank[7][:, E:2 * E], table("before"), chosen[:, 1, :], start=False, stop=True)
                mm(bank[7][:, 2 * E:3 * E], table("ones"), chosen[:, 0, :], start=True, stop=False)
                mm(bank[7][:, 2 * E:3 * E], table("ones"), chosen[:, 1, :], start=False, stop=True).then_inc(ranks_ready[l], 1)

            SPREAD_BANKS = [4, 0, 1, 7]

            def gather(l, i):
                pe.wait_ge(pick_ready[l], i + 1)
                for half in range(2):
                    after(pe, acc_added[l], 4 * (i - 2) + 2 + half)
                    for t in range(4):
                        for tt in range(NT):
                            last = mm(bank[half][:, t * P:(t + 1) * P], xs[:, tt, 4 * half + t::KT],
                                      pick[:, tt, :, :].rearrange("p e s -> p (e s)"), start=(tt == 0), stop=(tt == 1))
                    last.then_inc(gathered[l], 1)

            def gate_up(l, i, use):
                pe.wait_ge(xg_dve[l], i + 1)
                pe.wait_ge(xg_act[l], i + 1)
                for k, done, read in ((0, gate_done, silu_ready), (1, up_done, hid_ready)):
                    after(pe, read[l], i)
                    for e in range(2):
                        use(2 * k + e)
                    for t in range(KT):
                        for e in range(2):
                            last = mm(bank[2 + k][e * CAP:(e + 1) * CAP, :], xgT[:, t, e * CAP:(e + 1) * CAP],
                                      slot8(first_moe[l] + 2 * k + e)[:, t, :], start=(t == 0), stop=(t == KT - 1))
                    last.then_inc(done[l], 1)

            def transpose_hidden(l, i):
                pe.wait_ge(hid_ready[l], i + 1)
                after(pe, acc_added[l], 4 * (i - 1) + 1)
                for m in range(FT):
                    last = tr(bank[4][:, m * P:(m + 1) * P], hid[:, m * P:(m + 1) * P], ident)
                last.then_inc(hidT_psum[l], 1)

            def weights_by_slot(l, i):
                pe.wait_ge(pickw_ready[l], i + 1)
                after(pe, acc_added[l], 4 * i)
                for tt in range(NT):
                    last = tr(bank[7][:, tt * P:(tt + 1) * P], pick_w[:, tt, :, :].rearrange("p e s -> p (e s)"), ident)
                last.then_inc(pickwT_psum[l], 1)

            def down(l, i, use):
                pe.wait_ge(hidT_ready[l], i + 1)
                for e in range(2):
                    use(4 + e)
                for n in range(2):
                    for m in range(FT):
                        for e in range(2):
                            last = mm(bank[5 + n][e * CAP:(e + 1) * CAP, :], hidT[:, m, e * CAP:(e + 1) * CAP],
                                      slot4(first_moe[l] + 4 + e)[:, m, n * 512:(n + 1) * 512], start=(m == 0), stop=(m == FT - 1))
                    last.then_inc(down_done[l], 1)

            def spread(l, i):
                pe.wait_ge(y_dve[l], i + 1)
                pe.wait_ge(y_act[l], i + 1)
                pe.wait_ge(pickwT_ready[l], i + 1)
                for k, b in enumerate(SPREAD_BANKS):
                    tt, n = divmod(k, 2)
                    mm(bank[b][:, :], pick_wT[:, tt, :], y_slot[:, n * 512:(n + 1) * 512], start=True, stop=True).then_inc(spread_ready[l], 1)

            def experts(l):
                def pair(i, first, last):
                    def use(j):
                        u = first_moe[l] + j
                        pe.wait_ge(loaded[slot_no(u)], 16 * (u // NSLOT + 1) + 16 * i)
                    gate_up(l, i, use)
                    if not first:
                        spread(l, i - 1)
                    transpose_hidden(l, i)
                    if not last:
                        gather(l, i + 1)
                    weights_by_slot(l, i)
                    down(l, i, use)

                gather(l, 0)
                pair(0, True, False)
                with pe.Fori(1, PAIRS - 1) as i:
                    pair(i, False, False)
                pair(PAIRS - 1, False, True)
                spread(l, PAIRS - 1)

            def overflow(l):
                pe.wait_ge(flag_ready[l], 1)
                flag = pe.value_load(crowded_i[0:1, 0:1], min_val=0, max_val=1)
                with pe.If(flag > 0):
                    pe.wait_ge(acc_added[l], 4 * PAIRS)
                    tr(bank[6][:, 0:P], ident, ident).then_inc(ov_pe[l], 1)
                    with pe.Fori(0, E) as e:
                        for s in range(3):
                            pe.wait_ge(ov_loaded[s][l], 16 * e + 16)
                        for r in range(2):
                            n = e * 12 + 6 * r
                            m = e * 4 + 2 * r
                            pe.wait_ge(ov_dve[l], n + 2)
                            for half in range(2):
                                for t in range(4):
                                    for tt in range(NT):
                                        mm(bank[half][:, t * P:(t + 1) * P], xs[:, tt, 4 * half + t::KT],
                                           pick[:, tt, :, :].rearrange("p e s -> p (e s)"), start=(tt == 0), stop=(tt == 1))
                            for tt in range(NT):
                                last = tr(bank[2][:, tt * P:(tt + 1) * P], pick_w[:, tt, :, :].rearrange("p e s -> p (e s)"), ident)
                            last.then_inc(ov_pe[l], 1)
                            pe.wait_ge(ov_dve[l], n + 3)
                            pe.wait_ge(ov_act[l], m + 1)
                            for k in range(2):
                                w = ring[:, k, :].rearrange("p (t n) -> p t n", t=KT)
                                for mt in range(FT):
                                    for t in range(KT):
                                        last = mm(bank[2 + k][:, mt * P:(mt + 1) * P], w[:, t, mt * P:(mt + 1) * P], xgT[:, t, :],
                                                  start=(t == 0), stop=(t == KT - 1))
                            last.then_inc(ov_pe[l], 1)
                            pe.wait_ge(ov_dve[l], n + 4)
                            w = ring[:, 2, :].rearrange("p (t n) -> p t n", t=4)
                            hid_all = hid.rearrange("p (m s) -> p m s", s=P)
                            for c in range(KT):
                                for mt in range(FT):
                                    last = mm(bank[4 + c // 4][:, (c % 4) * P:(c % 4 + 1) * P], w[:, mt, c * P:(c + 1) * P],
                                              hid_all[:, mt, :], start=(mt == 0), stop=(mt == FT - 1))
                            last.then_inc(ov_pe[l], 1)
                            pe.wait_ge(ov_dve[l], n + 5)
                            for c in range(KT):
                                last = tr(bank[6 + c // 4][:, (c % 4) * P:(c % 4 + 1) * P], yT[:, c, :], ident)
                            last.then_inc(ov_pe[l], 1)
                            pe.wait_ge(ov_act[l], m + 2)
                            for tt in range(NT):
                                for c in range(2):
                                    last = mm(bank[6 * (1 - tt) + c][:, :], pick_wT[:, tt, :], y_slot[:, c * 512:(c + 1) * 512],
                                              start=True, stop=True)
                            last.then_inc(ov_pe[l], 1)
                            pe.wait_ge(ov_dve[l], n + 6)
                            tr(bank[6][:, 0:P], ident, ident).then_inc(ov_pe[l], 1)
                with pe.Else():
                    pe.nop()

            pe.wait_ge(tables_loaded, 32)
            pe.wait_ge(rel_loaded, 16)
            pe.wait_ge(mask_row, 1)
            mm(bank[6][0:HEADS, 0:BIAS_W], rel_w[:, :], bucket_rows, start=True, stop=True).then_inc(dist_ready, 1)
            for tt in range(NT):
                pe.wait_ge(x_loaded, 16)
                transpose_x(0, tt)
            xT_here(0, NT - 1)

            def moba_group(g):
                u, part = divmod(g, 2)
                if part == 0:
                    arrived(u)
                if u % 3 < 2:
                    last = project_T(0, g, slot8(u), [tile_cols(2 * part), tile_cols(2 * part + 1)])
                else:
                    last = project_tok(0, g, slot8(u), part)
                last.then_inc(proj_ready[0], 1)

            for g in range(6):
                moba_group(g)
            pe.wait_ge(hankel_loaded, 32)
            for j in range(HEADS // 2):
                after(pe, bias_copied, j - 1)
                mm(bank[6 + j % 2][:, :], flip, hankel[j // 4][:, 2 * (j % 4):2 * (j % 4) + 2, :].rearrange("p h k -> p (h k)"),
                   start=True, stop=True).then_inc(flipped, 1)

            def moba_job(h, br):
                if h == 0:
                    pe.wait_ge(proj_dve[0], 3)
                    pe.wait_ge(proj_act[0], 3)
                    pe.wait_ge(bias_copied, HEADS // 2)
                if h == 8:
                    pe.wait_ge(proj_dve[0], 6)
                    pe.wait_ge(proj_act[0], 6)
                half = slice(DH * (h % 2), DH * (h % 2) + DH)
                return dict(q=qT[half, h // 2, :], k=kT[half, h // 2, :], v=lambda kt: v_tok[:, kt, h * DH:(h + 1) * DH])
            attention(0, moba_job, None)
            for k in range(4, 8):
                out_piece(0, k)
            route_tokens(0)
            experts(0)
            overflow(0)

            for tt in range(NT):
                normed(0, 1, tt)
                transpose_x(2, tt)
            xT_here(2, NT - 1)
            u0 = first_use[1]

            def nsa_group(g):
                if g == 2:
                    proj_bank_free(1, g)
                    for tt in range(NT):
                        for t in range(KT):
                            last = mm(bank[0][:, tt * P:(tt + 1) * P], xT[:, t, tt * P:(tt + 1) * P],
                                      gate_w[:, t * 3 * HEADS:t * 3 * HEADS + P], start=(t == 0), stop=(t == KT - 1))
                    last.then_inc(proj_ready[1], 1)
                    return
                k = g if g < 2 else g - 1
                part = k % 2
                use = u0 + {0: 0, 1: 1, 2: 2, 3: 5, 4: 6}[k // 2]
                if part == 0:
                    arrived(use)
                w = slot8(use)
                if g < 7:
                    last = project_T(1, g, w, [tile_cols(2 * part), tile_cols(2 * part + 1)])
                elif part == 0:
                    last = project_T(1, g, w, [tile_cols(0), tile_cols(1)])
                else:
                    proj_bank_free(1, g)
                    for tt in range(NT):
                        for t in range(KT):
                            last = mm(bank[g % 2][:, tt * 256:(tt + 1) * 256], xT[:, t, tt * P:(tt + 1) * P], w[:, t, 256:512],
                                      start=(t == 0), stop=(t == KT - 1))
                last.then_inc(proj_ready[1], 1)

            for g in range(3):
                nsa_group(g)
            for b in range(2):
                last = tr(bank[6][:, b * 16:(b + 1) * 16], pos_rows[:, b, :], ident[0:16, 0:16])
            last.then_inc(cpos_ready, 1)
            for g in (3, 4):
                nsa_group(g)
            for b in range(2):
                arrived(u0 + 3 + b)
            pe.wait_ge(cin_ready, 1)
            pe.wait_ge(pads_ready, 3)
            for lp in range(16):
                for b in range(2):
                    last = mm(bank[2][CMP_ROWS * b:CMP_ROWS * (b + 1), 0:CMP_HID], cmp_in[:, b, lp, :], slot16(u0 + 3 + b)[:, lp, :],
                              start=(lp == 0), stop=(lp == 15))
            last.then_inc(chid_psum, 1)
            nsa_group(5)
            pe.wait_ge(chid_ready, 1)
            for f in range(2):
                last = tr(bank[3][:, f * P:(f + 1) * P], cmp_hid[:, f * P:(f + 1) * P], ident)
            last.then_inc(chidT_psum, 1)
            nsa_group(6)
            pe.wait_ge(chidT_ready, 1)
            for f in range(2):
                for hp in (0, DH):
                    mm(bank[4][hp:hp + DH, 0:P], cmp_w2[:, 0, f, :], cmp_hidT[:, f, :], start=(f == 0), stop=(f == 1))
            for hkv in range(KV):
                at = CMP_ROWS + hkv * N_CMP
                for f in range(2):
                    for g in range(GROUP):
                        last = mm(bank[5][32 * g:32 * g + N_CMP, hkv * DH:(hkv + 1) * DH],
                                  cmp_hidT[:, f, at:at + N_CMP], cmp_w2[:, 1, f, :], start=(f == 0), stop=(f == 1))
            last.then_inc(ckv_psum, 1)
            nsa_group(7)
            pe.wait_ge(ckv_ready, 1 + GROUP)
            pe.wait_ge(proj_dve[1], 4)
            pe.wait_ge(proj_act[1], 3)
            for tt in range(NT):
                for h in range(HEADS):
                    half = slice(DH * (h % 2), DH * (h % 2) + DH)
                    c = (tt * HEADS // 2 + h // 2) * 16
                    last = mm(bank[2 + h % 2][:, c:c + N_CMP],
                              qT[half, h // 2, tt * P:(tt + 1) * P], cmp_keyT[half, (h // GROUP) * N_CMP:(h // GROUP + 1) * N_CMP],
                              start=True, stop=True)
            last.then_inc(cs_ready, 1)
            for g in (8, 9, 10):
                nsa_group(g)
            pe.wait_ge(cp_ready, 1)
            for b in range(2):
                for tt in range(NT):
                    for g in (2 * b, 2 * b + 1):
                        last = tr(bank[4 + b][:, (g % 2) * SEQ + tt * P:(g % 2) * SEQ + (tt + 1) * P],
                                  cmp_p[:, tt, 4 * g:4 * g + 4, :].rearrange("p h n -> p (h n)"), ident)
                last.then_inc(cpT_psum, 1)
            pe.wait_ge(cpT_dve, 1)
            pe.wait_ge(cpT_act, 1)
            pe.wait_ge(proj_dve[1], 6)
            pe.wait_ge(proj_act[1], 5)

            def nsa_job(h, b):
                hkv = h // GROUP
                half = slice(DH * (h % 2), DH * (h % 2) + DH)
                return dict(q=qT[half, h // 2, :], k=nsa_kT[half, b, 2 * (hkv % 2) + hkv // 2, :],
                            v=lambda kt: nsa_v[:, b, kt, hkv * DH:(hkv + 1) * DH])

            def compressed(h, ps):
                hkv, g = divmod(h, GROUP)
                at = slice(32 * g, 32 * g + N_CMP)
                return mm(ps, cmp_val[at, hkv, :], cmp_pT[at, hkv, :], start=False, stop=True)
            attention(1, nsa_job, compressed)
            for k in range(4, 8):
                out_piece(1, k)
            route_tokens(1)
            experts(1)
            overflow(1)

        @block.vector
        def _(dve):
            v = nc.vector
            links = [0]

            def link(ins):
                links[0] += 1
                ins.then_inc(dve_chain, 1)
                dve.wait_ge(dve_chain, links[0])

            def softmax_steps(l, scale):
                n_steps = len(job_pairs[l])
                for s in range(n_steps + 4):
                    if s < n_steps:
                        m, _ = job_pairs[l][s]
                        dve.wait_ge(scores_ready[l], s + 1)
                        after(dve, probsT_ready[l], s - 2)
                        for a in range(2):
                            for tt, (x, y) in enumerate(((0, P), (P, 3 * P))):
                                last = v.tensor_tensor_reduce(
                                    out=probs[:, 2 * (s % 3) + a, x:y], in0=bank[2 + a][:, x:y], in1=bias[:, 2 * m + a, P - tt * P:SEQ],
                                    scale=1.0, scalar=-3e38, op0=ALU.add, op1=ALU.max, accum_out=job_max[:, s % 3, a, tt:tt + 1])
                        last.then_inc(scores_read[l], 1)
                        dve.wait_ge(scores_read[l], s + 1)
                        v.tensor_scalar(job_max[:, s % 3, :, :], job_max[:, s % 3, :, :], -1.0, None, ALU.mult).then_inc(max_ready[l], 1)
                    if s >= 4 and (s - 3 == n_steps or job_pairs[l][s - 3][0] != job_pairs[l][s - 4][0]):
                        m = job_pairs[l][s - 4][0]
                        dve.wait_ge(pv_done[l], s - 3)
                        v.tensor_copy(oT[:, m, :], bank[6 + m % 2][:, 0:SEQ]).then_inc(o_copied[l], 1)
                    if 1 <= s <= n_steps:
                        j = s - 1
                        dve.wait_ge(exp_ready[l], j + 1)
                        ins = v.reciprocal(job_scale[:, j % 3, :, :], job_sum[:, j % 3, :, :])
                        if scale:
                            link(ins)
                            ins = v.tensor_tensor(job_scale[:, j % 3, :, :], job_scale[:, j % 3, :, :], scale(*job_pairs[l][j]), ALU.mult)
                        ins.then_inc(scale_ready[l], 1)
                    beside_step(l, s)
                    if 2 <= s < n_steps + 2:
                        j = s - 2
                        dve.wait_ge(probsT_ready[l], j + 1)
                        after(dve, pv_done[l], j - 1)
                        v.tensor_copy(probsT[:, 2 * (j % 2), :], bank[4][:, 0:3 * P]).then_inc(probsT_dve[l], 1)

            def beside_step(l, s):
                for kind, k in beside[l].get(s, []):
                    if kind == "out":
                        add_piece(l, k)
                    elif k % 2 == 0:
                        moba_copy(k)

            def add_piece(l, k):
                c, tt, n = k // 4, k // 2 % 2, k % 2
                a = acc[:, tt, n * 512:(n + 1) * 512]
                dve.wait_ge(mix_ready[l], k + 1)
                if c == 0:
                    v.scalar_tensor_tensor(a, xs[:, tt, n * 512:(n + 1) * 512], ALPHA, bank[k % 2][:, :], ALU.mult, ALU.add).then_inc(mix_added[l], 1)
                else:
                    dve.wait_ge(mix_added[l], k - 3)
                    v.tensor_tensor(a, a, bank[k % 2][:, :], ALU.add).then_inc(mix_added[l], 1)

            def count_half(tt, n):
                return v.bn_stats(stats[:, tt, 6 * n:6 * n + 6], acc[:, tt, n * 512:(n + 1) * 512])

            def norm_tile(l, n, tt):
                k = norm_tiles(l, n, tt)
                link(v.bn_aggr(moments[:, tt, :], stats[:, tt, :]))
                v.tensor_scalar(rstd[:, tt:tt + 1], moments[:, tt, 1:2], EPS, None, ALU.add).then_inc(var_ready, 1)
                dve.wait_ge(std_ready, k)
                link(v.reciprocal(rstd[:, tt:tt + 1], rstd[:, tt:tt + 1]))
                v.tensor_scalar(acc[:, tt, :], acc[:, tt, :], moments[:, tt, 0:1], rstd[:, tt:tt + 1], ALU.subtract, ALU.mult).then_inc(norm_scaled, 1)
                dve.wait_ge(norm_scaled, k)
                dve.wait_ge(norm_loaded, 32 * (2 * l + n + 1))
                link(v.tensor_tensor(acc[:, tt, 0:DVE_COLS], acc[:, tt, 0:DVE_COLS], norm_w[:, 0, 0:DVE_COLS], ALU.mult))
                v.tensor_tensor(xs[:, tt, 0:DVE_COLS], acc[:, tt, 0:DVE_COLS], norm_w[:, 1, 0:DVE_COLS], ALU.add).then_inc(norm_dve, 1)

            def attention_norm(l):
                for tt in range(NT):
                    for n in range(2):
                        add_piece(l, 4 + 2 * tt + n)
                        dve.wait_ge(mix_added[l], 4 + 2 * tt + n + 1)
                        last = count_half(tt, n)
                    link(last)
                    norm_tile(l, 0, tt)

            def route_tokens(l):
                def wide(x):
                    return x.unsqueeze(2).to_broadcast([P, NT, E])

                def flat_table(name, n):
                    return table(name).unsqueeze(1).to_broadcast([P, NT, n])

                pr = route[:, 0, :, :]
                dve.wait_ge(logits_ready[l], 1)
                link(v.tensor_tensor(pr, bank[6][:, 0:NT * P].rearrange("p (t e) -> p t e", e=P)[:, :, 0:E],
                                     router_bias[:, :].unsqueeze(1).to_broadcast([P, NT, E]), ALU.add))
                link(v.tensor_reduce(one[:, 0, :], pr, AX, ALU.max))
                v.tensor_tensor(pr, pr, wide(one[:, 0, :]), ALU.subtract).then_inc(logits_shifted[l], 1)
                dve.wait_ge(logits_exp[l], 1)
                link(v.tensor_reduce(one[:, 1, :], pr, AX, ALU.add))
                link(v.reciprocal(one[:, 2, :], one[:, 1, :]))
                link(v.tensor_tensor(pr, pr, wide(one[:, 2, :]), ALU.mult))
                g4 = pr.rearrange("p t (g e) -> p t g e", e=EG)
                pairs = [(small[:, 0, :, :], small[:, 1, :, :], 0), (small[:, 2, :, :], small[:, 3, :, :], 2)]
                for hi, lo, a in pairs:
                    v.tensor_tensor(hi, g4[:, :, :, a], g4[:, :, :, a + 1], ALU.max)
                    link(v.tensor_tensor(lo, g4[:, :, :, a], g4[:, :, :, a + 1], ALU.min))
                v.tensor_tensor(small[:, 4, :, :], small[:, 0, :, :], small[:, 2, :, :], ALU.max)
                v.tensor_tensor(small[:, 5, :, :], small[:, 0, :, :], small[:, 2, :, :], ALU.min)
                link(v.tensor_tensor(small[:, 6, :, :], small[:, 1, :, :], small[:, 3, :, :], ALU.max))
                link(v.tensor_tensor(small[:, 5, :, :], small[:, 5, :, :], small[:, 6, :, :], ALU.max))
                link(v.tensor_tensor(small[:, 7, :, :], small[:, 4, :, :], small[:, 5, :, :], ALU.add))
                def wide8(x):
                    return x.unsqueeze(2).to_broadcast([P, NT, NG])
                link(v.tensor_reduce(one[:, 3, :], small[:, 7, :, :], AX, ALU.max))
                link(v.tensor_tensor(small[:, 0, :, :], small[:, 7, :, :], wide8(one[:, 3, :]), ALU.is_equal))
                link(v.tensor_tensor(small[:, 0, :, :], small[:, 0, :, :], flat_table("first8", NG), ALU.mult))
                link(v.tensor_reduce(one[:, 3, :], small[:, 0, :, :], AX, ALU.max))
                link(v.tensor_tensor(small[:, 1, :, :], small[:, 0, :, :], wide8(one[:, 3, :]), ALU.is_equal))
                link(v.tensor_scalar(small[:, 2, :, :], small[:, 1, :, :], 4.0, -4.0, ALU.mult, ALU.add))
                cand = route[:, 1, :, :]
                link(v.tensor_tensor(cand.rearrange("p t (g e) -> p t g e", e=EG), g4,
                                     small[:, 2, :, :].unsqueeze(3).to_broadcast([P, NT, NG, EG]), ALU.add))
                hot = [route[:, 3, :, :], route[:, 4, :, :]]
                for k in range(2):
                    link(v.tensor_reduce(one[:, 4 + k, :], cand, AX, ALU.max))
                    link(v.tensor_tensor(route[:, 2, :, :], cand, wide(one[:, 4 + k, :]), ALU.is_equal))
                    link(v.tensor_tensor(route[:, 2, :, :], route[:, 2, :, :], flat_table("first32", E), ALU.mult))
                    link(v.tensor_reduce(one[:, 3, :], route[:, 2, :, :], AX, ALU.max))
                    link(v.tensor_tensor(hot[k], route[:, 2, :, :], wide(one[:, 3, :]), ALU.is_equal))
                    if k == 0:
                        link(v.scalar_tensor_tensor(cand, hot[0], -16.0, cand, ALU.mult, ALU.add))
                v.tensor_tensor(chosen[:, :, :], hot[0], hot[1], ALU.add).then_inc(chosen_ready[l], 1)
                link(v.tensor_tensor(one[:, 6, :], one[:, 4, :], one[:, 5, :], ALU.add))
                link(v.reciprocal(one[:, 7, :], one[:, 6, :]))
                for k in range(2):
                    link(v.tensor_tensor(one[:, 4 + k, :], one[:, 4 + k, :], one[:, 7, :], ALU.mult))
                    link(v.tensor_tensor(hot[k], hot[k], wide(one[:, 4 + k, :]), ALU.mult))
                link(v.tensor_tensor(weight[:, :, :], hot[0], hot[1], ALU.add))
                dve.wait_ge(ranks_ready[l], 1)
                ranks = bank[7][:, 0:NT * E].rearrange("p (t e) -> p t e", e=E)
                link(v.scalar_tensor_tensor(route[:, 5, :, :], ranks, 1.0, chosen[:, :, :], ALU.add, ALU.mult))
                link(v.tensor_scalar(slot_of[:, :, :], route[:, 5, :, :], -1.0, None, ALU.add))
                link(v.tensor_reduce(crowded[:, :], bank[7][:, NT * E:(NT + 1) * E], AX, ALU.max))
                link(v.tensor_scalar(crowded[:, :], crowded[:, :], float(CAP), None, ALU.is_gt))
                v.tensor_copy(crowded_i[:, :], crowded[:, :]).then_inc(flag_ready[l], 1)

            def choice(l, i):
                v.tensor_tensor(pick, table("slot").rearrange("p (e s) -> p e s", e=2).unsqueeze(1).to_broadcast([P, NT, 2, CAP]),
                                slot_of[:, :, bass.ds(2 * i, 2)].unsqueeze(3).to_broadcast([P, NT, 2, CAP]), ALU.is_equal).then_inc(pick_ready[l], 1)

            def experts(l):
                def hidden(i):
                    dve.wait_ge(up_done[l], i + 1)
                    dve.wait_ge(silu_ready[l], i + 1)
                    v.tensor_tensor(hid, silu, bank[3][:, :], ALU.mult).then_inc(hid_ready[l], 1)

                def add(i):
                    after(dve, acc_added[l], 4 * i)
                    for k, b in enumerate((4, 0, 1, 7)):
                        tt, n = divmod(k, 2)
                        dve.wait_ge(spread_ready[l], 4 * i + k + 1)
                        c = acc[:, tt, n * 512:(n + 1) * 512]
                        v.tensor_tensor(c, c, bank[b][:, :], ALU.add).then_inc(acc_added[l], 1)

                def copy_xg(i):
                    dve.wait_ge(gathered[l], 2 * i + 1)
                    v.tensor_copy(xgT[:, 0:4, :].rearrange("p t s -> p (t s)"), bank[0][:, :]).then_inc(xg_dve[l], 1)

                def copy_y(i):
                    dve.wait_ge(down_done[l], 2 * i + 1)
                    v.tensor_copy(y_slot[:, 0:512], bank[5][:, :]).then_inc(y_dve[l], 1)

                def pair(i, first, last):
                    if not first:
                        dve.wait_ge(pickwT_psum[l], i)
                    dve.wait_ge(pick_ready[l], i + 1)
                    v.tensor_tensor(pick_w, pick, weight[:, :, bass.ds(2 * i, 2)].unsqueeze(3).to_broadcast([P, NT, 2, CAP]),
                                    ALU.mult).then_inc(pickw_ready[l], 1)
                    if not last:
                        dve.wait_ge(pickw_ready[l], i + 1)
                        dve.wait_ge(gathered[l], 2 * i + 2)
                        choice(l, i + 1)
                    hidden(i)
                    if not first:
                        add(i - 1)
                    if not last:
                        copy_xg(i + 1)
                    copy_y(i)

                dve.wait_ge(flag_ready[l], 1)
                dve.wait_ge(acc_started[l], 1)
                choice(l, 0)
                copy_xg(0)
                pair(0, True, False)
                with dve.Fori(1, PAIRS - 1) as i:
                    pair(i, False, False)
                pair(PAIRS - 1, False, True)
                add(PAIRS - 1)
                dve.wait_ge(acc_added[l], 4 * PAIRS)

            def overflow(l):
                dve.wait_ge(flag_ready[l], 1)
                flag = dve.value_load(crowded_i[0:1, 0:1], min_val=0, max_val=1)
                flat = lambda x: x.rearrange("p t e s -> p t (e s)")
                with dve.If(flag > 0):
                    dve.wait_ge(ov_pe[l], 1)
                    with dve.Fori(0, E) as e:
                        for r in range(2):
                            n = e * 12 + 6 * r
                            k = e * 12 + 6 * r + 1
                            if r == 0:
                                dve.wait_ge(ov_pe[l], k)
                            v.tensor_scalar(route[:, 6, :, :], slot_of[:, :, :], -float(CAP + P * r), None, ALU.add).then_inc(ov_dve[l], 1)
                            dve.wait_ge(ov_dve[l], n + 1)
                            v.tensor_tensor(flat(pick), table("slot2").unsqueeze(1).to_broadcast([P, NT, P]),
                                            route[:, 6, :, bass.ds(e, 1)].to_broadcast([P, NT, P]), ALU.is_equal).then_inc(ov_chain[l], 1)
                            dve.wait_ge(ov_chain[l], e * 2 + r + 1)
                            v.tensor_tensor(flat(pick_w), flat(pick), weight[:, :, bass.ds(e, 1)].to_broadcast([P, NT, P]),
                                            ALU.mult).then_inc(ov_dve[l], 1)
                            dve.wait_ge(ov_pe[l], k + 1)
                            v.tensor_copy(xgT[:, 0:4, :].rearrange("p t s -> p (t s)"), bank[0][:, :])
                            v.tensor_copy(xgT[:, 4:8, :].rearrange("p t s -> p (t s)"), bank[1][:, :]).then_inc(ov_dve[l], 1)
                            dve.wait_ge(ov_silu[l], e * 2 + r + 1)
                            v.tensor_tensor(hid, silu, bank[3][:, :], ALU.mult).then_inc(ov_dve[l], 1)
                            dve.wait_ge(ov_pe[l], k + 3)
                            v.tensor_copy(yT[:, 0:4, :].rearrange("p t s -> p (t s)"), bank[4][:, :])
                            v.tensor_copy(yT[:, 4:8, :].rearrange("p t s -> p (t s)"), bank[5][:, :]).then_inc(ov_dve[l], 1)
                            dve.wait_ge(ov_pe[l], k + 5)
                            for tt in range(NT):
                                for c in range(2):
                                    a = acc[:, tt, c * 512:(c + 1) * 512]
                                    last = v.tensor_tensor(a, a, bank[6 * (1 - tt) + c][:, :], ALU.add)
                            last.then_inc(ov_dve[l], 1)
                            dve.wait_ge(ov_dve[l], n + 6)
                with dve.Else():
                    dve.nop()

            def expert_norm(l):
                for tt in range(NT):
                    for n in range(2):
                        last = count_half(tt, n)
                link(last)
                for tt in range(NT):
                    norm_tile(l, 1, tt)

            dve.wait_ge(dist_ready, 1)
            v.tensor_copy(dist_row, bank[6][0:HEADS, 0:BIAS_W]).then_inc(dist_copied, 1)

            def moba_copy(g):
                u = g // 2
                hh = u // 3
                dve.wait_ge(proj_ready[0], g + 1)
                if u % 3 == 0:
                    ins = v.tensor_scalar(qT[:, 4 * hh:4 * hh + 2, :].rearrange("p m q -> p (m q)"), bank[0][:, :], DH ** -0.5, None, ALU.mult)
                elif u % 3 == 1:
                    ins = v.tensor_copy(kT[:, 4 * hh:4 * hh + 2, :].rearrange("p m q -> p (m q)"), bank[0][:, :])
                else:
                    ins = v.tensor_copy(v_tok[:, 0, hh * 512:(hh + 1) * 512], bank[0][:, :])
                ins.then_inc(proj_dve[0], 1)

            for g in (0, 2, 4):
                moba_copy(g)
            for j in range(HEADS // 2):
                dve.wait_ge(flipped, j + 1)
                v.tensor_copy(bias[:, 2 * j:2 * j + 2, :].rearrange("p h k -> p (h k)"), bank[6 + j % 2][:, :]).then_inc(bias_copied, 1)
            dve.wait_ge(bias_copied, HEADS // 2)
            softmax_steps(0, None)
            attention_norm(0)
            route_tokens(0)
            experts(0)
            overflow(0)
            expert_norm(0)

            def nsa_copy(g):
                dve.wait_ge(proj_ready[1], g + 1)
                if g == 0:
                    ins = copy_cmp_in(v.tensor_copy, 0, bank[0])
                elif g < 7:
                    c = g // 2 - 2
                    ins = v.tensor_scalar(qT[:, 4 * c + 2:4 * c + 4, :].rearrange("p m q -> p (m q)"), bank[0][:, :], DH ** -0.5, None, ALU.mult)
                else:
                    ins = v.tensor_copy(nsa_v[:, (g - 8) // 2, :, :].rearrange("p k n -> p (k n)"), bank[0][:, :])
                ins.then_inc(proj_dve[1], 1)

            nsa_copy(0)
            dve.wait_ge(gate_exp, 1)
            link(v.tensor_scalar(gates[:, :, :], gates[:, :, :], 1.0, None, ALU.add))
            v.reciprocal(gates[:, :, :], gates[:, :, :]).then_inc(proj_dve[1], 1)
            dve.wait_ge(cpos_ready, 1)
            link(v.tensor_copy(pos_cols[:, :, :].rearrange("p b l -> p (b l)"), bank[6][:, 0:32]))
            dve.wait_ge(proj_dve[1], 2)
            dve.wait_ge(proj_act[1], 1)
            cin = cmp_in[:, :, :, 0:KV * N_CMP]
            for b in range(2):
                last = v.tensor_tensor(cin[:, b, :, :], cin[:, b, :, :], pos_cols[:, b, :].unsqueeze(2).to_broadcast([P, 16, KV * N_CMP]), ALU.add)
            last.then_inc(cin_ready, 1)
            nsa_copy(4)
            nsa_copy(6)
            dve.wait_ge(ckv_psum, 1)
            v.tensor_copy(cmp_keyT[:, :], bank[4][:, 0:CMP_ROWS]).then_inc(ckv_ready, 1)
            for g in range(GROUP):
                at = slice(32 * g, 32 * g + N_CMP)
                v.tensor_copy(cmp_val[at, :, :].rearrange("p h d -> p (h d)"), bank[5][at, 0:KV * DH]).then_inc(ckv_ready, 1)
            v.memset(cmp_p, 0.0).then_inc(cs_centred, 1)
            dve.wait_ge(cs_ready, 1)
            dve.wait_ge(cs_centred, 1)
            cp = cmp_p[:, :, :, 0:N_CMP]
            for tt in range(NT):
                unseen = table("unseen")[:, 16 * tt:16 * tt + N_CMP].unsqueeze(1).to_broadcast([P, HEADS // 2, N_CMP])
                for odd in range(2):
                    link(v.tensor_tensor(cp[:, tt, odd::2, :],
                                         bank[2 + odd][:, tt * 128:(tt + 1) * 128].rearrange("p (h n) -> p h n", n=16)[:, :, 0:N_CMP],
                                         unseen, ALU.add))
            link(v.tensor_reduce(cmp_max[:, :, :], cp, AX, ALU.max))
            v.tensor_tensor(cp, cp, cmp_max[:, :, :].unsqueeze(3).to_broadcast([P, NT, HEADS, N_CMP]), ALU.subtract).then_inc(cs_centred, 1)
            nsa_copy(8)
            dve.wait_ge(cs_exp, 1)
            link(v.tensor_reduce(cmp_sum[:, :, :], cp, AX, ALU.add))
            link(v.reciprocal(cmp_sum[:, :, :], cmp_sum[:, :, :]))
            gate3 = gates[:, :, :].rearrange("p t (h b) -> p t h b", b=3)
            link(v.tensor_tensor(cmp_sum[:, :, :], cmp_sum[:, :, :], gate3[:, :, :, 0], ALU.mult))
            for tt in range(NT):
                seen_tt = table("seen")[:, 16 * tt:16 * tt + N_CMP].unsqueeze(1).to_broadcast([P, HEADS, N_CMP])
                link(v.tensor_tensor(cp[:, tt, :, :], cp[:, tt, :, :], seen_tt, ALU.mult))
            v.tensor_tensor(cp, cp, cmp_sum[:, :, :].unsqueeze(3).to_broadcast([P, NT, HEADS, N_CMP]), ALU.mult).then_inc(cp_ready, 1)
            nsa_copy(10)
            dve.wait_ge(cpT_psum, 1)
            v.tensor_copy(cmp_pT[:, 0:2, :].rearrange("p g q -> p (g q)"), bank[4][:, :]).then_inc(cpT_dve, 1)
            softmax_steps(1, lambda m, b: gate3[:, :, 2 * m:2 * m + 2, 1 + b].rearrange("p t a -> p a t"))
            attention_norm(1)
            route_tokens(1)
            experts(1)
            overflow(1)
            expert_norm(1)

        @block.scalar
        def _(act):
            s_ = nc.scalar

            def xT_copy(n, tt):
                for half in range(2):
                    act.wait_ge(xT_ready, 2 * (NT * n + tt) + half + 1)
                    s_.copy(xT[:, 4 * half:4 * half + 4, tt * P:(tt + 1) * P],
                            bank[4 + half][:, :].rearrange("p (t q) -> p t q", q=P)).then_inc(xT_copied, 1)

            def softmax_steps(l):
                n_steps = len(job_pairs[l])
                for s in range(n_steps + 2):
                    if s < n_steps:
                        act.wait_ge(max_ready[l], s + 1)
                        for a in range(2):
                            for tt, (x, y) in enumerate(((0, P), (P, 3 * P))):
                                pr = probs[:, 2 * (s % 3) + a, x:y]
                                last = s_.activation(pr, pr, ACT.Exp, bias=job_max[:, s % 3, a, tt:tt + 1],
                                                     accum_out=job_sum[:, s % 3, a, tt:tt + 1])
                        last.then_inc(exp_ready[l], 1)
                    for kind, k in beside[l].get(s, []):
                        if kind == "proj" and k % 2 == 1:
                            moba_copy(k)
                    if s >= 2:
                        j = s - 2
                        act.wait_ge(probsT_ready[l], j + 1)
                        after(act, pv_done[l], j - 1)
                        s_.copy(probsT[:, 2 * (j % 2) + 1, :], bank[5][:, 0:3 * P]).then_inc(probsT_act[l], 1)

            def norm(l, n):
                for tt in range(NT):
                    act.wait_ge(var_ready, norm_tiles(l, n, tt))
                    s_.activation(rstd[:, tt:tt + 1], rstd[:, tt:tt + 1], ACT.Sqrt).then_inc(std_ready, 1)
                    if l + n < 2:
                        xT_copy(2 * l + n + 1, tt)

            def route_tokens(l):
                act.wait_ge(logits_shifted[l], 1)
                s_.activation(route[:, 0, :, :], route[:, 0, :, :], ACT.Exp).then_inc(logits_exp[l], 1)

            def experts(l):
                def gated(i):
                    act.wait_ge(gate_done[l], i + 1)
                    after(act, hid_ready[l], i)
                    s_.activation(silu, bank[2][:, :], ACT.Silu).then_inc(silu_ready[l], 1)

                def copy_hidT(i):
                    act.wait_ge(hidT_psum[l], i + 1)
                    s_.copy(hidT.rearrange("p m s -> p (m s)"), bank[4][:, :]).then_inc(hidT_ready[l], 1)

                def copy_xg(i):
                    act.wait_ge(gathered[l], 2 * i + 2)
                    s_.copy(xgT[:, 4:8, :].rearrange("p t s -> p (t s)"), bank[1][:, :]).then_inc(xg_act[l], 1)

                def copy_pickwT(i):
                    act.wait_ge(pickwT_psum[l], i + 1)
                    s_.copy(pick_wT.rearrange("p t q -> p (t q)"), bank[7][:, 0:SEQ]).then_inc(pickwT_ready[l], 1)

                def copy_y(i):
                    act.wait_ge(down_done[l], 2 * i + 2)
                    s_.copy(y_slot[:, 512:1024], bank[6][:, :]).then_inc(y_act[l], 1)

                def pair(i, first, last):
                    gated(i)
                    copy_hidT(i)
                    if not last:
                        copy_xg(i + 1)
                    copy_pickwT(i)
                    copy_y(i)

                copy_xg(0)
                pair(0, True, False)
                with act.Fori(1, PAIRS - 1) as i:
                    pair(i, False, False)
                pair(PAIRS - 1, False, True)

            def overflow(l):
                act.wait_ge(flag_ready[l], 1)
                flag = act.value_load(crowded_i[0:1, 0:1], min_val=0, max_val=1)
                with act.If(flag > 0):
                    with act.Fori(0, E) as e:
                        for r in range(2):
                            k = e * 12 + 6 * r + 1
                            act.wait_ge(ov_pe[l], k + 1)
                            s_.copy(pick_wT.rearrange("p t q -> p (t q)"), bank[2][:, 0:SEQ]).then_inc(ov_act[l], 1)
                            act.wait_ge(ov_pe[l], k + 2)
                            s_.activation(silu, bank[2][:, :], ACT.Silu).then_inc(ov_silu[l], 1)
                            act.wait_ge(ov_pe[l], k + 4)
                            s_.copy(y_slot[:, 0:512], bank[6][:, :])
                            s_.copy(y_slot[:, 512:1024], bank[7][:, :]).then_inc(ov_act[l], 1)
                with act.Else():
                    act.nop()

            for tt in range(NT):
                xT_copy(0, tt)

            def moba_copy(g):
                u = g // 2
                hh = u // 3
                act.wait_ge(proj_ready[0], g + 1)
                if u % 3 == 0:
                    ins = s_.mul(qT[:, 4 * hh + 2:4 * hh + 4, :].rearrange("p m q -> p (m q)"), bank[1][:, :], DH ** -0.5)
                elif u % 3 == 1:
                    ins = s_.copy(kT[:, 4 * hh + 2:4 * hh + 4, :].rearrange("p m q -> p (m q)"), bank[1][:, :])
                else:
                    ins = s_.copy(v_tok[:, 1, hh * 512:(hh + 1) * 512], bank[1][:, :])
                ins.then_inc(proj_act[0], 1)

            for g in (1, 3, 5):
                moba_copy(g)
            softmax_steps(0)
            norm(0, 0)
            route_tokens(0)
            experts(0)
            overflow(0)
            norm(0, 1)

            act.wait_ge(proj_ready[1], 2)
            copy_cmp_in(s_.copy, 1, bank[1]).then_inc(proj_act[1], 1)
            act.wait_ge(proj_ready[1], 3)
            s_.activation(gates[:, :, :], bank[0][:, 0:NT * P].rearrange("p (t n) -> p t n", n=P)[:, :, 0:3 * HEADS],
                          ACT.Exp, scale=-1.0).then_inc(gate_exp, 1)

            def nsa_copy(g):
                act.wait_ge(proj_ready[1], g + 1)
                if g < 7:
                    c = (g - 3) // 2
                    last = s_.mul(qT[:, 4 * c:4 * c + 2, :].rearrange("p m q -> p (m q)"), bank[1][:, :], DH ** -0.5)
                else:
                    for dst in (0, DH):
                        for a in range(2):
                            last = s_.copy(nsa_kT[dst:dst + DH, (g - 7) // 2, 2 * a:2 * a + 2, :].rearrange("p j q -> p (j q)"),
                                           bank[1][DH * a:DH * a + DH, :])
                last.then_inc(proj_act[1], 1)

            nsa_copy(3)
            act.wait_ge(chid_psum, 1)
            s_.activation(cmp_hid[:, :], bank[2][:, 0:CMP_HID], ACT.Gelu_apprx_tanh).then_inc(chid_ready, 1)
            nsa_copy(5)
            act.wait_ge(chidT_psum, 1)
            s_.copy(cmp_hidT[:, :, :].rearrange("p f n -> p (f n)"), bank[3][:, 0:CMP_HID]).then_inc(chidT_ready, 1)
            nsa_copy(7)
            act.wait_ge(cs_centred, 2)
            cp = cmp_p[:, :, :, 0:N_CMP].rearrange("p t h n -> p (t h) n")
            s_.activation(cp, cp, ACT.Exp).then_inc(cs_exp, 1)
            nsa_copy(9)
            act.wait_ge(cpT_psum, 2)
            s_.copy(cmp_pT[:, 2:4, :].rearrange("p g q -> p (g q)"), bank[5][:, :]).then_inc(cpT_act, 1)
            softmax_steps(1)
            norm(1, 0)
            route_tokens(1)
            experts(1)
            overflow(1)
            norm(1, 1)


_INS = ['x', 'rel_bias', 'router_w', 'router_b', 'ln_g', 'ln_b', 'moba_w_in', 'moba_w_out', 'nsa_w_in', 'nsa_w_out',
        'nsa_pos_k', 'nsa_pos_v', 'nsa_ck_w1', 'nsa_ck_w2', 'nsa_cv_w1', 'nsa_cv_w2', 'moe_w_gate', 'moe_w_up', 'moe_w_down']


def kernel(**inputs):
    import concourse.bacc as bacc
    from concourse.bass_utils import run_bass_kernel_spmd

    nc = bacc.Bacc("TRN2", target_bir_lowering=False, num_devices=1)
    arrays, args = {}, []
    for name in _INS:
        a = np.ascontiguousarray(inputs[name])
        arrays[f"in_{name}"] = a
        args.append(nc.dram_tensor(f"in_{name}", a.shape, mybir.dt.from_np(a.dtype), kind="ExternalInput").ap())
    tables, place = shape_tables()
    arrays["in_tables"] = tables
    args.append(nc.dram_tensor("in_tables", tables.shape, F32, kind="ExternalInput").ap())
    out = nc.dram_tensor("out", (1, SEQ, D), F32, kind="ExternalOutput").ap()
    build(nc, *args, place, out)
    return run_bass_kernel_spmd(nc, [arrays], core_ids=[0]).results[0]["out"]
```

```python
from contextlib import ExitStack

import numpy as np

import concourse.bass as bass
from concourse import mybir

F32 = mybir.dt.float32
I32 = mybir.dt.int32
ALU = mybir.AluOpType
ACT = mybir.ActivationFunctionType
AX = mybir.AxisListType.X

P = 128
D = 1024
SEQ = 256
NT = SEQ // P
KT = D // P
HEADS, DH = 16, 64
KV = 4
GROUP = HEADS // KV
LAYERS = 2
BUCKETS, MAX_DIST = 32, 128
CMP_LEN, CMP_STRIDE, CMP_HID = 32, 16, 256
N_CMP = (SEQ - CMP_LEN) // CMP_STRIDE + 1
CMP_ROWS = 64
E, EG, NG = 32, 4, 8
FF = 512
FT = FF // P
CAP = 64
PAIRS = E // 2
SPARE_PAIRS = (5, 11)
ALPHA = (2 * LAYERS) ** 0.25
EPS = 1e-5
NEG = -1e30
BIAS_W = 384
SLOT = 4096
NSLOT = 6
SMALL_LOADS = 6 * 16
OV_PE = 2 * 6


def t5_buckets(n):
    exact = BUCKETS // 2
    nf = np.maximum(n, 1).astype(np.float32)
    large = exact + (np.log(nf / np.float32(exact)) / np.float32(np.log(MAX_DIST / exact))
                     * (BUCKETS - exact)).astype(np.int32)
    return np.where(n < exact, n, np.minimum(large, BUCKETS - 1))


def shape_tables():
    p = np.arange(P)
    cols = {}
    cols["ident"] = np.eye(P)
    cols["before"] = (p[:, None] < p[None, :]).astype(float)
    cols["ones"] = np.ones((P, P))
    cols["slot"] = np.tile(np.arange(P) % CAP, (P, 1))
    cols["slot2"] = np.tile(np.arange(P), (P, 1))
    cols["first32"] = np.tile(E - np.arange(E), (P, 1))
    cols["first8"] = np.tile(NG - np.arange(NG), (P, 1))
    q = np.arange(NT)[None, :, None] * P + p[:, None, None]
    seen = np.arange(16)[None, None, :] * CMP_STRIDE + CMP_LEN - 1 <= q
    cols["seen"] = seen.reshape(P, -1)
    cols["unseen"] = np.where(seen, 0.0, NEG).reshape(P, -1)
    dist = np.arange(BIAS_W) - (P - 1)
    hot = np.zeros((P, BIAS_W))
    hot[t5_buckets(np.maximum(dist, 0)), np.arange(BIAS_W)] = dist >= 0
    hot[BUCKETS] = dist < 0
    cols["bucket"] = hot
    at, place = 0, {}
    for name, c in cols.items():
        place[name] = (at, at + c.shape[1])
        at += c.shape[1]
    return np.ascontiguousarray(np.concatenate(list(cols.values()), 1), dtype=np.float32), place


def after(eng, sem, value):
    if not isinstance(value, int) or value > 0:
        eng.wait_ge(sem, value)


def build(nc, x_in, rel_bias, router_w, router_b, ln_g, ln_b, moba_w_in, moba_w_out, nsa_w_in, nsa_w_out,
          nsa_pos_k, nsa_pos_v, nsa_ck_w1, nsa_ck_w2, nsa_cv_w1, nsa_cv_w2,
          moe_w_gate, moe_w_up, moe_w_down, tables, place, out):
    ctx = ExitStack()
    with ctx:
        def sb(name, shape, dt=F32):
            return ctx.enter_context(nc.sbuf_tensor(name, shape, dt))

        def sem(name):
            return ctx.enter_context(nc.semaphore(name))

        def sem2(name):
            return [sem(f"{name}_{l}") for l in range(LAYERS)]

        ring = sb("ring", [P, NSLOT, SLOT])
        xs = sb("xs", [P, NT, D])
        acc = sb("acc", [P, NT, D])
        norm_w = sb("norm_w", [P, 2, D])
        bias = sb("bias", [P, HEADS, SEQ])
        xT = sb("xT", [P, KT, SEQ])
        work = sb("work", [P, 4 * 2048])
        tab = sb("tab", [P, place["bucket"][0]])
        softmax_area = sb("softmax_area", [P, SLOT])
        probs = softmax_area[:, 0:18 * P].rearrange("p (j k) -> p j k", k=3 * P)
        probsT = softmax_area[:, 18 * P:30 * P].rearrange("p (j k) -> p j k", k=3 * P)
        rel_w = sb("rel_w", [BUCKETS + 1, HEADS])
        router = sb("router", [P, (KT - 1) * E + P])
        gate_w = sb("gate_w", [P, (KT - 1) * 3 * HEADS + P])
        router_bias = sb("router_bias", [P, E])
        pos_rows = sb("pos_rows", [16, 2, P])
        pos_cols = sb("pos_cols", [P, 2, 16])
        cmp_w2 = sb("cmp_w2", [P, 2, 2, DH])
        gates = sb("gates", [P, NT, 3 * HEADS])
        cmp_hid = sb("cmp_hid", [P, CMP_HID])
        cmp_hidT = sb("cmp_hidT", [P, 2, P])
        cmp_keyT = sb("cmp_keyT", [P, 80])
        cmp_val = sb("cmp_val", [P, KV, DH])
        cmp_max = sb("cmp_max", [P, NT, HEADS])
        cmp_sum = sb("cmp_sum", [P, NT, HEADS])
        job_max = sb("job_max", [P, 3, 2, NT])
        job_sum = sb("job_sum", [P, 3, 2, NT])
        job_scale = sb("job_scale", [P, 3, 2, NT])
        stats = sb("stats", [P, NT, 12])
        moments = sb("moments", [P, NT, 2])
        rstd = sb("rstd", [P, NT])
        one = sb("one", [P, 8, NT])
        slot_of = sb("slot_of", [P, NT, E])
        chosen = sb("chosen", [P, NT, E])
        weight = sb("weight", [P, NT, E])
        crowded = sb("crowded", [P, 1])
        crowded_i = sb("crowded_i", [P, 1], I32)

        bank = [ctx.enter_context(nc.psum_tensor(f"bank{i}", [P, 512], F32)) for i in range(8)]
        dist_dram = nc.dram_tensor("dist_rows", [HEADS, BIAS_W], F32)

        bucket_rows = acc[0:BUCKETS + 1, 0, 0:BIAS_W]
        dist_row = acc[0:HEADS, 1, 0:BIAS_W]

        def table(name, n=P):
            a, b = place[name]
            return tab[0:n, a:b]

        ident = table("ident")

        def bias_for(h, tt):
            n = (tt + 1) * P
            whole = bias[:, h, :]
            return bass.AP(tensor=whole.tensor, offset=whole.offset + n - 1, ap=[list(whole.ap[0]), [-1, n]])

        qT = work[:, 0:2048].rearrange("p (m q) -> p m q", q=SEQ)
        kT = work[:, 2048:4096].rearrange("p (m q) -> p m q", q=SEQ)
        v_tok = work[:, 4096:6144].rearrange("p (k n) -> p k n", k=NT)
        oT = work[:, 6144:8192].rearrange("p (m q) -> p m q", q=SEQ)
        nsa_kT = work[:, 2048:4096].rearrange("p (b k q) -> p b k q", b=2, k=KV)
        nsa_v = work[:, 4096:5120].rearrange("p (b k n) -> p b k n", b=2, k=NT)
        cmp_p = work[:, 5120:6144].rearrange("p (t h n) -> p t h n", t=NT, n=32)
        cmp_sT = work[:, 6144:7168].rearrange("p (b n) -> p b n", b=2)
        cmp_pT = xT[:, 0:4, :]
        cmp_in = acc[:, :, :].rearrange("p t d -> p (t d)").rearrange("p (b l n) -> p b l n", b=2, l=16)
        xgT = work[:, 0:1024].rearrange("p (t s) -> p t s", s=P)
        yT = work[:, 1024:2048].rearrange("p (t s) -> p t s", s=P)
        y_slot = work[:, 2048:3072]
        hid = work[:, 3072:3584]
        silu = work[:, 3584:4096]
        pick = work[:, 4096:4352].rearrange("p (t e s) -> p t e s", t=NT, e=2)
        pick_w = work[:, 4352:4608].rearrange("p (t e s) -> p t e s", t=NT, e=2)
        pick_wT = work[:, 4608:4864].rearrange("p (t q) -> p t q", t=NT)
        hidT = work[:, 5504:6016].rearrange("p (m s) -> p m s", s=P)
        route = work[:, 4864:5376].rearrange("p (k t e) -> p k t e", t=NT, e=E)
        small = work[:, 5376:5504].rearrange("p (k t g) -> p k t g", t=NT, g=NG)

        def cols(w, c):
            return w[:, c * 512:(c + 1) * 512].rearrange("(p t) n -> p t n", t=KT)

        def rows(w, c):
            return w[c * 512:(c + 1) * 512, :].rearrange("(m p) n -> p m n", p=P)

        moba_uses = [cols(moba_w_in[0], c) for c in (0, 2, 4, 1, 3, 5)] + [rows(moba_w_out[0], c) for c in (0, 1)]
        cmp_w1 = [w[0].rearrange("(l p) n -> p l n", p=P) for w in (nsa_ck_w1, nsa_cv_w1)]
        nsa_uses = ([cols(nsa_w_in[0], c) for c in (2, 0, 1)] + cmp_w1 + [cols(nsa_w_in[0], c) for c in (3, 4)]
                    + [rows(nsa_w_out[0], c) for c in (0, 1)])
        first_use = [0, len(moba_uses) + 3 * E]
        first_moe = [len(moba_uses), len(moba_uses) + 3 * E + len(nsa_uses)]
        USES_PER_PAIR = 6
        DOWN_PAIR, UP_PAIR = SPARE_PAIRS
        spare_roles = [{DOWN_PAIR: (4, 5)}, {DOWN_PAIR: (4, 5), UP_PAIR: (3,)}]
        spared = [first_moe[l] + i * USES_PER_PAIR + j for l in range(LAYERS) for i in spare_roles[l] for j in spare_roles[l][i]]

        def stretches(pairs, end):
            out_, at = [], 1
            for p in pairs:
                out_.append((at, p, p))
                at = p + 1
            return out_ + [(at, end, None)]

        def loads_through(u):
            return 16 * (u // NSLOT + 1 - sum(v < u and v % NSLOT == u % NSLOT for v in spared))

        def spare_weights(j):
            if j == 5:
                halves = [x.rearrange("p a b -> p (a b)").rearrange("p (t n) -> p t n", t=2) for x in (oT, xT)]
                return lambda t, a, b: halves[t // 2][:, t % 2, a:b]
            if j == 4:
                whole = softmax_area[:, :].rearrange("p (t n) -> p t n", t=4)
            else:
                whole = bias[:, :, :].rearrange("p h k -> p (h k)").rearrange("p (t n) -> p t n", t=KT)
            return lambda t, a, b: whole[:, t, a:b]

        def slot_no(u):
            return u % NSLOT

        def slot8(u):
            return ring[:, slot_no(u), :].rearrange("p (t n) -> p t n", t=KT)

        def slot4(u):
            return ring[:, slot_no(u), :].rearrange("p (t n) -> p t n", t=4)

        def slot16(u):
            return ring[:, slot_no(u), :].rearrange("p (t n) -> p t n", t=16)

        loaded = [sem(f"loaded{s}") for s in range(NSLOT)]
        x_loaded, tables_loaded, small_loaded = sem("x_loaded"), sem("tables_loaded"), sem("small_loaded")
        norm_loaded = sem("norm_loaded")
        spare_loaded = {j: sem2(f"spare{j}_loaded") for j in (3, 4, 5)}
        mask_row, rel_loaded = sem("mask_row"), sem("rel_loaded")
        dist_ready, dist_copied, dist_stored, bias_loaded = (
            sem("dist_ready"), sem("dist_copied"), sem("dist_stored"), sem("bias_loaded"))
        xT_ready, xT_copied = sem("xT_ready"), sem("xT_copied")
        proj_ready, proj_dve, proj_act = sem2("proj_ready"), sem2("proj_dve"), sem2("proj_act")
        scores_ready, scores_read = sem2("scores_ready"), sem2("scores_read")
        max_ready, exp_ready, scale_ready, probs_dve, probs_pool = (
            sem2("max_ready"), sem2("exp_ready"), sem2("scale_ready"), sem2("probs_dve"), sem2("probs_pool"))
        probsT_ready, probsT_dve, probsT_act = sem2("probsT_ready"), sem2("probsT_dve"), sem2("probsT_act")
        pv_done, o_copied = sem2("pv_done"), sem2("o_copied")
        mix_ready, mix_added = sem2("mix_ready"), sem2("mix_added")
        var_ready, std_ready, normed_tiles = sem("var_ready"), sem("std_ready"), sem("normed_tiles")
        pads_ready = sem("pads_ready")
        gate_ready, gate_exp, gates_ready = sem("gate_ready"), sem("gate_exp"), sem("gates_ready")
        cpos_ready, cpos_copied = sem("cpos_ready"), sem("cpos_copied")
        cin_copied, cin_ready = sem("cin_copied"), sem("cin_ready")
        chid_psum, chid_ready = sem("chid_psum"), sem("chid_ready")
        chidT_psum, chidT_ready = sem("chidT_psum"), sem("chidT_ready")
        ckv_psum, ckv_ready = sem("ckv_psum"), sem("ckv_ready")
        cs_ready, cs_centred, cs_exp, cp_ready = sem("cs_ready"), sem("cs_centred"), sem("cs_exp"), sem("cp_ready")
        csT_psum, csT_dve, csT_act = sem("csT_psum"), sem("csT_dve"), sem("csT_act")
        cpT_psum, cpT_dve, cpT_act = sem("cpT_psum"), sem("cpT_dve"), sem("cpT_act")
        logits_ready, logits_shifted, logits_exp = sem2("logits_ready"), sem2("logits_shifted"), sem2("logits_exp")
        chosen_ready, ranks_ready, flag_ready = sem2("chosen_ready"), sem2("ranks_ready"), sem2("flag_ready")
        pick_ready, pickw_ready, pickwT_psum, pickwT_ready = (
            sem2("pick_ready"), sem2("pickw_ready"), sem2("pickwT_psum"), sem2("pickwT_ready"))
        gathered, xg_dve, xg_act = sem2("gathered"), sem2("xg_dve"), sem2("xg_act")
        gate_done, up_done, silu_ready, hid_ready = (
            sem2("gate_done"), sem2("up_done"), sem2("silu_ready"), sem2("hid_ready"))
        hidT_psum, hidT_ready = sem2("hidT_psum"), sem2("hidT_ready")
        down_done, y_dve, y_act = sem2("down_done"), sem2("y_dve"), sem2("y_act")
        spread_ready, acc_added, acc_started = sem2("spread_ready"), sem2("acc_added"), sem2("acc_started")
        dve_chain = sem("dve_chain")
        ov_loaded = [sem2(f"ov_loaded{s}") for s in range(3)]
        ov_pe, ov_dve, ov_act = sem2("ov_pe"), sem2("ov_dve"), sem2("ov_act")
        ov_silu, ov_chain = sem2("ov_silu"), sem2("ov_chain")
        stored = sem("stored")

        freed = {}
        for l, uses in enumerate((moba_uses, nsa_uses)):
            for n in (0, 1):
                freed[first_use[l] + len(uses) - 2 + n] = (mix_ready[l], 4 * (n + 1))
        for n in range(6):
            freed[n] = (proj_ready[0], 2 * n + 2)
        for n, g in ((0, 2), (1, 5), (2, 7), (5, 9), (6, 11)):
            freed[first_use[1] + n] = (proj_ready[1], g)
        for n in (3, 4):
            freed[first_use[1] + n] = (chid_psum, 1)

        PAIR_USES = [("gate", 0), ("gate", 1), ("up", 0), ("up", 1), ("down", 0), ("down", 1)]

        def pair_freed(l, j, i):
            kind, _ = PAIR_USES[j]
            if kind == "down":
                return down_done[l], 2 * i + 2
            return (gate_done if kind == "gate" else up_done)[l], i + 1

        def slot_for(kind, s):
            r = ring[:, s, :]
            return r.rearrange("p (t n) -> p t n", t=4 if kind == "down" else KT)

        def copy_cmp_in(copy, b, ps):
            for hkv in range(KV):
                for o in range(2):
                    src = ps[DH * (hkv % 2):DH * (hkv % 2) + DH, (hkv // 2) * SEQ + o:(hkv // 2) * SEQ + o + 1]
                    src = bass.AP(tensor=src.tensor, offset=src.offset, ap=[list(src.ap[0]), [2, 16], [CMP_STRIDE, N_CMP]])
                    last = copy(cmp_in[DH * o:DH * o + DH, b, :, hkv * N_CMP:(hkv + 1) * N_CMP], src)
            return last

        job_pairs = [[(m, 0) for m in range(HEADS // 2)],
                     [(m, b) for m in range(HEADS // 2) for b in range(2)]]
        beside = [{0: [("proj", 6), ("proj", 7)], 1: [("proj", 8)], 2: [("proj", 9), ("proj", 10)], 3: [("proj", 11)],
                   8: [("out", 0)], 9: [("out", 1), ("out", 2)], 10: [("out", 3)]},
                  {0: [("proj", 10)], 1: [("cmp", 0)], 12: [("out", 0)], 13: [("out", 1)], 14: [("out", 2)], 15: [("out", 3)]}]

        def norm_tiles(l, n, tt):
            return NT * (2 * l + n) + tt + 1

        block = ctx.enter_context(nc.Block())

        @block.sync
        def _(sp):
            def load_fixed(l, uses):
                for n, src in enumerate(uses):
                    u = first_use[l] + n
                    if u >= NSLOT:
                        sp.wait_ge(*released(u - NSLOT))
                    dst = ring[:, slot_no(u), :].rearrange("p (t n) -> p t n", t=src.shape[1])
                    sp.dma_start(dst, src).then_inc(loaded[slot_no(u)], 16)

            def released(u):
                if u in freed:
                    return freed[u]
                l = 0 if u < first_use[1] else 1
                i, j = divmod(u - first_moe[l], USES_PER_PAIR)
                return pair_freed(l, j, i)

            def weights_of(l, kind, e):
                src = {"gate": moe_w_gate, "up": moe_w_up, "down": moe_w_down}[kind][l, bass.ds(e, 1), :, :]
                if kind == "down":
                    return src.rearrange("a (m p) n -> p (a m) n", p=P)
                return src.rearrange("a (p t) n -> p (a t) n", t=KT)

            def load_pair(l, i, j):
                kind, e = PAIR_USES[j]
                s = slot_no(first_moe[l] + j)
                sp.dma_start(slot_for(kind, s), weights_of(l, kind, 2 * i + e)).then_inc(loaded[s], 16)

            def load_pair_after(l, i, j, before=None):
                sp.wait_ge(*pair_freed(l, j, i - 1 if before is None else before))
                load_pair(l, i, j)

            def load_spares_early(l):
                sp.wait_ge(pv_done[l], len(job_pairs[l]))
                sp.dma_start(softmax_area[:, :].rearrange("p (t n) -> p t n", t=4),
                             weights_of(l, "down", 2 * DOWN_PAIR)).then_inc(spare_loaded[4][l], 16)
                if UP_PAIR in spare_roles[l]:
                    sp.dma_start(bias[:, :, :].rearrange("p h k -> p (h k)").rearrange("p (t n) -> p t n", t=KT),
                                 weights_of(l, "up", 2 * UP_PAIR + 1)).then_inc(spare_loaded[3][l], 16)

            def load_spares_late(l):
                down = weights_of(l, "down", 2 * DOWN_PAIR + 1)
                halves = [x.rearrange("p a b -> p (a b)").rearrange("p (t n) -> p t n", t=2) for x in (oT, xT)]
                sp.wait_ge(mix_ready[l], 8)
                sp.dma_start(halves[0], down[:, 0:2, :]).then_inc(spare_loaded[5][l], 16)
                sp.wait_ge(logits_ready[l], 1)
                sp.dma_start(halves[1], down[:, 2:4, :]).then_inc(spare_loaded[5][l], 16)

            def load_spare_pair(l, i):
                for j in range(USES_PER_PAIR):
                    if j not in spare_roles[l][i]:
                        load_pair_after(l, i, j)
                for j in range(USES_PER_PAIR):
                    load_pair_after(l, i + 1, j, i - 1 if j in spare_roles[l][i] else i)

            sp.dma_start(xs[:, :, :], x_in[0].rearrange("(t p) d -> p t d", p=P)).then_inc(x_loaded, 16)
            sp.dma_start(tab[:, :], tables[:, 0:place["bucket"][0]]).then_inc(tables_loaded, 16)
            sp.dma_start(bucket_rows, tables[0:BUCKETS + 1, place["bucket"][0]:place["bucket"][1]]).then_inc(tables_loaded, 16)
            for l, uses in enumerate((moba_uses, nsa_uses)):
                load_fixed(l, uses)
                for j in range(USES_PER_PAIR):
                    if j == 4:
                        load_spares_early(l)
                    sp.wait_ge(*released(first_moe[l] + j - NSLOT))
                    load_pair(l, 0, j)
                load_spares_late(l)
                for first, end, spare in stretches(spare_roles[l], PAIRS):
                    with sp.Fori(first if first == 1 else first + 1, end) as i:
                        for j in range(USES_PER_PAIR):
                            load_pair_after(l, i, j)
                    if spare:
                        load_spare_pair(l, spare)
                sp.wait_ge(flag_ready[l], 1)
                flag = sp.value_load(crowded_i[0:1, 0:1], min_val=0, max_val=1)
                with sp.If(flag > 0):
                    for j in range(USES_PER_PAIR):
                        sp.wait_ge(*pair_freed(l, j, PAIRS - 1))
                    with sp.Fori(0, E) as e:
                        sp.wait_ge(ov_pe[l], e * OV_PE + 1)
                        for s, kind in enumerate(("gate", "up", "down")):
                            sp.dma_start(slot_for(kind, s), weights_of(l, kind, e)).then_inc(ov_loaded[s][l], 16)
                    sp.wait_ge(ov_pe[l], E * OV_PE + 1)
                with sp.Else():
                    sp.nop()
            for tt in range(NT):
                sp.wait_ge(normed_tiles, norm_tiles(1, 1, tt))
                sp.dma_start(out[0, tt * P:(tt + 1) * P, :], xs[:, tt, :]).then_inc(stored, 16)
            sp.wait_ge(stored, 16 * NT)

        @block.gpsimd
        def _(pool):
            nc.gpsimd.memset(rel_w[BUCKETS:BUCKETS + 1, :], NEG).then_inc(mask_row, 1)
            pool.dma_start(rel_w[0:BUCKETS, :], rel_bias).then_inc(rel_loaded, 16)
            pool.wait_ge(mask_row, 1)
            nc.gpsimd.memset(router[:, KT * E:], 0.0).then_inc(pads_ready, 1)
            nc.gpsimd.memset(gate_w[:, KT * 3 * HEADS:], 0.0).then_inc(pads_ready, 1)
            pool.dma_start(router[:, 0:KT * E].rearrange("p (t n) -> p t n", t=KT),
                           router_w.rearrange("(p t) n -> p t n", t=KT)).then_inc(small_loaded, 16)
            pool.dma_start(router_bias[:, :], bass.AP(tensor=router_b.tensor, offset=0, ap=[[0, P], [1, E]])).then_inc(small_loaded, 16)
            for b, src in enumerate((nsa_pos_k, nsa_pos_v)):
                pool.dma_start(pos_rows[:, b, :], src[0].rearrange("(l o) d -> l (o d)", o=2)).then_inc(small_loaded, 16)
            for b, src in enumerate((nsa_ck_w2, nsa_cv_w2)):
                pool.dma_start(cmp_w2[:, b, :, :], src[0].rearrange("(f p) d -> p f d", p=P)).then_inc(small_loaded, 16)
            pool.wait_ge(dist_copied, 1)
            pool.dma_start(dist_dram.ap(), dist_row).then_inc(dist_stored, 16)
            pool.wait_ge(dist_stored, 16)
            pool.dma_start(bias[:, :, :], bass.AP(tensor=dist_dram.ap().tensor, offset=0, ap=[[1, P], [BIAS_W, HEADS], [1, SEQ]])).then_inc(bias_loaded, 16)
            pool.dma_start(gate_w[:, 0:KT * 3 * HEADS].rearrange("p (t n) -> p t n", t=KT),
                           nsa_w_in[0][:, 2560:2608].rearrange("(p t) n -> p t n", t=KT)).then_inc(small_loaded, 16)

            def load_norm(k):
                if k:
                    pool.wait_ge(normed_tiles, NT * k)
                for w, src in enumerate((ln_g, ln_b)):
                    pool.dma_start(norm_w[:, w, :], bass.AP(tensor=src.tensor, offset=k * D, ap=[[0, P], [1, D]])).then_inc(norm_loaded, 16)

            def scale_probs(l):
                for s in range(len(job_pairs[l])):
                    pool.wait_ge(scale_ready[l], s + 1)
                    pr = probs[:, 2 * (s % 3) + 1, 0:P]
                    nc.gpsimd.tensor_scalar(pr, pr, job_scale[:, s % 3, 1, 0:1], None, ALU.mult).then_inc(probs_pool[l], 1)

            load_norm(0)
            for l in range(LAYERS):
                if l:
                    nc.gpsimd.memset(cmp_in[:, :, :, KV * N_CMP:], 0.0).then_inc(pads_ready, 1)
                scale_probs(l)
                load_norm(2 * l + 1)
                if l + 1 < LAYERS:
                    load_norm(2 * l + 2)

        @block.tensor
        def _(pe):
            mm, tr = nc.tensor.matmul, nc.tensor.transpose

            def arrived(u):
                pe.wait_ge(loaded[slot_no(u)], loads_through(u))

            def transpose_x(n, tt):
                after(pe, xT_copied, 2 * (NT * n + tt))
                for half in range(2):
                    for t in range(4):
                        last = tr(bank[4 + half][:, t * P:(t + 1) * P], xs[:, tt, 4 * half + t::KT], ident)
                    last.then_inc(xT_ready, 1)

            def xT_here(n, tt):
                pe.wait_ge(xT_copied, 2 * (NT * n + tt + 1))

            def normed(l, n, tt):
                k = norm_tiles(l, n, tt)
                pe.wait_ge(normed_tiles, k)

            def proj_bank_free(l, g):
                after(pe, proj_dve[l] if g % 2 == 0 else proj_act[l], g // 2)

            def project_T(l, g, w, lhs_cols):
                proj_bank_free(l, g)
                for n, pick_cols in enumerate(lhs_cols):
                    for t in range(KT):
                        last = mm(bank[g % 2][:, n * SEQ:(n + 1) * SEQ], pick_cols(w, t), xT[:, t, :],
                                  start=(t == 0), stop=(t == KT - 1))
                return last

            def project_tok(l, g, w, tt, width=512):
                proj_bank_free(l, g)
                for t in range(KT):
                    last = mm(bank[g % 2][:, 0:width], xT[:, t, tt * P:(tt + 1) * P], w[:, t, 0:width],
                              start=(t == 0), stop=(t == KT - 1))
                return last

            def tile_cols(m):
                return lambda w, t: w[:, t, m * P:(m + 1) * P]

            def attention(l, job, project, compressed=None, transpose_cmp=None):
                n_steps = len(job_pairs[l])
                for s in range(n_steps + 3):
                    if s < n_steps:
                        m, br = job_pairs[l][s]
                        after(pe, scores_read[l], s)
                        if br == 1 and s == 1:
                            pe.wait_ge(proj_act[l], 5)
                        both = [job(2 * m + a, br) for a in range(2)]
                        for a in range(2):
                            mm(bank[2 + a][:, 0:P], both[a]["q"][:, 0:P], both[a]["k"][:, 0:P], start=True, stop=True)
                        for a in range(2):
                            last = mm(bank[2 + a][:, P:3 * P], both[a]["q"][:, P:SEQ], both[a]["k"], start=True, stop=True)
                        last.then_inc(scores_ready[l], 1)
                    for kind, k in beside[l].get(s, []):
                        if kind == "proj":
                            project(k)
                        elif kind == "out":
                            out_piece(l, k)
                        else:
                            transpose_cmp()
                    if 0 <= s - 2 < n_steps:
                        j = s - 2
                        if j == 0 and compressed:
                            pe.wait_ge(cpT_dve, 1)
                            pe.wait_ge(cpT_act, 1)
                        pe.wait_ge(probs_dve[l], j + 1)
                        pe.wait_ge(probs_pool[l], j + 1)
                        after(pe, probsT_dve[l], j)
                        after(pe, probsT_act[l], j)
                        for a in range(2):
                            for b in range(3):
                                last = tr(bank[4 + a][:, b * P:(b + 1) * P], probs[:, 2 * (j % 3) + a, b * P:(b + 1) * P], ident)
                        last.then_inc(probsT_ready[l], 1)
                    if 0 <= s - 3:
                        j = s - 3
                        m, br = job_pairs[l][j]
                        final = j + 1 == n_steps or job_pairs[l][j + 1][0] != m
                        both = [job(2 * m + a, br) for a in range(2)]
                        pe.wait_ge(probsT_dve[l], j + 1)
                        pe.wait_ge(probsT_act[l], j + 1)
                        if br == 0:
                            after(pe, o_copied[l], m - 1)
                        elif j == 1:
                            pe.wait_ge(proj_dve[l], 6)
                        ps = [bank[6 + m % 2][DH * a:DH * a + DH, :] for a in range(2)]
                        pt = [probsT[:, 2 * (j % 2) + a, :] for a in range(2)]
                        for a in range(2):
                            mm(ps[a][:, 0:SEQ], both[a]["v"](0), pt[a][:, 0:SEQ], start=br == 0, stop=False)
                        for a in range(2):
                            last = mm(ps[a][:, P:SEQ], both[a]["v"](1), pt[a][:, SEQ:3 * P], start=False, stop=final and not compressed)
                        if final and compressed:
                            for a in range(2):
                                last = compressed(2 * m + a, ps[a][:, 0:SEQ])
                        last.then_inc(pv_done[l], 1)

            def out_piece(l, k):
                c, tt, n = k // 4, k // 2 % 2, k % 2
                if k % 4 == 0:
                    arrived(first_moe[l] - 2 + c)
                    pe.wait_ge(o_copied[l], 4 * (c + 1))
                after(pe, mix_added[l], k - 1)
                w = slot4(first_moe[l] - 2 + c)
                for t in range(4):
                    last = mm(bank[k % 2][:, :], oT[:, 4 * c + t, tt * P:(tt + 1) * P], w[:, t, n * 512:(n + 1) * 512],
                              start=(t == 0), stop=(t == 3))
                last.then_inc(mix_ready[l], 1)

            def keep_warm(n):
                for _ in range(n):
                    mm(bank[2][:, :], ident, tab[:, 0:512], start=True, stop=True)

            def route_tokens(l):
                for tt in range(NT):
                    normed(l, 0, tt)
                    transpose_x(2 * l + 1, tt)
                    if tt == 0:
                        pe.wait_ge(small_loaded, SMALL_LOADS)
                        pe.wait_ge(pads_ready, 2)
                    xT_here(2 * l + 1, tt)
                    for t in range(KT):
                        last = mm(bank[6][:, tt * P:(tt + 1) * P], xT[:, t, tt * P:(tt + 1) * P], router[:, t * E:t * E + P],
                                  start=(t == 0), stop=(t == KT - 1))
                last.then_inc(logits_ready[l], 1)
                keep_warm(8)
                pe.wait_ge(chosen_ready[l], 1)
                mm(bank[7][:, 0:E], table("before"), chosen[:, 0, :], start=True, stop=True)
                mm(bank[7][:, E:2 * E], table("ones"), chosen[:, 0, :], start=True, stop=False)
                mm(bank[7][:, E:2 * E], table("before"), chosen[:, 1, :], start=False, stop=True)
                mm(bank[7][:, 2 * E:3 * E], table("ones"), chosen[:, 0, :], start=True, stop=False)
                mm(bank[7][:, 2 * E:3 * E], table("ones"), chosen[:, 1, :], start=False, stop=True).then_inc(ranks_ready[l], 1)
                keep_warm(1)

            SPREAD_BANKS = [4, 0, 1, 7]

            def gather(l, i):
                pe.wait_ge(pick_ready[l], i + 1)
                for half in range(2):
                    after(pe, acc_added[l], 4 * (i - 2) + 2 + half)
                    for t in range(4):
                        for tt in range(NT):
                            last = mm(bank[half][:, t * P:(t + 1) * P], xs[:, tt, 4 * half + t::KT],
                                      pick[:, tt, :, :].rearrange("p e s -> p (e s)"), start=(tt == 0), stop=(tt == 1))
                    last.then_inc(gathered[l], 1)

            def gate_up(l, i, weights):
                pe.wait_ge(xg_dve[l], i + 1)
                pe.wait_ge(xg_act[l], i + 1)
                for k, done, read in ((0, gate_done, silu_ready), (1, up_done, hid_ready)):
                    after(pe, read[l], i)
                    w = [weights(2 * k + e) for e in range(2)]
                    for t in range(KT):
                        for e in range(2):
                            last = mm(bank[2 + k][e * CAP:(e + 1) * CAP, :], xgT[:, t, e * CAP:(e + 1) * CAP],
                                      w[e](t, 0, FF), start=(t == 0), stop=(t == KT - 1))
                    last.then_inc(done[l], 1)

            def transpose_hidden(l, i):
                pe.wait_ge(hid_ready[l], i + 1)
                after(pe, acc_added[l], 4 * (i - 1) + 1)
                for m in range(FT):
                    last = tr(bank[4][:, m * P:(m + 1) * P], hid[:, m * P:(m + 1) * P], ident)
                last.then_inc(hidT_psum[l], 1)

            def weights_by_slot(l, i):
                pe.wait_ge(pickw_ready[l], i + 1)
                after(pe, acc_added[l], 4 * i)
                for tt in range(NT):
                    last = tr(bank[7][:, tt * P:(tt + 1) * P], pick_w[:, tt, :, :].rearrange("p e s -> p (e s)"), ident)
                last.then_inc(pickwT_psum[l], 1)

            def down(l, i, weights):
                pe.wait_ge(hidT_ready[l], i + 1)
                w = [weights(4 + e) for e in range(2)]
                for n in range(2):
                    for m in range(FT):
                        for e in range(2):
                            last = mm(bank[5 + n][e * CAP:(e + 1) * CAP, :], hidT[:, m, e * CAP:(e + 1) * CAP],
                                      w[e](m, n * 512, (n + 1) * 512), start=(m == 0), stop=(m == FT - 1))
                    last.then_inc(down_done[l], 1)

            def spread(l, i):
                pe.wait_ge(y_dve[l], i + 1)
                pe.wait_ge(y_act[l], i + 1)
                pe.wait_ge(pickwT_ready[l], i + 1)
                for k, b in enumerate(SPREAD_BANKS):
                    tt, n = divmod(k, 2)
                    mm(bank[b][:, :], pick_wT[:, tt, :], y_slot[:, n * 512:(n + 1) * 512], start=True, stop=True).then_inc(spread_ready[l], 1)

            def experts(l):
                def pair(i, first=False, last=False, since=None, spare=None):
                    since = i if since is None else since

                    def weights(j):
                        if spare and j in spare_roles[l][spare]:
                            pe.wait_ge(spare_loaded[j][l], 32 if j == 5 else 16)
                            return spare_weights(j)
                        u = first_moe[l] + since * USES_PER_PAIR + j
                        pe.wait_ge(loaded[slot_no(u)], (i - since) * 16 + loads_through(u))
                        whole = slot8(u) if j < 4 else slot4(u)
                        return lambda t, a, b: whole[:, t, a:b]

                    gate_up(l, i, weights)
                    if not first:
                        spread(l, i - 1)
                    transpose_hidden(l, i)
                    if not last:
                        gather(l, i + 1)
                    weights_by_slot(l, i)
                    down(l, i, weights)

                gather(l, 0)
                pair(0, first=True)
                for first, end, spare in stretches(spare_roles[l], PAIRS - 1):
                    with pe.Fori(first, end) as i:
                        pair(i, since=first)
                    if spare:
                        pair(spare, spare=spare)
                pair(PAIRS - 1, last=True)
                spread(l, PAIRS - 1)

            def overflow(l):
                pe.wait_ge(flag_ready[l], 1)
                flag = pe.value_load(crowded_i[0:1, 0:1], min_val=0, max_val=1)
                with pe.If(flag > 0):
                    pe.wait_ge(acc_added[l], 4 * PAIRS)
                    tr(bank[6][:, 0:P], ident, ident).then_inc(ov_pe[l], 1)
                    with pe.Fori(0, E) as e:
                        for s in range(3):
                            pe.wait_ge(ov_loaded[s][l], 16 * e + 16)
                        for r in range(2):
                            n = e * 12 + 6 * r
                            m = e * 4 + 2 * r
                            pe.wait_ge(ov_dve[l], n + 2)
                            for half in range(2):
                                for t in range(4):
                                    for tt in range(NT):
                                        mm(bank[half][:, t * P:(t + 1) * P], xs[:, tt, 4 * half + t::KT],
                                           pick[:, tt, :, :].rearrange("p e s -> p (e s)"), start=(tt == 0), stop=(tt == 1))
                            for tt in range(NT):
                                last = tr(bank[2][:, tt * P:(tt + 1) * P], pick_w[:, tt, :, :].rearrange("p e s -> p (e s)"), ident)
                            last.then_inc(ov_pe[l], 1)
                            pe.wait_ge(ov_dve[l], n + 3)
                            pe.wait_ge(ov_act[l], m + 1)
                            for k in range(2):
                                w = ring[:, k, :].rearrange("p (t n) -> p t n", t=KT)
                                for mt in range(FT):
                                    for t in range(KT):
                                        last = mm(bank[2 + k][:, mt * P:(mt + 1) * P], w[:, t, mt * P:(mt + 1) * P], xgT[:, t, :],
                                                  start=(t == 0), stop=(t == KT - 1))
                            last.then_inc(ov_pe[l], 1)
                            pe.wait_ge(ov_dve[l], n + 4)
                            w = ring[:, 2, :].rearrange("p (t n) -> p t n", t=4)
                            hid_all = hid.rearrange("p (m s) -> p m s", s=P)
                            for c in range(KT):
                                for mt in range(FT):
                                    last = mm(bank[4 + c // 4][:, (c % 4) * P:(c % 4 + 1) * P], w[:, mt, c * P:(c + 1) * P],
                                              hid_all[:, mt, :], start=(mt == 0), stop=(mt == FT - 1))
                            last.then_inc(ov_pe[l], 1)
                            pe.wait_ge(ov_dve[l], n + 5)
                            for c in range(KT):
                                last = tr(bank[6 + c // 4][:, (c % 4) * P:(c % 4 + 1) * P], yT[:, c, :], ident)
                            last.then_inc(ov_pe[l], 1)
                            pe.wait_ge(ov_act[l], m + 2)
                            for tt in range(NT):
                                for c in range(2):
                                    last = mm(bank[6 * (1 - tt) + c][:, :], pick_wT[:, tt, :], y_slot[:, c * 512:(c + 1) * 512],
                                              start=True, stop=True)
                            last.then_inc(ov_pe[l], 1)
                            pe.wait_ge(ov_dve[l], n + 6)
                            tr(bank[6][:, 0:P], ident, ident).then_inc(ov_pe[l], 1)
                with pe.Else():
                    pe.nop()

            pe.wait_ge(x_loaded, 16)
            pe.wait_ge(tables_loaded, 32)
            transpose_x(0, 0)
            pe.wait_ge(rel_loaded, 16)
            pe.wait_ge(mask_row, 1)
            mm(bank[6][0:HEADS, 0:BIAS_W], rel_w[:, :], bucket_rows, start=True, stop=True).then_inc(dist_ready, 1)
            transpose_x(0, 1)
            xT_here(0, NT - 1)

            def moba_group(g):
                u, part = divmod(g, 2)
                if part == 0:
                    arrived(u)
                if u % 3 < 2:
                    last = project_T(0, g, slot8(u), [tile_cols(2 * part), tile_cols(2 * part + 1)])
                else:
                    last = project_tok(0, g, slot8(u), part)
                last.then_inc(proj_ready[0], 1)

            for g in range(6):
                moba_group(g)
            def moba_job(h, br):
                if h == 0:
                    pe.wait_ge(proj_dve[0], 3)
                    pe.wait_ge(proj_act[0], 3)
                if h == 8:
                    pe.wait_ge(proj_dve[0], 6)
                    pe.wait_ge(proj_act[0], 6)
                half = slice(DH * (h % 2), DH * (h % 2) + DH)
                return dict(q=qT[half, h // 2, :], k=kT[half, h // 2, :], v=lambda kt: v_tok[:, kt, h * DH:(h + 1) * DH])
            attention(0, moba_job, moba_group)
            for k in range(4, 8):
                out_piece(0, k)
            route_tokens(0)
            experts(0)
            overflow(0)

            for tt in range(NT):
                normed(0, 1, tt)
                transpose_x(2, tt)
            xT_here(2, NT - 1)
            u0 = first_use[1]

            def nsa_group(g):
                if g == 2:
                    proj_bank_free(1, g)
                    for tt in range(NT):
                        for t in range(KT):
                            last = mm(bank[0][:, tt * P:(tt + 1) * P], xT[:, t, tt * P:(tt + 1) * P],
                                      gate_w[:, t * 3 * HEADS:t * 3 * HEADS + P], start=(t == 0), stop=(t == KT - 1))
                    last.then_inc(proj_ready[1], 1)
                    return
                k = g if g < 2 else g - 1
                part = k % 2
                use = u0 + {0: 0, 1: 1, 2: 2, 3: 5, 4: 6}[k // 2]
                if part == 0:
                    arrived(use)
                w = slot8(use)
                if g < 7:
                    last = project_T(1, g, w, [tile_cols(2 * part), tile_cols(2 * part + 1)])
                elif part == 0:
                    last = project_T(1, g, w, [tile_cols(0), tile_cols(1)])
                else:
                    proj_bank_free(1, g)
                    for tt in range(NT):
                        for t in range(KT):
                            last = mm(bank[g % 2][:, tt * 256:(tt + 1) * 256], xT[:, t, tt * P:(tt + 1) * P], w[:, t, 256:512],
                                      start=(t == 0), stop=(t == KT - 1))
                last.then_inc(proj_ready[1], 1)

            for g in range(3):
                nsa_group(g)
            for b in range(2):
                last = tr(bank[6][:, b * 16:(b + 1) * 16], pos_rows[:, b, :], ident[0:16, 0:16])
            last.then_inc(cpos_ready, 1)
            for g in (3, 4):
                nsa_group(g)
            for b in range(2):
                arrived(u0 + 3 + b)
            pe.wait_ge(cin_ready, 1)
            pe.wait_ge(pads_ready, 3)
            for lp in range(16):
                for b in range(2):
                    last = mm(bank[2][CMP_ROWS * b:CMP_ROWS * (b + 1), 0:CMP_HID], cmp_in[:, b, lp, :], slot16(u0 + 3 + b)[:, lp, :],
                              start=(lp == 0), stop=(lp == 15))
            last.then_inc(chid_psum, 1)
            nsa_group(5)
            pe.wait_ge(chid_ready, 1)
            for f in range(2):
                last = tr(bank[3][:, f * P:(f + 1) * P], cmp_hid[:, f * P:(f + 1) * P], ident)
            last.then_inc(chidT_psum, 1)
            nsa_group(6)
            pe.wait_ge(chidT_ready, 1)
            for f in range(2):
                for hp in (0, DH):
                    mm(bank[4][hp:hp + DH, 0:P], cmp_w2[:, 0, f, :], cmp_hidT[:, f, :], start=(f == 0), stop=(f == 1))
            for hkv in range(KV):
                at = CMP_ROWS + hkv * N_CMP
                for f in range(2):
                    for g in range(GROUP):
                        last = mm(bank[5][32 * g:32 * g + N_CMP, hkv * DH:(hkv + 1) * DH],
                                  cmp_hidT[:, f, at:at + N_CMP], cmp_w2[:, 1, f, :], start=(f == 0), stop=(f == 1))
            last.then_inc(ckv_psum, 1)
            nsa_group(7)
            pe.wait_ge(ckv_ready, 1 + GROUP)
            pe.wait_ge(proj_dve[1], 4)
            pe.wait_ge(proj_act[1], 3)
            for hkv in range(KV):
                for g in range(GROUP):
                    half = slice(DH * (g % 2), DH * (g % 2) + DH)
                    last = mm(bank[2 + hkv // 2][32 * g:32 * g + 32, hkv % 2 * SEQ:(hkv % 2 + 1) * SEQ],
                              cmp_keyT[half, hkv * N_CMP:hkv * N_CMP + 32], qT[half, (hkv * GROUP + g) // 2, :],
                              start=True, stop=True)
            last.then_inc(csT_psum, 1)
            nsa_group(8)
            pe.wait_ge(csT_dve, 1)
            pe.wait_ge(csT_act, 1)
            for tt in range(NT):
                for hkv in range(KV):
                    at = hkv % 2 * SEQ + tt * P
                    last = tr(bank[6 + tt][:, hkv * P:(hkv + 1) * P], cmp_sT[:, hkv // 2, at:at + P], ident)
            last.then_inc(cs_ready, 1)
            nsa_group(9)

            def transpose_cmp():
                pe.wait_ge(cp_ready, 1)
                for b in range(2):
                    for tt in range(NT):
                        for g in (2 * b, 2 * b + 1):
                            last = tr(bank[4 + b][:, (g % 2) * SEQ + tt * P:(g % 2) * SEQ + (tt + 1) * P],
                                      cmp_p[:, tt, 4 * g:4 * g + 4, :].rearrange("p h n -> p (h n)"), ident)
                    last.then_inc(cpT_psum, 1)

            pe.wait_ge(proj_dve[1], 5)
            pe.wait_ge(proj_act[1], 4)

            def nsa_job(h, b):
                hkv = h // GROUP
                half = slice(DH * (h % 2), DH * (h % 2) + DH)
                return dict(q=qT[half, h // 2, :], k=nsa_kT[half, b, 2 * (hkv % 2) + hkv // 2, :],
                            v=lambda kt: nsa_v[:, b, kt, hkv * DH:(hkv + 1) * DH])

            def compressed(h, ps):
                hkv, g = divmod(h, GROUP)
                at = slice(32 * g, 32 * g + N_CMP)
                return mm(ps, cmp_val[at, hkv, :], cmp_pT[at, hkv, :], start=False, stop=True)
            attention(1, nsa_job, nsa_group, compressed, transpose_cmp)
            for k in range(4, 8):
                out_piece(1, k)
            route_tokens(1)
            experts(1)
            overflow(1)

        @block.vector
        def _(dve):
            v = nc.vector
            links = [0]

            def link(ins):
                links[0] += 1
                ins.then_inc(dve_chain, 1)
                dve.wait_ge(dve_chain, links[0])

            def softmax_steps(l, scale):
                n_steps = len(job_pairs[l])
                for s in range(n_steps + 4):
                    if s < n_steps:
                        m, _ = job_pairs[l][s]
                        dve.wait_ge(scores_ready[l], s + 1)
                        after(dve, probsT_ready[l], s - 2)
                        for a in range(2):
                            for tt, (x, y) in enumerate(((0, P), (P, 3 * P))):
                                last = v.tensor_tensor_reduce(
                                    out=probs[:, 2 * (s % 3) + a, x:y], in0=bank[2 + a][:, x:y], in1=bias_for(2 * m + a, tt),
                                    scale=1.0, scalar=-3e38, op0=ALU.add, op1=ALU.max, accum_out=job_max[:, s % 3, a, tt:tt + 1])
                        last.then_inc(scores_read[l], 1)
                        dve.wait_ge(scores_read[l], s + 1)
                        v.tensor_scalar(job_max[:, s % 3, :, :], job_max[:, s % 3, :, :], -1.0, None, ALU.mult).then_inc(max_ready[l], 1)
                    if s >= 4 and (s - 3 == n_steps or job_pairs[l][s - 3][0] != job_pairs[l][s - 4][0]):
                        m = job_pairs[l][s - 4][0]
                        dve.wait_ge(pv_done[l], s - 3)
                        v.tensor_copy(oT[:, m, :], bank[6 + m % 2][:, 0:SEQ]).then_inc(o_copied[l], 1)
                    if 1 <= s <= n_steps:
                        j = s - 1
                        dve.wait_ge(exp_ready[l], j + 1)
                        ins = v.reciprocal(job_scale[:, j % 3, :, :], job_sum[:, j % 3, :, :])
                        if scale:
                            link(ins)
                            ins = v.tensor_tensor(job_scale[:, j % 3, :, :], job_scale[:, j % 3, :, :], scale(*job_pairs[l][j]), ALU.mult)
                        ins.then_inc(scale_ready[l], 1)
                        dve.wait_ge(scale_ready[l], j + 1)
                        for a, tt, x, y in ((0, 0, 0, P), (0, 1, P, 3 * P), (1, 1, P, 3 * P)):
                            pr = probs[:, 2 * (j % 3) + a, x:y]
                            last = v.tensor_scalar(pr, pr, job_scale[:, j % 3, a, tt:tt + 1], None, ALU.mult)
                        last.then_inc(probs_dve[l], 1)
                    beside_step(l, s)
                    if 2 <= s < n_steps + 2:
                        j = s - 2
                        dve.wait_ge(probsT_ready[l], j + 1)
                        after(dve, pv_done[l], j - 1)
                        v.tensor_copy(probsT[:, 2 * (j % 2), :], bank[4][:, 0:3 * P]).then_inc(probsT_dve[l], 1)

            def beside_step(l, s):
                for kind, k in beside[l].get(s, []):
                    if kind == "out":
                        add_piece(l, k)
                    elif kind == "cmp":
                        dve.wait_ge(cpT_psum, 1)
                        v.tensor_copy(cmp_pT[:, 0:2, :].rearrange("p g q -> p (g q)"), bank[4][:, :]).then_inc(cpT_dve, 1)
                    elif k % 2 == 0:
                        (moba_copy if l == 0 else nsa_copy)(k)

            def add_piece(l, k):
                c, tt, n = k // 4, k // 2 % 2, k % 2
                a = acc[:, tt, n * 512:(n + 1) * 512]
                dve.wait_ge(mix_ready[l], k + 1)
                if c == 0:
                    v.scalar_tensor_tensor(a, xs[:, tt, n * 512:(n + 1) * 512], ALPHA, bank[k % 2][:, :], ALU.mult, ALU.add).then_inc(mix_added[l], 1)
                else:
                    dve.wait_ge(mix_added[l], k - 3)
                    v.tensor_tensor(a, a, bank[k % 2][:, :], ALU.add).then_inc(mix_added[l], 1)

            def count_half(tt, n):
                return v.bn_stats(stats[:, tt, 6 * n:6 * n + 6], acc[:, tt, n * 512:(n + 1) * 512])

            def variance(tt):
                link(v.bn_aggr(moments[:, tt, :], stats[:, tt, :]))
                v.tensor_scalar(rstd[:, tt:tt + 1], moments[:, tt, 1:2], EPS, None, ALU.add).then_inc(var_ready, 1)

            def norm_tile(l, n, tt):
                k = norm_tiles(l, n, tt)
                dve.wait_ge(norm_loaded, 32 * (2 * l + n + 1))
                v.scalar_tensor_tensor(acc[:, tt, :], acc[:, tt, :], moments[:, tt, 0:1], norm_w[:, 0, :], ALU.subtract, ALU.mult)
                dve.wait_ge(std_ready, k)
                link(v.reciprocal(rstd[:, tt:tt + 1], rstd[:, tt:tt + 1]))
                v.scalar_tensor_tensor(xs[:, tt, :], acc[:, tt, :], rstd[:, tt:tt + 1], norm_w[:, 1, :], ALU.mult, ALU.add).then_inc(normed_tiles, 1)

            def attention_norm(l):
                for tt in range(NT):
                    for n in range(2):
                        add_piece(l, 4 + 2 * tt + n)
                        dve.wait_ge(mix_added[l], 4 + 2 * tt + n + 1)
                        last = count_half(tt, n)
                    link(last)
                    variance(tt)
                    norm_tile(l, 0, tt)

            def route_tokens(l):
                def wide(x):
                    return x.unsqueeze(2).to_broadcast([P, NT, E])

                def flat_table(name, n):
                    return table(name).unsqueeze(1).to_broadcast([P, NT, n])

                pr = route[:, 0, :, :]
                dve.wait_ge(logits_ready[l], 1)
                link(v.tensor_tensor(pr, bank[6][:, 0:NT * P].rearrange("p (t e) -> p t e", e=P)[:, :, 0:E],
                                     router_bias[:, :].unsqueeze(1).to_broadcast([P, NT, E]), ALU.add))
                link(v.tensor_reduce(one[:, 0, :], pr, AX, ALU.max))
                v.tensor_tensor(pr, pr, wide(one[:, 0, :]), ALU.subtract).then_inc(logits_shifted[l], 1)
                dve.wait_ge(logits_exp[l], 1)
                link(v.tensor_reduce(one[:, 1, :], pr, AX, ALU.add))
                link(v.reciprocal(one[:, 2, :], one[:, 1, :]))
                link(v.tensor_tensor(pr, pr, wide(one[:, 2, :]), ALU.mult))
                g4 = pr.rearrange("p t (g e) -> p t g e", e=EG)
                pairs = [(small[:, 0, :, :], small[:, 1, :, :], 0), (small[:, 2, :, :], small[:, 3, :, :], 2)]
                for hi, lo, a in pairs:
                    v.tensor_tensor(hi, g4[:, :, :, a], g4[:, :, :, a + 1], ALU.max)
                    link(v.tensor_tensor(lo, g4[:, :, :, a], g4[:, :, :, a + 1], ALU.min))
                v.tensor_tensor(small[:, 4, :, :], small[:, 0, :, :], small[:, 2, :, :], ALU.max)
                v.tensor_tensor(small[:, 5, :, :], small[:, 0, :, :], small[:, 2, :, :], ALU.min)
                link(v.tensor_tensor(small[:, 6, :, :], small[:, 1, :, :], small[:, 3, :, :], ALU.max))
                link(v.tensor_tensor(small[:, 5, :, :], small[:, 5, :, :], small[:, 6, :, :], ALU.max))
                link(v.tensor_tensor(small[:, 7, :, :], small[:, 4, :, :], small[:, 5, :, :], ALU.add))
                def wide8(x):
                    return x.unsqueeze(2).to_broadcast([P, NT, NG])
                link(v.tensor_reduce(one[:, 3, :], small[:, 7, :, :], AX, ALU.max))
                link(v.tensor_tensor(small[:, 0, :, :], small[:, 7, :, :], wide8(one[:, 3, :]), ALU.is_equal))
                link(v.tensor_tensor(small[:, 0, :, :], small[:, 0, :, :], flat_table("first8", NG), ALU.mult))
                link(v.tensor_reduce(one[:, 3, :], small[:, 0, :, :], AX, ALU.max))
                link(v.tensor_tensor(small[:, 1, :, :], small[:, 0, :, :], wide8(one[:, 3, :]), ALU.is_equal))
                link(v.tensor_scalar(small[:, 2, :, :], small[:, 1, :, :], 4.0, -4.0, ALU.mult, ALU.add))
                cand = route[:, 1, :, :]
                link(v.tensor_tensor(cand.rearrange("p t (g e) -> p t g e", e=EG), g4,
                                     small[:, 2, :, :].unsqueeze(3).to_broadcast([P, NT, NG, EG]), ALU.add))
                hot = [route[:, 3, :, :], route[:, 4, :, :]]
                for k in range(2):
                    link(v.tensor_reduce(one[:, 4 + k, :], cand, AX, ALU.max))
                    link(v.tensor_tensor(route[:, 2, :, :], cand, wide(one[:, 4 + k, :]), ALU.is_equal))
                    link(v.tensor_tensor(route[:, 2, :, :], route[:, 2, :, :], flat_table("first32", E), ALU.mult))
                    link(v.tensor_reduce(one[:, 3, :], route[:, 2, :, :], AX, ALU.max))
                    link(v.tensor_tensor(hot[k], route[:, 2, :, :], wide(one[:, 3, :]), ALU.is_equal))
                    if k == 0:
                        link(v.scalar_tensor_tensor(cand, hot[0], -16.0, cand, ALU.mult, ALU.add))
                v.tensor_tensor(chosen[:, :, :], hot[0], hot[1], ALU.add).then_inc(chosen_ready[l], 1)
                link(v.tensor_tensor(one[:, 6, :], one[:, 4, :], one[:, 5, :], ALU.add))
                link(v.reciprocal(one[:, 7, :], one[:, 6, :]))
                for k in range(2):
                    link(v.tensor_tensor(one[:, 4 + k, :], one[:, 4 + k, :], one[:, 7, :], ALU.mult))
                    link(v.tensor_tensor(hot[k], hot[k], wide(one[:, 4 + k, :]), ALU.mult))
                link(v.tensor_tensor(weight[:, :, :], hot[0], hot[1], ALU.add))
                dve.wait_ge(ranks_ready[l], 1)
                ranks = bank[7][:, 0:NT * E].rearrange("p (t e) -> p t e", e=E)
                link(v.scalar_tensor_tensor(route[:, 5, :, :], ranks, 1.0, chosen[:, :, :], ALU.add, ALU.mult))
                link(v.tensor_scalar(slot_of[:, :, :], route[:, 5, :, :], -1.0, None, ALU.add))
                choice(l, 0)
                link(v.tensor_reduce(crowded[:, :], bank[7][:, NT * E:(NT + 1) * E], AX, ALU.max))
                link(v.tensor_scalar(crowded[:, :], crowded[:, :], float(CAP), None, ALU.is_gt))
                v.tensor_copy(crowded_i[:, :], crowded[:, :]).then_inc(flag_ready[l], 1)

            def choice(l, i):
                v.tensor_tensor(pick, table("slot").rearrange("p (e s) -> p e s", e=2).unsqueeze(1).to_broadcast([P, NT, 2, CAP]),
                                slot_of[:, :, bass.ds(2 * i, 2)].unsqueeze(3).to_broadcast([P, NT, 2, CAP]), ALU.is_equal).then_inc(pick_ready[l], 1)

            def experts(l):
                def hidden(i):
                    dve.wait_ge(up_done[l], i + 1)
                    dve.wait_ge(silu_ready[l], i + 1)
                    v.tensor_tensor(hid, silu, bank[3][:, :], ALU.mult).then_inc(hid_ready[l], 1)

                def add(i, last=False):
                    after(dve, acc_added[l], 4 * i)
                    for k, b in enumerate((4, 0, 1, 7)):
                        tt, n = divmod(k, 2)
                        dve.wait_ge(spread_ready[l], 4 * i + k + 1)
                        c = acc[:, tt, n * 512:(n + 1) * 512]
                        v.tensor_tensor(c, c, bank[b][:, :], ALU.add).then_inc(acc_added[l], 1)
                        if last:
                            dve.wait_ge(acc_added[l], 4 * i + k + 1)
                            ins = count_half(tt, n)
                            if k == 3:
                                link(ins)

                def copy_xg(i):
                    dve.wait_ge(gathered[l], 2 * i + 1)
                    v.tensor_copy(xgT[:, 0:4, :].rearrange("p t s -> p (t s)"), bank[0][:, :]).then_inc(xg_dve[l], 1)

                def copy_y(i):
                    dve.wait_ge(down_done[l], 2 * i + 1)
                    v.tensor_copy(y_slot[:, 0:512], bank[5][:, :]).then_inc(y_dve[l], 1)

                def pair(i, first, last):
                    if not first:
                        dve.wait_ge(pickwT_psum[l], i)
                    dve.wait_ge(pick_ready[l], i + 1)
                    v.tensor_tensor(pick_w, pick, weight[:, :, bass.ds(2 * i, 2)].unsqueeze(3).to_broadcast([P, NT, 2, CAP]),
                                    ALU.mult).then_inc(pickw_ready[l], 1)
                    if not last:
                        dve.wait_ge(pickw_ready[l], i + 1)
                        dve.wait_ge(gathered[l], 2 * i + 2)
                        choice(l, i + 1)
                    hidden(i)
                    if not first:
                        add(i - 1)
                    if not last:
                        copy_xg(i + 1)
                    copy_y(i)

                dve.wait_ge(flag_ready[l], 1)
                dve.wait_ge(acc_started[l], 1)
                copy_xg(0)
                pair(0, True, False)
                with dve.Fori(1, PAIRS - 1) as i:
                    pair(i, False, False)
                pair(PAIRS - 1, False, True)
                add(PAIRS - 1, last=True)

            def overflow(l):
                dve.wait_ge(flag_ready[l], 1)
                flag = dve.value_load(crowded_i[0:1, 0:1], min_val=0, max_val=1)
                flat = lambda x: x.rearrange("p t e s -> p t (e s)")
                with dve.If(flag > 0):
                    dve.wait_ge(ov_pe[l], 1)
                    with dve.Fori(0, E) as e:
                        for r in range(2):
                            n = e * 12 + 6 * r
                            k = e * 12 + 6 * r + 1
                            if r == 0:
                                dve.wait_ge(ov_pe[l], k)
                            v.tensor_scalar(route[:, 6, :, :], slot_of[:, :, :], -float(CAP + P * r), None, ALU.add).then_inc(ov_dve[l], 1)
                            dve.wait_ge(ov_dve[l], n + 1)
                            v.tensor_tensor(flat(pick), table("slot2").unsqueeze(1).to_broadcast([P, NT, P]),
                                            route[:, 6, :, bass.ds(e, 1)].to_broadcast([P, NT, P]), ALU.is_equal).then_inc(ov_chain[l], 1)
                            dve.wait_ge(ov_chain[l], e * 2 + r + 1)
                            v.tensor_tensor(flat(pick_w), flat(pick), weight[:, :, bass.ds(e, 1)].to_broadcast([P, NT, P]),
                                            ALU.mult).then_inc(ov_dve[l], 1)
                            dve.wait_ge(ov_pe[l], k + 1)
                            v.tensor_copy(xgT[:, 0:4, :].rearrange("p t s -> p (t s)"), bank[0][:, :])
                            v.tensor_copy(xgT[:, 4:8, :].rearrange("p t s -> p (t s)"), bank[1][:, :]).then_inc(ov_dve[l], 1)
                            dve.wait_ge(ov_silu[l], e * 2 + r + 1)
                            v.tensor_tensor(hid, silu, bank[3][:, :], ALU.mult).then_inc(ov_dve[l], 1)
                            dve.wait_ge(ov_pe[l], k + 3)
                            v.tensor_copy(yT[:, 0:4, :].rearrange("p t s -> p (t s)"), bank[4][:, :])
                            v.tensor_copy(yT[:, 4:8, :].rearrange("p t s -> p (t s)"), bank[5][:, :]).then_inc(ov_dve[l], 1)
                            dve.wait_ge(ov_pe[l], k + 5)
                            for tt in range(NT):
                                for c in range(2):
                                    a = acc[:, tt, c * 512:(c + 1) * 512]
                                    last = v.tensor_tensor(a, a, bank[6 * (1 - tt) + c][:, :], ALU.add)
                            last.then_inc(ov_dve[l], 1)
                            dve.wait_ge(ov_dve[l], n + 6)
                    for tt in range(NT):
                        for c in range(2):
                            last = count_half(tt, c)
                    last.then_inc(ov_chain[l], 1)
                    dve.wait_ge(ov_chain[l], 2 * E + 1)
                with dve.Else():
                    dve.nop()

            def expert_norm(l):
                for tt in range(NT):
                    variance(tt)
                for tt in range(NT):
                    norm_tile(l, 1, tt)

            dve.wait_ge(dist_ready, 1)
            v.tensor_copy(dist_row, bank[6][0:HEADS, 0:BIAS_W]).then_inc(dist_copied, 1)

            def moba_copy(g):
                u = g // 2
                hh = u // 3
                dve.wait_ge(proj_ready[0], g + 1)
                if u % 3 == 0:
                    ins = v.tensor_scalar(qT[:, 4 * hh:4 * hh + 2, :].rearrange("p m q -> p (m q)"), bank[0][:, :], DH ** -0.5, None, ALU.mult)
                elif u % 3 == 1:
                    ins = v.tensor_copy(kT[:, 4 * hh:4 * hh + 2, :].rearrange("p m q -> p (m q)"), bank[0][:, :])
                else:
                    ins = v.tensor_copy(v_tok[:, 0, hh * 512:(hh + 1) * 512], bank[0][:, :])
                ins.then_inc(proj_dve[0], 1)

            for g in (0, 2, 4):
                moba_copy(g)
            dve.wait_ge(bias_loaded, 16)
            softmax_steps(0, None)
            attention_norm(0)
            route_tokens(0)
            experts(0)
            overflow(0)
            expert_norm(0)

            def nsa_copy(g):
                dve.wait_ge(proj_ready[1], g + 1)
                if g == 0:
                    ins = copy_cmp_in(v.tensor_copy, 0, bank[0])
                elif g < 7:
                    c = g // 2 - 2
                    ins = v.tensor_scalar(qT[:, 4 * c + 2:4 * c + 4, :].rearrange("p m q -> p (m q)"), bank[0][:, :], DH ** -0.5, None, ALU.mult)
                else:
                    ins = v.tensor_copy(nsa_v[:, (g - 8) // 2, :, :].rearrange("p k n -> p (k n)"), bank[0][:, :])
                ins.then_inc(proj_dve[1], 1)

            nsa_copy(0)
            dve.wait_ge(gate_exp, 1)
            link(v.tensor_scalar(gates[:, :, :], gates[:, :, :], 1.0, None, ALU.add))
            v.reciprocal(gates[:, :, :], gates[:, :, :]).then_inc(proj_dve[1], 1)
            dve.wait_ge(cpos_ready, 1)
            link(v.tensor_copy(pos_cols[:, :, :].rearrange("p b l -> p (b l)"), bank[6][:, 0:32]))
            dve.wait_ge(proj_dve[1], 2)
            dve.wait_ge(proj_act[1], 1)
            cin = cmp_in[:, :, :, 0:KV * N_CMP]
            for b in range(2):
                last = v.tensor_tensor(cin[:, b, :, :], cin[:, b, :, :], pos_cols[:, b, :].unsqueeze(2).to_broadcast([P, 16, KV * N_CMP]), ALU.add)
            last.then_inc(cin_ready, 1)
            nsa_copy(4)
            nsa_copy(6)
            dve.wait_ge(ckv_psum, 1)
            v.tensor_copy(cmp_keyT[:, :], bank[4][:, 0:80]).then_inc(ckv_ready, 1)
            for g in range(GROUP):
                at = slice(32 * g, 32 * g + N_CMP)
                v.tensor_copy(cmp_val[at, :, :].rearrange("p h d -> p (h d)"), bank[5][at, 0:KV * DH]).then_inc(ckv_ready, 1)
            v.memset(cmp_p, 0.0).then_inc(cs_centred, 1)
            dve.wait_ge(csT_psum, 1)
            v.tensor_copy(cmp_sT[:, 0, :], bank[2][:, :]).then_inc(csT_dve, 1)
            nsa_copy(8)
            dve.wait_ge(cs_ready, 1)
            dve.wait_ge(cs_centred, 1)
            cp = cmp_p[:, :, :, 0:N_CMP]
            for tt in range(NT):
                unseen = table("unseen")[:, 16 * tt:16 * tt + N_CMP].unsqueeze(1).to_broadcast([P, HEADS, N_CMP])
                link(v.tensor_tensor(cp[:, tt, :, :], bank[6 + tt][:, :].rearrange("p (h n) -> p h n", n=32)[:, :, 0:N_CMP], unseen, ALU.add))
            link(v.tensor_reduce(cmp_max[:, :, :], cp, AX, ALU.max))
            v.tensor_tensor(cp, cp, cmp_max[:, :, :].unsqueeze(3).to_broadcast([P, NT, HEADS, N_CMP]), ALU.subtract).then_inc(cs_centred, 1)
            dve.wait_ge(cs_exp, 1)
            link(v.tensor_reduce(cmp_sum[:, :, :], cp, AX, ALU.add))
            link(v.reciprocal(cmp_sum[:, :, :], cmp_sum[:, :, :]))
            gate3 = gates[:, :, :].rearrange("p t (h b) -> p t h b", b=3)
            link(v.tensor_tensor(cmp_sum[:, :, :], cmp_sum[:, :, :], gate3[:, :, :, 0], ALU.mult))
            for tt in range(NT):
                seen_tt = table("seen")[:, 16 * tt:16 * tt + N_CMP].unsqueeze(1).to_broadcast([P, HEADS, N_CMP])
                link(v.tensor_tensor(cp[:, tt, :, :], cp[:, tt, :, :], seen_tt, ALU.mult))
            v.tensor_tensor(cp, cp, cmp_sum[:, :, :].unsqueeze(3).to_broadcast([P, NT, HEADS, N_CMP]), ALU.mult).then_inc(cp_ready, 1)
            softmax_steps(1, lambda m, b: gate3[:, :, 2 * m:2 * m + 2, 1 + b].rearrange("p t a -> p a t"))
            attention_norm(1)
            route_tokens(1)
            experts(1)
            overflow(1)
            expert_norm(1)

        @block.scalar
        def _(act):
            s_ = nc.scalar

            def xT_copy(n, tt):
                for half in range(2):
                    act.wait_ge(xT_ready, 2 * (NT * n + tt) + half + 1)
                    s_.copy(xT[:, 4 * half:4 * half + 4, tt * P:(tt + 1) * P],
                            bank[4 + half][:, :].rearrange("p (t q) -> p t q", q=P)).then_inc(xT_copied, 1)

            def softmax_steps(l):
                n_steps = len(job_pairs[l])
                for s in range(n_steps + 2):
                    if s < n_steps:
                        act.wait_ge(max_ready[l], s + 1)
                        for a in range(2):
                            for tt, (x, y) in enumerate(((0, P), (P, 3 * P))):
                                pr = probs[:, 2 * (s % 3) + a, x:y]
                                last = s_.activation(pr, pr, ACT.Exp, bias=job_max[:, s % 3, a, tt:tt + 1],
                                                     accum_out=job_sum[:, s % 3, a, tt:tt + 1])
                        last.then_inc(exp_ready[l], 1)
                    for kind, k in beside[l].get(s, []):
                        if kind == "cmp":
                            act.wait_ge(cpT_psum, 2)
                            s_.copy(cmp_pT[:, 2:4, :].rearrange("p g q -> p (g q)"), bank[5][:, :]).then_inc(cpT_act, 1)
                        if kind == "proj" and k % 2 == 1:
                            moba_copy(k)
                    if s >= 2:
                        j = s - 2
                        act.wait_ge(probsT_ready[l], j + 1)
                        after(act, pv_done[l], j - 1)
                        s_.copy(probsT[:, 2 * (j % 2) + 1, :], bank[5][:, 0:3 * P]).then_inc(probsT_act[l], 1)

            def norm(l, n):
                for tt in range(NT):
                    act.wait_ge(var_ready, norm_tiles(l, n, tt))
                    s_.activation(rstd[:, tt:tt + 1], rstd[:, tt:tt + 1], ACT.Sqrt).then_inc(std_ready, 1)
                    if n == 0:
                        xT_copy(2 * l + 1, tt)
                if n == 1 and l + 1 < LAYERS:
                    for tt in range(NT):
                        xT_copy(2 * l + 2, tt)

            def route_tokens(l):
                act.wait_ge(logits_shifted[l], 1)
                s_.activation(route[:, 0, :, :], route[:, 0, :, :], ACT.Exp).then_inc(logits_exp[l], 1)
                s_.mul(acc[:, :, :].rearrange("p t d -> p (t d)"), xs[:, :, :].rearrange("p t d -> p (t d)"), ALPHA).then_inc(acc_started[l], 1)

            def experts(l):
                def gated(i):
                    act.wait_ge(gate_done[l], i + 1)
                    after(act, hid_ready[l], i)
                    s_.activation(silu, bank[2][:, :], ACT.Silu).then_inc(silu_ready[l], 1)

                def copy_hidT(i):
                    act.wait_ge(hidT_psum[l], i + 1)
                    s_.copy(hidT.rearrange("p m s -> p (m s)"), bank[4][:, :]).then_inc(hidT_ready[l], 1)

                def copy_xg(i):
                    act.wait_ge(gathered[l], 2 * i + 2)
                    s_.copy(xgT[:, 4:8, :].rearrange("p t s -> p (t s)"), bank[1][:, :]).then_inc(xg_act[l], 1)

                def copy_pickwT(i):
                    act.wait_ge(pickwT_psum[l], i + 1)
                    s_.copy(pick_wT.rearrange("p t q -> p (t q)"), bank[7][:, 0:SEQ]).then_inc(pickwT_ready[l], 1)

                def copy_y(i):
                    act.wait_ge(down_done[l], 2 * i + 2)
                    s_.copy(y_slot[:, 512:1024], bank[6][:, :]).then_inc(y_act[l], 1)

                def pair(i, first, last):
                    gated(i)
                    copy_hidT(i)
                    if not last:
                        copy_xg(i + 1)
                    copy_pickwT(i)
                    copy_y(i)

                copy_xg(0)
                pair(0, True, False)
                with act.Fori(1, PAIRS - 1) as i:
                    pair(i, False, False)
                pair(PAIRS - 1, False, True)

            def overflow(l):
                act.wait_ge(flag_ready[l], 1)
                flag = act.value_load(crowded_i[0:1, 0:1], min_val=0, max_val=1)
                with act.If(flag > 0):
                    with act.Fori(0, E) as e:
                        for r in range(2):
                            k = e * 12 + 6 * r + 1
                            act.wait_ge(ov_pe[l], k + 1)
                            s_.copy(pick_wT.rearrange("p t q -> p (t q)"), bank[2][:, 0:SEQ]).then_inc(ov_act[l], 1)
                            act.wait_ge(ov_pe[l], k + 2)
                            s_.activation(silu, bank[2][:, :], ACT.Silu).then_inc(ov_silu[l], 1)
                            act.wait_ge(ov_pe[l], k + 4)
                            s_.copy(y_slot[:, 0:512], bank[6][:, :])
                            s_.copy(y_slot[:, 512:1024], bank[7][:, :]).then_inc(ov_act[l], 1)
                with act.Else():
                    act.nop()

            for tt in range(NT):
                xT_copy(0, tt)

            def moba_copy(g):
                u = g // 2
                hh = u // 3
                act.wait_ge(proj_ready[0], g + 1)
                if u % 3 == 0:
                    ins = s_.mul(qT[:, 4 * hh + 2:4 * hh + 4, :].rearrange("p m q -> p (m q)"), bank[1][:, :], DH ** -0.5)
                elif u % 3 == 1:
                    ins = s_.copy(kT[:, 4 * hh + 2:4 * hh + 4, :].rearrange("p m q -> p (m q)"), bank[1][:, :])
                else:
                    ins = s_.copy(v_tok[:, 1, hh * 512:(hh + 1) * 512], bank[1][:, :])
                ins.then_inc(proj_act[0], 1)

            for g in (1, 3, 5):
                moba_copy(g)
            softmax_steps(0)
            norm(0, 0)
            route_tokens(0)
            experts(0)
            overflow(0)
            norm(0, 1)

            act.wait_ge(proj_ready[1], 2)
            copy_cmp_in(s_.copy, 1, bank[1]).then_inc(proj_act[1], 1)
            act.wait_ge(proj_ready[1], 3)
            s_.activation(gates[:, :, :], bank[0][:, 0:NT * P].rearrange("p (t n) -> p t n", n=P)[:, :, 0:3 * HEADS],
                          ACT.Exp, scale=-1.0).then_inc(gate_exp, 1)

            def nsa_copy(g):
                act.wait_ge(proj_ready[1], g + 1)
                if g < 7:
                    c = (g - 3) // 2
                    last = s_.mul(qT[:, 4 * c:4 * c + 2, :].rearrange("p m q -> p (m q)"), bank[1][:, :], DH ** -0.5)
                else:
                    for dst in (0, DH):
                        for a in range(2):
                            last = s_.copy(nsa_kT[dst:dst + DH, (g - 7) // 2, 2 * a:2 * a + 2, :].rearrange("p j q -> p (j q)"),
                                           bank[1][DH * a:DH * a + DH, :])
                last.then_inc(proj_act[1], 1)

            nsa_copy(3)
            act.wait_ge(chid_psum, 1)
            s_.activation(cmp_hid[:, :], bank[2][:, 0:CMP_HID], ACT.Gelu_apprx_tanh).then_inc(chid_ready, 1)
            nsa_copy(5)
            act.wait_ge(chidT_psum, 1)
            s_.copy(cmp_hidT[:, :, :].rearrange("p f n -> p (f n)"), bank[3][:, 0:CMP_HID]).then_inc(chidT_ready, 1)
            nsa_copy(7)
            act.wait_ge(csT_psum, 1)
            s_.copy(cmp_sT[:, 1, :], bank[3][:, :]).then_inc(csT_act, 1)
            act.wait_ge(cs_centred, 2)
            cp = cmp_p[:, :, :, 0:N_CMP].rearrange("p t h n -> p (t h) n")
            s_.activation(cp, cp, ACT.Exp).then_inc(cs_exp, 1)
            nsa_copy(9)
            softmax_steps(1)
            norm(1, 0)
            route_tokens(1)
            experts(1)
            overflow(1)
            norm(1, 1)


_INS = ['x', 'rel_bias', 'router_w', 'router_b', 'ln_g', 'ln_b', 'moba_w_in', 'moba_w_out', 'nsa_w_in', 'nsa_w_out',
        'nsa_pos_k', 'nsa_pos_v', 'nsa_ck_w1', 'nsa_ck_w2', 'nsa_cv_w1', 'nsa_cv_w2', 'moe_w_gate', 'moe_w_up', 'moe_w_down']


def kernel(**inputs):
    import concourse.bacc as bacc
    from concourse.bass_utils import run_bass_kernel_spmd

    nc = bacc.Bacc("TRN2", target_bir_lowering=False, num_devices=1)
    arrays, args = {}, []
    for name in _INS:
        a = np.ascontiguousarray(inputs[name])
        arrays[f"in_{name}"] = a
        args.append(nc.dram_tensor(f"in_{name}", a.shape, mybir.dt.from_np(a.dtype), kind="ExternalInput").ap())
    tables, place = shape_tables()
    arrays["in_tables"] = tables
    args.append(nc.dram_tensor("in_tables", tables.shape, F32, kind="ExternalInput").ap())
    out = nc.dram_tensor("out", (1, SEQ, D), F32, kind="ExternalOutput").ap()
    build(nc, *args, place, out)
    return run_bass_kernel_spmd(nc, [arrays], core_ids=[0]).results[0]["out"]
```
